# Optimizing a Trainium2 kernel written in Bass

```python
import jax, jax.numpy as jnp
from jax import lax
import numpy as np

D_MODEL = 1024
BATCH = 1
SEQ = 512
DEPTH = 2
DEC_BATCH = 8
DEC_SEQ = 4
PAST_LEN = 1024
PAGE_SIZE = 128

N_A_LAYERS = DEPTH // 2
N_B_LAYERS = DEPTH - N_A_LAYERS
CHUNK = 128
A_WIDTH = 3 * D_MODEL // 4
A_GROUPS = 4
A_GROUP_DIM = A_WIDTH // A_GROUPS
MEM_TOKENS = 256
MEM_HEADS = 4
MEM_HEAD_DIM = 64
MEM_WIDTH = MEM_HEADS * MEM_HEAD_DIM
HEAD_DIM = 64
NSA_HEADS = A_WIDTH // HEAD_DIM
NSA_KV_HEADS = 4
GQA_GROUP = NSA_HEADS // NSA_KV_HEADS
NSA_WIDTH = NSA_HEADS * HEAD_DIM
KV_WIDTH = NSA_KV_HEADS * HEAD_DIM
N_BRANCH = 3
CMP_BLOCK = 32
CMP_STRIDE = 16
CMP_RATIO = CMP_BLOCK // CMP_STRIDE
CMP_HIDDEN = 2 * HEAD_DIM
SEL_BLOCK = 64
SEL_TOPK = 16
WINDOW = 512
SEL_Q_BLOCK = 32
ROPE_THETA = 500000.0
ROPE_DIM = HEAD_DIM // 4
D_FF = 4 * D_MODEL
DEEPNORM_ALPHA = (2.0 * DEPTH) ** 0.25
DEEPNORM_BETA = (8.0 * DEPTH) ** -0.25
LN_EPS = 1e-5
NEG = -1e30
FORCE_BONUS = 1e4

kernel_name = "yoco_gmlp_nsa_memory_decoder_step"

def layer_norm(x, g, b):
    xf = x.astype(jnp.float32)
    mu = xf.mean(-1, keepdims=True)
    var = jnp.square(xf - mu).mean(-1, keepdims=True)
    return ((xf - mu) * lax.rsqrt(var + LN_EPS) * g.astype(jnp.float32) + b.astype(jnp.float32)).astype(x.dtype)

def rope(x, pos):
    half = ROPE_DIM // 2
    inv_freq = ROPE_THETA ** (-jnp.arange(half, dtype=jnp.float32) / half)
    ang = pos.astype(jnp.float32)[:, None] * inv_freq[None, :]
    ang = ang.reshape((pos.shape[0],) + (1,) * (x.ndim - 3) + (half,))
    cos, sin = jnp.cos(ang), jnp.sin(ang)
    xr = x[..., :ROPE_DIM].astype(jnp.float32)
    x1, x2 = xr[..., :half], xr[..., half:]
    rot = jnp.concatenate([x1 * cos - x2 * sin, x2 * cos + x1 * sin], axis=-1)
    return jnp.concatenate([rot.astype(x.dtype), x[..., ROPE_DIM:]], axis=-1)

def masked_softmax(s, mask):
    s = jnp.where(mask, s, NEG)
    return jnp.where(mask, jax.nn.softmax(s, axis=-1), 0.0)

def spatial_gate(u, v, w_s, b_s):
    B, T = u.shape[:2]
    n_chunk = -(-T // CHUNK)
    pad = n_chunk * CHUNK - T
    vp = jnp.pad(v, ((0, 0), (0, pad), (0, 0), (0, 0))).reshape(B, n_chunk, CHUNK, A_GROUPS, A_GROUP_DIM)
    causal = jnp.tril(jnp.ones((CHUNK, CHUNK), dtype=bool))
    w = jnp.where(causal[None], w_s, 0.0).astype(v.dtype)
    mixed = jnp.einsum('gts,bcsgd->bctgd', w, vp) + b_s.T[None, None, :, :, None]
    mixed = mixed.reshape(B, n_chunk * CHUNK, A_GROUPS, A_GROUP_DIM)[:, :T]
    return u * mixed

def mem_attend(q, mem_kv):
    s = jnp.einsum('bthd,bmhd->bhtm', q, mem_kv[:, :, 0]).astype(jnp.float32) * (MEM_HEAD_DIM ** -0.5)
    p = jax.nn.softmax(s, axis=-1).astype(q.dtype)
    return jnp.einsum('bhtm,bmhd->bthd', p, mem_kv[:, :, 1])

def sq_relu_mlp(x, w_up, w_down):
    return jnp.square(jax.nn.relu(x @ w_up)) @ w_down

def mixer_a(x, mem_kv, w_in, ln_g, ln_b, w_s, b_s, w_out):
    B, T = x.shape[:2]
    proj = x @ w_in
    uv = jax.nn.gelu(proj[..., :2 * A_WIDTH])
    u = uv[..., :A_WIDTH]
    v = layer_norm(uv[..., A_WIDTH:], ln_g, ln_b)
    mixed = spatial_gate(u.reshape(B, T, A_GROUPS, A_GROUP_DIM), v.reshape(B, T, A_GROUPS, A_GROUP_DIM), w_s, b_s)
    q_mem = proj[..., 2 * A_WIDTH:].reshape(B, T, MEM_HEADS, MEM_HEAD_DIM)
    o_mem = mem_attend(q_mem, mem_kv).reshape(B, T, MEM_WIDTH)
    return jnp.concatenate([mixed.reshape(B, T, A_WIDTH), o_mem], axis=-1) @ w_out, v

def mixer_b(x, pos, mem_kv, attend, w_in, w_out):
    B, T = x.shape[:2]
    proj = x @ w_in
    q = rope(proj[..., :NSA_WIDTH].reshape(B, T, NSA_HEADS, HEAD_DIM), pos)
    gates = jax.nn.sigmoid(proj[..., NSA_WIDTH:NSA_WIDTH + N_BRANCH * NSA_HEADS].reshape(B, T, NSA_HEADS, N_BRANCH))
    q_mem = proj[..., NSA_WIDTH + N_BRANCH * NSA_HEADS:].reshape(B, T, MEM_HEADS, MEM_HEAD_DIM)
    o_nsa = attend(q, gates)
    o_mem = mem_attend(q_mem, mem_kv).reshape(B, T, MEM_WIDTH)
    return jnp.concatenate([o_nsa, o_mem], axis=-1) @ w_out

def shared_rows(h, pos, w_kv_shared):
    B, T = h.shape[:2]
    kv = (h @ w_kv_shared).reshape(B, T, N_BRANCH, 2, NSA_KV_HEADS, HEAD_DIM)
    k = rope(kv[:, :, :, 0], pos)
    return jnp.stack([k, kv[:, :, :, 1]], axis=3)

def compress(rows, cmp_pe, w_phi1, w_phi2):
    B, L = rows.shape[:2]
    n_str = -(-L // CMP_STRIDE)
    x = jnp.pad(rows, ((0, 0), (0, n_str * CMP_STRIDE - L), (0, 0), (0, 0), (0, 0)))
    x = x.reshape(B, n_str, CMP_STRIDE, 2, NSA_KV_HEADS, HEAD_DIM)
    n_cmp = n_str - CMP_RATIO + 1
    w1 = w_phi1.reshape(CMP_RATIO, CMP_STRIDE, 2, HEAD_DIM, CMP_HIDDEN)
    h = jnp.einsum('lcd,lcde->ce', cmp_pe, w_phi1)[:, None, :]
    for j in range(CMP_RATIO):
        h = h + jnp.einsum('bnschd,scde->bnche', x, w1[j])[:, j:j + n_cmp]
    return jnp.einsum('bnche,ced->bnchd', jax.nn.gelu(h), w_phi2)

def to_sel_blocks(rows):
    B, L = rows.shape[:2]
    n_slc = -(-L // SEL_BLOCK)
    x = jnp.pad(rows, ((0, 0), (0, n_slc * SEL_BLOCK - L), (0, 0), (0, 0), (0, 0)))
    return x.reshape(B, n_slc, SEL_BLOCK, 2, NSA_KV_HEADS, HEAD_DIM)

def nsa_query_block(q, gates, t_pos, kv_cmp, slc_blocks, win_kv, win_pos):
    B, Q = q.shape[:2]
    dt = q.dtype
    scale = HEAD_DIM ** -0.5
    qg = q.reshape(B, Q, NSA_KV_HEADS, GQA_GROUP, HEAD_DIM)
    n_cmp = kv_cmp.shape[1]
    cmp_start = jnp.arange(n_cmp) * CMP_STRIDE
    m_cmp = (cmp_start + CMP_BLOCK - 1)[None, :] <= t_pos[:, None]
    s_cmp = jnp.einsum('bqgrd,bngd->bgrqn', qg, kv_cmp[:, :, 0]).astype(jnp.float32) * scale
    p_cmp = masked_softmax(s_cmp, m_cmp)
    o_cmp = jnp.einsum('bgrqn,bngd->bqgrd', p_cmp.astype(dt), kv_cmp[:, :, 1])
    n_slc = slc_blocks.shape[1]
    sel_start = jnp.arange(n_slc) * SEL_BLOCK
    overlap = ((cmp_start[:, None] < sel_start[None, :] + SEL_BLOCK)
               & (cmp_start[:, None] + CMP_BLOCK > sel_start[None, :])).astype(jnp.float32)
    imp = jnp.einsum('bgrqn,nj->bgqj', p_cmp, overlap)
    blk = jnp.arange(n_slc)[None, :]
    cur = (t_pos // SEL_BLOCK)[:, None]
    forced = (blk == 0) | (blk == cur) | (blk == cur - 1)
    causal = sel_start[None, :] <= t_pos[:, None]
    score = jnp.where(causal, imp + FORCE_BONUS * forced.astype(jnp.float32), NEG)
    n_top = min(SEL_TOPK, n_slc)
    top_val, top_idx = lax.top_k(score, n_top)
    bi = jnp.arange(B)[:, None, None, None]
    gi = jnp.arange(NSA_KV_HEADS)[None, :, None, None]
    sel = slc_blocks[bi, top_idx, :, :, gi, :]
    sel = sel.reshape(B, NSA_KV_HEADS, Q, n_top * SEL_BLOCK, 2, HEAD_DIM)
    k_pos = top_idx[..., None] * SEL_BLOCK + jnp.arange(SEL_BLOCK)
    m_sel = ((top_val > NEG / 2)[..., None] & (k_pos <= t_pos[None, None, :, None, None]))
    m_sel = m_sel.reshape(B, NSA_KV_HEADS, 1, Q, n_top * SEL_BLOCK)
    s_sel = jnp.einsum('bqgrd,bgqkd->bgrqk', qg, sel[..., 0, :]).astype(jnp.float32) * scale
    p_sel = masked_softmax(s_sel, m_sel)
    o_sel = jnp.einsum('bgrqk,bgqkd->bqgrd', p_sel.astype(dt), sel[..., 1, :])
    diff = t_pos[:, None] - win_pos[None, :]
    m_win = (diff >= 0) & (diff < WINDOW) & (win_pos[None, :] >= 0)
    s_win = jnp.einsum('bqgrd,bkgd->bgrqk', qg, win_kv[:, :, 0]).astype(jnp.float32) * scale
    p_win = masked_softmax(s_win, m_win)
    o_win = jnp.einsum('bgrqk,bkgd->bqgrd', p_win.astype(dt), win_kv[:, :, 1])
    g = gates.reshape(B, Q, NSA_KV_HEADS, GQA_GROUP, N_BRANCH, 1)
    o = g[..., 0, :] * o_cmp + g[..., 1, :] * o_sel + g[..., 2, :] * o_win
    return o.reshape(B, Q, NSA_WIDTH)

def run_trunk(x, pos, mem_kv, nsa_context, p):
    v_rows = []
    attend, nsa_state = None, None
    for l in range(DEPTH):
        if l < N_A_LAYERS:
            mix, v = mixer_a(x, mem_kv[l], p["w_in_a"][l], p["ln_v_g"][l], p["ln_v_b"][l],
                             p["w_spatial"][l], p["b_spatial"][l], p["w_out_a"][l])
            v_rows.append(v)
        else:
            if l == N_A_LAYERS:
                attend, nsa_state = nsa_context(x)
            i = l - N_A_LAYERS
            mix = mixer_b(x, pos, mem_kv[l], attend, p["w_in_b"][i], p["w_out_b"][i])
        x = layer_norm(DEEPNORM_ALPHA * x + mix, p["ln1_g"][l], p["ln1_b"][l])
        x = layer_norm(DEEPNORM_ALPHA * x + sq_relu_mlp(x, p["w_up"][l], p["w_down"][l]), p["ln2_g"][l], p["ln2_b"][l])
    return x, jnp.stack(v_rows), nsa_state

def setup_inputs(seed: int = 0) -> dict:
    key = jax.random.key(seed)
    ks = iter(jax.random.split(key, 40))

    def nrm(shape, scale):
        return jax.random.normal(next(ks), shape, jnp.float32) * scale

    n_pages = PAST_LEN // PAGE_SIZE
    n_used = DEC_BATCH * n_pages
    n_pool = n_used + max(1, n_used // 4)
    page_table = jax.random.permutation(next(ks), n_pool)[:n_used].reshape(DEC_BATCH, n_pages).astype(jnp.int32)
    win_buf = min(WINDOW, PAST_LEN)
    a_in = 2 * A_WIDTH + MEM_WIDTH
    b_in = NSA_WIDTH + N_BRANCH * NSA_HEADS + MEM_WIDTH
    return {
        "x_prompt": nrm((BATCH, SEQ, D_MODEL), 1.0),
        "x_sample": nrm((DEC_BATCH, DEC_SEQ, D_MODEL), 1.0),
        "cache_cmp_kv": nrm((n_pool, PAGE_SIZE, 2, NSA_KV_HEADS, HEAD_DIM), 1.0),
        "cache_slc_kv": nrm((n_pool, PAGE_SIZE, 2, NSA_KV_HEADS, HEAD_DIM), 1.0),
        "cache_win_kv": nrm((DEC_BATCH, win_buf, 2, NSA_KV_HEADS, HEAD_DIM), 1.0),
        "cache_mem_kv": nrm((DEPTH, DEC_BATCH, MEM_TOKENS, 2, MEM_HEADS, MEM_HEAD_DIM), 1.0),
        "page_table": page_table,
        "mem_prompt": nrm((BATCH, MEM_TOKENS, D_MODEL), 1.0),
        "w_in_a": nrm((N_A_LAYERS, D_MODEL, a_in), D_MODEL ** -0.5),
        "ln_v_g": 1.0 + nrm((N_A_LAYERS, A_WIDTH), 0.05),
        "ln_v_b": nrm((N_A_LAYERS, A_WIDTH), 0.02),
        "w_spatial": nrm((N_A_LAYERS, A_GROUPS, CHUNK, CHUNK), CHUNK ** -0.5),
        "b_spatial": 1.0 + nrm((N_A_LAYERS, A_GROUPS, CHUNK), 0.1),
        "w_out_a": nrm((N_A_LAYERS, A_WIDTH + MEM_WIDTH, D_MODEL), (A_WIDTH + MEM_WIDTH) ** -0.5 * DEEPNORM_BETA),
        "w_in_b": nrm((N_B_LAYERS, D_MODEL, b_in), D_MODEL ** -0.5),
        "w_out_b": nrm((N_B_LAYERS, NSA_WIDTH + MEM_WIDTH, D_MODEL), (NSA_WIDTH + MEM_WIDTH) ** -0.5 * DEEPNORM_BETA),
        "w_kv_shared": nrm((D_MODEL, N_BRANCH * 2 * KV_WIDTH), D_MODEL ** -0.5),
        "cmp_pe": nrm((CMP_BLOCK, 2, HEAD_DIM), 0.1),
        "w_phi1": nrm((CMP_BLOCK, 2, HEAD_DIM, CMP_HIDDEN), (CMP_BLOCK * HEAD_DIM) ** -0.5),
        "w_phi2": nrm((2, CMP_HIDDEN, HEAD_DIM), CMP_HIDDEN ** -0.5),
        "w_mem_kv": nrm((DEPTH, D_MODEL, 2 * MEM_WIDTH), D_MODEL ** -0.5),
        "ln1_g": 1.0 + nrm((DEPTH, D_MODEL), 0.05),
        "ln1_b": nrm((DEPTH, D_MODEL), 0.02),
        "ln2_g": 1.0 + nrm((DEPTH, D_MODEL), 0.05),
        "ln2_b": nrm((DEPTH, D_MODEL), 0.02),
        "w_up": nrm((DEPTH, D_MODEL, D_FF), D_MODEL ** -0.5),
        "w_down": nrm((DEPTH, D_FF, D_MODEL), D_FF ** -0.5 * DEEPNORM_BETA),
    }

def reference(x_prompt, x_sample, cache_cmp_kv, cache_slc_kv, cache_win_kv, cache_mem_kv, page_table, mem_prompt,
              w_in_a, ln_v_g, ln_v_b, w_spatial, b_spatial, w_out_a, w_in_b, w_out_b, w_kv_shared, cmp_pe,
              w_phi1, w_phi2, w_mem_kv, ln1_g, ln1_b, ln2_g, ln2_b, w_up, w_down):
    p = {"w_in_a": w_in_a, "ln_v_g": ln_v_g, "ln_v_b": ln_v_b, "w_spatial": w_spatial, "b_spatial": b_spatial,
         "w_out_a": w_out_a, "w_in_b": w_in_b, "w_out_b": w_out_b, "ln1_g": ln1_g, "ln1_b": ln1_b,
         "ln2_g": ln2_g, "ln2_b": ln2_b, "w_up": w_up, "w_down": w_down}

    Bp, S = x_prompt.shape[:2]
    pos_p = jnp.arange(S, dtype=jnp.int32)
    mem_kv_prompt = jnp.einsum('bmd,lde->lbme', mem_prompt, w_mem_kv).reshape(
        DEPTH, Bp, MEM_TOKENS, 2, MEM_HEADS, MEM_HEAD_DIM)

    def prompt_ctx(h):
        rows = shared_rows(h, pos_p, w_kv_shared)
        cmp_rows, slc_rows, win_rows = rows[:, :, 0], rows[:, :, 1], rows[:, :, 2]
        kv_cmp = compress(cmp_rows, cmp_pe, w_phi1, w_phi2)
        slc_blocks = to_sel_blocks(slc_rows)
        win_pad = jnp.pad(win_rows, ((0, 0), (WINDOW, 0), (0, 0), (0, 0), (0, 0)))

        def attend(q, gates):
            n_blk = S // SEL_Q_BLOCK
            qb = q.reshape(Bp, n_blk, SEL_Q_BLOCK, NSA_HEADS, HEAD_DIM).swapaxes(0, 1)
            gb = gates.reshape(Bp, n_blk, SEL_Q_BLOCK, NSA_HEADS, N_BRANCH).swapaxes(0, 1)

            def body(args):
                c, qc, gc = args
                t0 = c * SEL_Q_BLOCK
                t_pos = t0 + jnp.arange(SEL_Q_BLOCK, dtype=jnp.int32)
                win = lax.dynamic_slice_in_dim(win_pad, t0, WINDOW + SEL_Q_BLOCK, axis=1)
                win_pos = t0 - WINDOW + jnp.arange(WINDOW + SEL_Q_BLOCK, dtype=jnp.int32)
                return nsa_query_block(qc, gc, t_pos, kv_cmp, slc_blocks, win, win_pos)

            out = lax.map(body, (jnp.arange(n_blk, dtype=jnp.int32), qb, gb))
            return out.swapaxes(0, 1).reshape(Bp, S, NSA_WIDTH)

        return attend, (cmp_rows, slc_rows, win_rows[:, S - min(WINDOW, S):])

    y_prompt, _, (cmp_kv_prompt, slc_kv_prompt, win_kv_prompt) = run_trunk(
        x_prompt, pos_p, mem_kv_prompt, prompt_ctx, p)

    Bs, T = x_sample.shape[:2]
    past_len = page_table.shape[1] * PAGE_SIZE
    pos_s = past_len + jnp.arange(T, dtype=jnp.int32)
    n_buf = cache_win_kv.shape[1]

    def sample_ctx(h):
        rows = shared_rows(h, pos_s, w_kv_shared)
        new_cmp, new_slc, new_win = rows[:, :, 0], rows[:, :, 1], rows[:, :, 2]
        past_cmp = cache_cmp_kv[page_table].reshape(Bs, past_len, 2, NSA_KV_HEADS, HEAD_DIM)
        past_slc = cache_slc_kv[page_table].reshape(Bs, past_len, 2, NSA_KV_HEADS, HEAD_DIM)
        kv_cmp = compress(jnp.concatenate([past_cmp, new_cmp], axis=1), cmp_pe, w_phi1, w_phi2)
        slc_blocks = to_sel_blocks(jnp.concatenate([past_slc, new_slc], axis=1))
        win_all = jnp.concatenate([cache_win_kv, new_win], axis=1)
        win_pos = past_len - n_buf + jnp.arange(n_buf + T, dtype=jnp.int32)

        def attend(q, gates):
            return nsa_query_block(q, gates, pos_s, kv_cmp, slc_blocks, win_all, win_pos)

        return attend, (new_cmp, new_slc, win_all[:, T:])

    y_sample, gmlp_v_sample, (cmp_kv_sample, slc_kv_sample, win_kv_sample) = run_trunk(
        x_sample, pos_s, cache_mem_kv, sample_ctx, p)

    return (y_prompt, y_sample, cmp_kv_prompt, slc_kv_prompt, win_kv_prompt, mem_kv_prompt,
            cmp_kv_sample, slc_kv_sample, win_kv_sample, gmlp_v_sample)


_drawn_inputs = setup_inputs


def setup_inputs(seed=0):
    import zlib

    import numpy as np

    out = dict(_drawn_inputs(seed))
    spreads = {}
    factors = {'cache_cmp_kv': 3.864, 'cache_slc_kv': 6.299, 'ln_v_b': 2.841, 'cmp_pe': 5.979}
    for name, (base, spread) in spreads.items():
        noise = np.random.default_rng([zlib.crc32(name.encode()), seed]).standard_normal(out[name].shape)
        drawn = base * np.exp(spread * noise) if base else spread * noise
        out[name] = __import__('jax').numpy.asarray(drawn.astype(out[name].dtype))
    for name, factor in factors.items():
        out[name] = (out[name] * factor).astype(out[name].dtype)
    return out
```

```python
from contextlib import ExitStack

import numpy as np

import concourse.bass as bass
from concourse import mybir

F32 = mybir.dt.float32
F32R = mybir.dt.float32r
I32 = mybir.dt.int32
ACT = mybir.ActivationFunctionType
ALU = mybir.AluOpType
AX = mybir.AxisListType.X

P = 128
D = 1024
KD = D // P
SEQ, NB, DEC = 512, 8, 4
SAMP = NB * DEC
TOK = SEQ + SAMP
HALF = TOK // 2
NQT = SEQ // P
AW = 768
KA = AW // P
HD = 64
NH, NG, GQ = 12, 4, 3
FF = 4096
MEM = 256
PAST, PAGE = 1024, 128
STRIDE = 16
NSTR = PAST // STRIDE
NCS = NSTR - 1
NCP = SEQ // STRIDE - 1
ROW = 2 * NG * HD
EPS = 1e-5
ALPHA = 4.0 ** 0.25
SCALE = HD ** -0.5
NEG = -1e30
QROWS = NG * GQ * DEC

C_ID, C_ONE, C_CAUS, C_CMP, C_VAL = 0, 128, 256, 768, 896
C_COS, C_SIN, C_NEW, C_WIN = 897, 937, 977, 1037
C_OV, C_SUMR, C_J, C_BD, C_REP, C_K8, C_K16, C_EPS, C_MIX = 1041, 1055, 1103, 1117, 1125, 1157, 1158, 1159, 1160
NCONST = 1160

SLOT = 2048


def shape_constants():
    c = np.zeros((P, NCONST), np.float32)
    p = np.arange(P)
    c[:, C_ID:C_ID + P] = np.eye(P)
    c[:, C_ONE:C_ONE + P] = 1.0
    c[:, C_CAUS + 384:C_CAUS + 512] = np.where(p[None, :] <= p[:, None], 0.0, NEG)
    for i in range(NQT):
        n = np.arange(32)
        seen = (STRIDE * n[None, :] + 31 <= (P * i + p)[:, None]) & (n[None, :] < NCP)
        c[:, C_CMP + 32 * i:C_CMP + 32 * i + 32] = np.where(seen, 0.0, NEG)
    c[:, C_VAL] = (p >= 31)
    inv = (500000.0 ** (-np.arange(8, dtype=np.float32) / 8)).astype(np.float32)
    for j in range(NQT + 1):
        pos = (P * j + p if j < NQT else PAST + p % DEC).astype(np.float32)
        ang = pos[:, None] * inv[None, :]
        c[:, C_COS + 8 * j:C_COS + 8 * j + 8] = np.cos(ang)
        c[:, C_SIN + 8 * j:C_SIN + 8 * j + 8] = np.sin(ang)
    t = p % DEC
    for a in range(60):
        c[:, C_NEW + a] = np.where((a >= 28) & (a < 32) & (a - 28 <= t), 0.0, NEG)
    for s in range(4):
        c[:, C_WIN + s] = np.where(s >= t + 1, 0.0, NEG)
    for j in range(1, 15):
        c[:NCS, C_OV + j - 1] = (STRIDE * p[:NCS] < 64 * j + 64) & (STRIDE * p[:NCS] + 32 > 64 * j)
        c[:, C_J + j - 1] = j
    r = np.arange(QROWS)
    c[:QROWS, C_SUMR:C_SUMR + QROWS] = (r[:, None] // 12 == r[None, :] // 12) & (r[:, None] % 4 == r[None, :] % 4)
    c[:, C_BD:C_BD + 8] = p[:, None] // 4 == np.arange(8)[None, :]
    c[:DEC, C_REP:C_REP + 32] = p[:DEC, None] == np.arange(32)[None, :] % 4
    c[:, C_K8] = p % 8
    c[:, C_K16] = p % 16
    c[:, C_EPS] = EPS
    return c


def weight_slots(w):
    def cols(m, c0, n):
        return [(slice(0, P), slice(0, KD), m.rearrange("(k p) n -> p k n", p=P)[:, :, c0:c0 + n])]

    def merged(m, c0):
        m3 = m.rearrange("(h d) n -> d h n", d=HD)
        loads = [(slice(HD * e, HD * e + HD), slice(GQ * q, GQ * q + GQ),
                  m3[:, 6 * q + GQ * e:6 * q + GQ * e + GQ, c0:c0 + 256]) for q in range(2) for e in range(2)]
        return loads + [(slice(0, P), slice(KA, KD), m[AW:D, :].rearrange("(k p) n -> p k n", p=P)[:, :, c0:c0 + 256])]

    def down(m, half, tile):
        rows = m[half * FF // 2:(half + 1) * FF // 2, tile * P:(tile + 1) * P]
        return [(slice(0, P), slice(0, 16), rows.rearrange("(k p) n -> p k n", p=P))]

    slots = [cols(w["w_mem_kv"][l], 256 * c, 256) for l in range(2) for c in range(2)]
    slots += [cols(w["w_in_a"][0], 256 * c, 256) for c in range(7)]
    slots += [cols(w["w_out_a"][0], 256 * c, 256) for c in range(4)]
    mlp = [[], []]
    for l in range(2):
        for h in range(2):
            mlp[l] += [cols(w["w_up"][l], h * FF // 2 + 256 * c, 256) for c in range(8)]
            mlp[l] += [down(w["w_down"][l], h, m) for m in range(8)]
    slots += mlp[0]
    slots += [cols(w["w_kv_shared"], 256 * c, 256) for c in range(6)]
    slots += [cols(w["w_in_b"][0], c0, n) for c0, n in IN_B]
    slots += [merged(w["w_out_b"][0], 256 * c) for c in range(4)]
    slots += mlp[1]
    return slots


IN_B = [(0, 256), (256, 256), (512, 256), (768, 146), (914, 146)]
W_MEM, W_INA, W_OUTA, W_MLP0, W_KV, W_INB, W_OUTB, W_MLP1 = 0, 4, 11, 15, 47, 53, 58, 62
N_SLOTS = 94
T_MEM, T_INA, T_OUTA, T_MLP0 = 0, 8, 22, 30
T_KV = T_MLP0 + 2 * (16 + 8)
T_INB = T_KV + 30
T_OUTB = T_INB + 25
T_MLP1 = T_OUTB + 8


def build(nc, w, o, scratch):
    with ExitStack() as ctx:
        base = [(nc.sbuf_base + 31) // 32 * 32]

        def sb(name, shape, dt=F32, at=None):
            size = int(np.prod(shape[1:])) * 4
            if at is None:
                at = base[0]
                base[0] += (size + 31) // 32 * 32
            addr[name] = at
            return nc.alloc_sbuf_tensor_at(name, shape, dt, offset=at)

        addr = {}

        def sem(name):
            return ctx.enter_context(nc.semaphore(name))

        ps = ctx.enter_context(nc.psum_tensor("ps", [P, 8, 512], F32))

        cst = sb("cst", [P, NCONST])
        resid = sb("resid", [P, KD, TOK])
        XPAD = KD * TOK + 96
        x_hi = sb("x_hi", [P, XPAD], F32R)
        x_lo = sb("x_lo", [P, XPAD], F32R)
        w_raw = sb("w_raw", [P, 2, SLOT])
        w_hi = sb("w_hi", [P, 2, SLOT], F32R)
        w_lo = sb("w_lo", [P, 2, SLOT], F32R)
        arena = sb("arena", [P, 2 * 16 * TOK])
        h_hi = sb("h_hi", [P, 16, TOK], F32R, at=addr["arena"])
        h_lo = sb("h_lo", [P, 16, TOK], F32R, at=addr["arena"] + 16 * TOK * 4)
        xalt = sb("xalt", [P, 2 * KD * TOK], F32, at=addr["x_hi"])
        walt = sb("walt", [P, 4 * SLOT], F32, at=addr["w_hi"])
        sum1 = sb("sum1", [P, TOK])
        sum2 = sb("sum2", [P, TOK])
        sq = sb("sq", [P, 2, TOK])
        mean = sb("mean", [P, TOK])
        rstd = sb("rstd", [P, TOK])
        tmp = sb("tmp", [P, 2, TOK])
        lnp = sb("lnp", [P, 76])
        kc_s = sb("kc_s", [P, NB, 2, NSTR])
        vc_s = sb("vc_s", [NSTR, NB, NG * HD])
        pe_bias = sb("pe_bias", [P, 2])
        phi2 = sb("phi2", [P, 2, HD])
        kc_p = sb("kc_p", [P, 2, 32])
        vc_p = sb("vc_p", [32, NG * HD])
        pages_c = sb("pages_c", [P, 4], I32)
        rows_c = sb("rows_c", [P, 4], I32)
        pages_s = sb("pages_s", [P, NB], I32)
        rows_s = sb("rows_s", [P, NB], I32)
        q_bd = sb("q_bd", [P, 2, NB, QROWS])
        o_s = sb("o_s", [P, KD, SAMP])
        stat = sb("stat", [P, 64])
        assert base[0] <= nc.sbuf_usable_end, base[0]

        def x_tile(t, k):
            return t[:, k * TOK:(k + 1) * TOK]

        def x3(t):
            return t[:, 0:KD * TOK].rearrange("p (k t) -> p k t", k=KD)

        ident = cst[:, C_ID:C_ID + P]
        ones = cst[:, C_ONE:C_ONE + P]

        def region(t, at, *shape, parts=P):
            n = int(np.prod(shape))
            v = t[0:parts, at:at + n]
            names = "abcd"[:len(shape)]
            if len(shape) == 1:
                return v
            return v.rearrange(f"p ({' '.join(names)}) -> p {' '.join(names)}",
                               **{x: s for x, s in zip(names[:-1], shape[:-1])})

        stage_end = sem("stage_end")
        consts_in = sem("consts_in")
        raw_in = [sem("raw_in_even"), sem("raw_in_odd")]
        hi_ready = sem("hi_ready")
        split_ready = sem("split_ready")
        tile_done = sem("tile_done")
        read_act = sem("read_act")
        read_dve = sem("read_dve")
        outputs = sem("outputs")
        outputs_sp = sem("outputs_sp")
        act_step = sem("act_step")
        dve_step = sem("dve_step")
        pool_step = sem("pool_step")
        steps = {"act": 0, "dve": 0, "pool": 0}

        def act_chain(ins):
            steps["act"] += 1
            ins.then_inc(act_step, 1)
            return steps["act"]

        def dve_chain(ins):
            steps["dve"] += 1
            ins.then_inc(dve_step, 1)
            return steps["dve"]

        def pool_chain(ins):
            steps["pool"] += 1
            ins.then_inc(pool_step, 1)
            return steps["pool"]

        def meet(eng, stage):
            eng.drain().then_inc(stage_end, 1)
            eng.wait_ge(stage_end, 4 * (stage + 1))

        def tiles_through(s):
            return sum(tiles_of[:s + 1])

        slots = weight_slots(w)
        assert len(slots) == N_SLOTS
        loads_of = [len(s) for s in slots]
        mlp_tiles = ([2] * 8 + [1] * 8) * 2
        tiles_of = [2] * 15 + mlp_tiles + [5] * 11 + [2] * 4 + mlp_tiles

        def loaded(s):
            return 16 * sum(loads_of[i] for i in range(s % 2, s + 1, 2))

        dve_reads = [T_OUTA <= t < T_MLP0 or T_OUTB <= t < T_MLP1
                     or any(0 <= t - t0 < 48 and (t - t0) % 24 >= 16 for t0 in (T_MLP0, T_MLP1))
                     for t in range(T_MLP1 + 48)]

        def out_of(t):
            n = sum(x == dve_reads[t] for x in dve_reads[:t + 1])
            return (read_dve if dve_reads[t] else read_act), n

        def load_slot(sp, s, lots):
            for parts, ks, src in lots:
                n = src.shape[-1]
                dst = w_raw[parts, s % 2, 0:slot_k(s) * n].rearrange("p (k c) -> p k c", c=n)
                sp.dma_start(dst[:, ks, :], src).then_inc(raw_in[s % 2], 16)

        def slot_k(s):
            return max(ks.stop for _, ks, _ in slots[s])

        def slot_n(s):
            return slot_k(s) * slots[s][0][2].shape[-1]

        def split_hi(act, par, loaded_at, tiles_at, n):
            act.wait_ge(raw_in[par], loaded_at)
            if tiles_at is not None:
                act.wait_ge(tile_done, tiles_at)
            nc.scalar.activation(w_hi[:, par, 0:n], w_raw[:, par, 0:n], ACT.Copy).then_inc(hi_ready, 1)

        def split_lo(dve, s1, par, n):
            dve.wait_ge(hi_ready, s1)
            nc.vector.tensor_tensor(w_lo[:, par, 0:n], w_raw[:, par, 0:n], w_hi[:, par, 0:n].bitcast(F32),
                                    ALU.subtract).then_inc(split_ready, 1)

        def act_split(act, s):
            if s < N_SLOTS:
                split_hi(act, s % 2, loaded(s), tiles_through(s - 2) if s >= 2 else None, slot_n(s))

        def dve_split(dve, s):
            if s < N_SLOTS:
                split_lo(dve, s + 1, s % 2, slot_n(s))

        def product(out, terms, inc=None):
            for n, (lhsT, rhs) in enumerate(terms):
                mm = nc.tensor.matmul(out, lhsT, rhs, start=n == 0, stop=n == len(terms) - 1)
            if inc is not None:
                mm.then_inc(inc, 1)

        def split_terms(a_hi, a_lo, b_hi, b_lo):
            return [(a_hi, b_hi), (a_hi, b_lo), (a_lo, b_hi)]

        def feature_tile(pe, par, bank, c0, nk, width, src_hi, src_lo):
            wv_hi = w_hi[:, par, 0:nk * width].rearrange("p (k c) -> p k c", c=width)
            wv_lo = w_lo[:, par, 0:nk * width].rearrange("p (k c) -> p k c", c=width)
            for half in range(2):
                cols = slice(half * HALF, (half + 1) * HALF)
                terms = []
                for k in range(nk):
                    terms += split_terms(wv_hi[:, k, c0:c0 + P], wv_lo[:, k, c0:c0 + P],
                                         src_hi(k)[:, cols], src_lo(k)[:, cols])
                product(ps[:, bank + half, 0:HALF], terms, tile_done if half else None)

        def xk(t):
            return lambda k: x_tile(t, k)

        def pair(t):
            return ps[:, 2 * (t % 2):2 * (t % 2) + 2, 0:HALF]

        def halves(ap):
            return ap.rearrange("p (h t) -> p h t", h=2)

        def pe_feature_slots(pe, s0, n_slots, t0):
            for s in range(s0, s0 + n_slots):
                pe.wait_ge(split_ready, s + 1)
                for n in range(2):
                    t = t0 + 2 * (s - s0) + n
                    if t >= 2:
                        pe.wait_ge(*out_of(t - 2))
                    feature_tile(pe, s % 2, 2 * (t % 2), P * n, KD, 256, xk(x_hi), xk(x_lo))

        def pe_token_slot(pe, s, t0, n_tok_tiles, a_hi, a_lo, width):
            pe.wait_ge(split_ready, s + 1)
            wv_hi = w_hi[:, s % 2, 0:KD * width].rearrange("p (k c) -> p k c", c=width)
            wv_lo = w_lo[:, s % 2, 0:KD * width].rearrange("p (k c) -> p k c", c=width)
            for j in range(n_tok_tiles):
                t = t0 + j
                if t >= 2:
                    pe.wait_ge(*out_of(t - 2))
                terms = []
                for k in range(KD):
                    terms += split_terms(a_hi(k, j), a_lo(k, j), wv_hi[:, k, :], wv_lo[:, k, :])
                product(ps[:, 2 * (t % 2), 0:width], terms, tile_done)

        sums_used = sem("sums_used")
        sq_ready = sem("sq_ready")
        sum1_done = sem("sum1_done")
        sum2_done = sem("sum2_done")
        mean_ready = sem("mean_ready")
        std_ready = sem("std_ready")
        var_ready = sem("var_ready")
        centred = sem("centred")
        ln_hi = sem("ln_hi")
        ln_lo = sem("ln_lo")
        n_ln = {"pe": 0, "act": 0, "dve": 0}
        n_lt = {"act": 0, "dve": KA}

        LN_TILES = [KA, KD, KD, KD, KD]

        def sums_at(ln):
            return sum(LN_TILES[:ln]) + ln + 1

        def act_square(act, src, par, ready, ready_at, ln, m):
            act.wait_ge(ready, ready_at)
            act.wait_ge(sum2_done, sums_at(ln) + m - 1)
            nc.scalar.activation(sq[:, par, :], src, ACT.Square).then_inc(sq_ready, 1)

        def pool_sums(pool, src, par, ready, ready_at, ln, m):
            pool.wait_ge(ready, ready_at)
            pool.wait_ge(sum1_done, sums_at(ln) + m)
            nc.gpsimd.tensor_tensor(sum1[:, :], sum1[:, :], src, ALU.add).then_inc(sum1_done, 1)
            pool.wait_ge(sq_ready, sum(LN_TILES[:ln]) + m + 1)
            pool.wait_ge(sum2_done, sums_at(ln) + m)
            nc.gpsimd.tensor_tensor(sum2[:, :], sum2[:, :], sq[:, par, :], ALU.add).then_inc(sum2_done, 1)

        def pool_clear_sums(pool, ln):
            if ln:
                pool.wait_ge(sums_used, ln)
            nc.gpsimd.memset(sum1[:, :], 0.0).then_inc(sum1_done, 1)
            nc.gpsimd.memset(sum2[:, :], 0.0).then_inc(sum2_done, 1)

        def pe_ln(pe, ln):
            pe.wait_ge(sum1_done, sums_at(ln) + LN_TILES[ln])
            pe.wait_ge(sum2_done, sums_at(ln) + LN_TILES[ln])
            for b, v in ((4, sum1), (6, sum2)):
                for half in range(2):
                    mm = nc.tensor.matmul(ps[:, b + half, 0:HALF], ones, v[:, half * HALF:(half + 1) * HALF],
                                          start=True, stop=True)
            mm.then_inc(sums_used, 1)

        def act_ln_stats(act, n_feat):
            n = n_ln["act"] = n_ln["act"] + 1
            act.wait_ge(sums_used, n)
            nc.scalar.activation(halves(mean[:, :]), ps[:, 4:6, 0:HALF], ACT.Copy, scale=1.0 / n_feat).then_inc(mean_ready, 1)
            act.wait_ge(var_ready, n)
            nc.scalar.activation(tmp[:, 0, :], tmp[:, 0, :], ACT.Sqrt,
                                 bias=cst[:, C_EPS:C_EPS + 1]).then_inc(std_ready, 1)

        def dve_ln_stats(dve, n_feat):
            n = n_ln["dve"] = n_ln["dve"] + 1
            dve.wait_ge(mean_ready, n)
            c = dve_chain(nc.vector.tensor_tensor(tmp[:, 1, :], mean[:, :], mean[:, :], ALU.mult))
            dve.wait_ge(dve_step, c)
            nc.vector.scalar_tensor_tensor(out=halves(tmp[:, 0, :]), in0=ps[:, 6:8, 0:HALF], scalar=1.0 / n_feat,
                                           in1=halves(tmp[:, 1, :]), op0=ALU.mult, op1=ALU.subtract).then_inc(var_ready, 1)
            dve.wait_ge(std_ready, n)
            c = dve_chain(nc.vector.reciprocal(rstd[:, :], tmp[:, 0, :]))
            dve.wait_ge(dve_step, c)

        def dve_centre(dve, x):
            c = dve_chain(nc.vector.tensor_tensor(x, x, mean[:, :], ALU.subtract))
            dve.wait_ge(dve_step, c)
            nc.vector.tensor_tensor(x, x, rstd[:, :], ALU.mult).then_inc(centred, 1)

        def act_gain(act, x, gain, shift, hi):
            n = n_lt["act"] = n_lt["act"] + 1
            act.wait_ge(centred, n)
            if hi is not None:
                nc.scalar.activation(hi, x, ACT.Identity, bias=shift, scale=gain)
            nc.scalar.activation(x, x, ACT.Identity, bias=shift, scale=gain).then_inc(ln_hi, 1)

        def ln_resid(which, eng, row):
            if which == "act":
                act_ln_stats(eng, D)
                for m in range(KD):
                    act_gain(eng, resid[:, m, :], lnp[:, row + m:row + m + 1], lnp[:, row + 8 + m:row + 9 + m],
                             x_tile(x_hi, m))
            else:
                dve_ln_stats(eng, D)
                for m in range(KD + 2):
                    if m < KD:
                        dve_centre(eng, resid[:, m, :])
                    if m >= 2:
                        n = n_lt["dve"] = n_lt["dve"] + 1
                        eng.wait_ge(ln_hi, n)
                        nc.vector.tensor_tensor(x_tile(x_lo, m - 2), resid[:, m - 2, :],
                                                x_tile(x_hi, m - 2).bitcast(F32), ALU.subtract).then_inc(ln_lo, 1)

        sq_h_ready = sem("sq_h_ready")
        h_hi_ready = sem("h_hi_ready")
        h_lo_ready = sem("h_lo_ready")
        MLP_W, MLP_T = (W_MLP0, W_MLP1), (T_MLP0, T_MLP1)

        def each(eng, count, body, last_apart):
            n = count - 1 if last_apart else count
            with eng.Fori(0, n) as i:
                body(i, False)
            if last_apart:
                body(count - 1, True)

        def pe_mlp(pe, l):
            for h in range(2):
                s0, t0 = MLP_W[l] + 16 * h, MLP_T[l] + 24 * h
                up_read, down_read = out_of(t0)[1], out_of(t0 + 16)[1]

                def up(i, last):
                    for e in range(2):
                        pe.wait_ge(split_ready, s0 + e + 1 + 2 * i)
                        for n in range(2):
                            pe.wait_ge(read_act, up_read + 2 * e + n - 2 + 4 * i)
                            feature_tile(pe, (s0 + e) % 2, 2 * ((t0 + n) % 2), P * n, KD, 256, xk(x_hi), xk(x_lo))

                def down(i, last):
                    for e in range(2):
                        pe.wait_ge(split_ready, s0 + 8 + e + 1 + 2 * i)
                        pe.wait_ge(read_dve, down_read + e - 2 + 2 * i)
                        feature_tile(pe, (s0 + e) % 2, 2 * ((t0 + e) % 2), 0, 16, P,
                                     lambda k: h_hi[:, k, :], lambda k: h_lo[:, k, :])

                if h == 0:
                    pe.wait_ge(ln_lo, 8 * (2 * l + 1))
                pe.wait_ge(*out_of(t0 - 1))
                each(pe, 4, up, False)
                pe.wait_ge(*out_of(t0 + 15))
                pe.wait_ge(h_lo_ready, 32 * l + 16 * h + 16)
                each(pe, 4, down, False)

        def act_mlp(act, l):
            for h in range(2):
                s0, t0, q0 = MLP_W[l] + 16 * h, MLP_T[l] + 24 * h, 32 * l + 16 * h

                def split(i, e, phase, tiles):
                    s = s0 + phase + e + 1
                    split_hi(act, s % 2, loaded(s) + 16 * i, tiles, SLOT)

                def up(i, last):
                    for e in range(2):
                        split(i, e, 0, t0 + 2 * e + 4 * i)
                        for n in range(2):
                            t, q = t0 + 2 * e + n, q0 + 2 * e + n
                            act.wait_ge(tile_done, t + 1 + 4 * i)
                            act.wait_ge(sq_h_ready, max(q - 1, 0) + 4 * i)
                            nc.scalar.activation(halves(tmp[:, n, :]), pair(t), ACT.Relu).then_inc(read_act, 1)
                            act.wait_ge(read_act, out_of(t)[1] + 4 * i)
                            nc.scalar.activation(h_hi[:, bass.ds(4 * i + 2 * e + n, 1), :], tmp[:, n:n + 1, :],
                                                 ACT.Square).then_inc(h_hi_ready, 1)

                def down(i, last):
                    for e in range(2):
                        if not (last and e == 1 and s0 + 16 == N_SLOTS):
                            split(i, e, 8, t0 + 16 + e + 2 * i)
                        if h == 1:
                            t = t0 + 16 + e
                            act_square(act, resid[:, bass.ds(2 * i + e, 1), :], e, read_dve, out_of(t)[1] + 2 * i,
                                       2 * l + 2, 2 * i + e)

                each(act, 4, up, False)
                each(act, 4, down, h == 1)

        def dve_mlp(dve, l):
            for h in range(2):
                s0, t0, q0 = MLP_W[l] + 16 * h, MLP_T[l] + 24 * h, 32 * l + 16 * h

                def up(i, last):
                    for e in range(2):
                        split_lo(dve, s0 + e + 2 + 2 * i, (s0 + e + 1) % 2, SLOT)
                        for n in range(2):
                            q = q0 + 2 * e + n
                            dve.wait_ge(sq_h_ready, q + 1 + 4 * i)
                            dve.wait_ge(h_hi_ready, q + 1 + 4 * i)
                            j = bass.ds(4 * i + 2 * e + n, 1)
                            nc.vector.tensor_tensor(h_lo[:, j, :], sq[:, n:n + 1, :], h_hi[:, j, :].bitcast(F32),
                                                    ALU.subtract).then_inc(h_lo_ready, 1)

                def down(i, last):
                    for e in range(2):
                        if not (last and e == 1 and s0 + 16 == N_SLOTS):
                            split_lo(dve, s0 + 8 + e + 2 + 2 * i, (s0 + e + 1) % 2, SLOT)
                        t = t0 + 16 + e
                        dve.wait_ge(tile_done, t + 1 + 2 * i)
                        r = resid[:, bass.ds(2 * i + e, 1), :].rearrange("p a (h t) -> p (a h) t", h=2)
                        if h == 0:
                            nc.vector.scalar_tensor_tensor(out=r, in0=r, scalar=ALPHA, in1=pair(t), op0=ALU.mult,
                                                           op1=ALU.add).then_inc(read_dve, 1)
                        else:
                            nc.vector.tensor_tensor(r, r, pair(t), ALU.add).then_inc(read_dve, 1)

                each(dve, 4, up, False)
                each(dve, 4, down, h == 1)

        def pool_mlp(pool, l):
            pool_clear_sums(pool, 2 * l + 2)
            for h in range(2):
                t0, q0 = MLP_T[l] + 24 * h, 32 * l + 16 * h

                def up(i, last):
                    for e in range(2):
                        for n in range(2):
                            t, q = t0 + 2 * e + n, q0 + 2 * e + n
                            pool.wait_ge(read_act, out_of(t)[1] + 4 * i)
                            pool.wait_ge(h_lo_ready, max(q - 1, 0) + 4 * i)
                            nc.gpsimd.tensor_tensor(sq[:, n, :], tmp[:, n, :], tmp[:, n, :],
                                                    ALU.mult).then_inc(sq_h_ready, 1)

                def down(i, last):
                    for e in range(2):
                        pool_sums(pool, resid[:, bass.ds(2 * i + e, 1), :].rearrange("p a t -> p (a t)"), e,
                                  read_dve, out_of(t0 + 16 + e)[1] + 2 * i, 2 * l + 2, 2 * i + e)

                each(pool, 4, up, False)
                if h == 1:
                    each(pool, 4, down, False)

        def sp_mlp(sp, l):
            m_up, m_down = w["w_up"][l].rearrange("(k p) n -> p k n", p=P), w["w_down"][l]
            for h in range(2):
                s0 = MLP_W[l] + 16 * h

                def up(i, last):
                    for e in range(2):
                        s = s0 + e
                        sp.wait_ge(split_ready, s - 1 + 2 * i)
                        dst = w_raw[:, s % 2, :].rearrange("p (k c) -> p k c", c=256)
                        sp.dma_start(dst, m_up[:, :, bass.ds(h * FF // 2 + 256 * e + 512 * i, 256)]).then_inc(raw_in[s % 2], 16)

                def down(i, last):
                    for e in range(2):
                        s = s0 + 8 + e
                        sp.wait_ge(split_ready, s - 1 + 2 * i)
                        dst = w_raw[:, s % 2, :].rearrange("p (k c) -> p k c", c=P)
                        rows = m_down[h * FF // 2:(h + 1) * FF // 2, bass.ds(P * e + 2 * P * i, P)]
                        sp.dma_start(dst, rows.rearrange("(k p) n -> p k n", p=P)).then_inc(raw_in[s % 2], 16)

                each(sp, 4, up, False)
                each(sp, 4, down, False)

        def sp_slots(sp, s0, n):
            for s in range(s0, s0 + n):
                if s >= 2:
                    sp.wait_ge(split_ready, s - 1)
                load_slot(sp, s, slots[s])

        small_in = sem("small_in")
        phi1_in = sem("phi1_in")
        phi1_b_in = sem("phi1_b_in")
        cmp_in = [sem("cmp_in_even"), sem("cmp_in_odd")]
        rows_ready = sem("rows_ready")
        turned = sem("turned")
        turned_act = sem("turned_act")
        turned_dve = sem("turned_dve")
        params_turned = sem("params_turned")
        params_read = sem("params_read")
        hidden = sem("hidden")
        gelued = sem("gelued")
        blocks = sem("blocks")
        blocks_read = sem("blocks_read")

        cmp_raw = [xalt, walt]
        xc = region(arena, 0, 2, 8, 512)
        phi1 = region(arena, 8192, 16, 2, P)
        gel = region(arena, 12288, 2, 512)
        pe_rows = region(arena, 13312, P, parts=32)
        pe_cols = region(arena, 13440, 32)
        ln_rows = region(arena, 13472, P, parts=76)

        def load_phi1(eng, dst, done):
            for e in range(2):
                src = w["w_phi1"].rearrange("(l e) c d n -> e d l c n", e=2)[e]
                for c in range(2):
                    eng.dma_start(dst[HD * e:HD * e + HD, :, c, :], src[:, :, c, :]).then_inc(done, 16)

        def sp_stage0(sp):
            pt = w["page_table"]
            for q in range(4):
                sp.dma_start(pages_c[:, q:q + 1], bass.AP(pt.tensor, pt.offset + 16 * q, [[1, 16], [0, 8], [1, 1]])
                             ).then_inc(small_in, 16)
            for b in range(NB):
                sp.dma_start(pages_s[:, b:b + 1], bass.AP(pt.tensor, pt.offset + 8 * b, [[1, 8], [0, 16], [1, 1]])
                             ).then_inc(small_in, 16)
            sp.dma_start(cst[:, :], w["consts"]).then_inc(consts_in, 16)
            row = 0
            for l in range(2):
                for name in ("ln1_g", "ln1_b", "ln2_g", "ln2_b"):
                    sp.dma_start(ln_rows[row:row + 8, :], w[name][l].rearrange("(k p) -> k p", p=P)).then_inc(small_in, 16)
                    row += 8
            for name in ("ln_v_g", "ln_v_b"):
                sp.dma_start(ln_rows[row:row + KA, :], w[name][0].rearrange("(k p) -> k p", p=P)).then_inc(small_in, 16)
                row += KA
            for c in range(2):
                for e in range(2):
                    src = w["cmp_pe"].rearrange("(l e) c d -> e c l d", e=2)[e, c]
                    sp.dma_start(pe_rows[16 * c:16 * c + 16, HD * e:HD * e + HD], src).then_inc(small_in, 16)
            for c in range(2):
                sp.dma_start(phi2[:, c, :], w["w_phi2"][c]).then_inc(small_in, 16)
            load_phi1(sp, phi1, phi1_in)

        N_SMALL = 16 * (4 + NB + 8 + 2 + 4 + 2)
        PHI1_ONCE = 16 * 4
        cmp_rows_dram = w["cache_cmp_kv"].rearrange("n (a s) c h d -> (n a) (s c h d)", s=STRIDE)

        def pool_stage0(pool):
            pool.wait_ge(rows_ready, 1)
            for q in range(4):
                if q >= 2:
                    pool.wait_ge(turned, 16 * (q - 1))
                nc.gpsimd.indirect_dma_start(cmp_raw[q % 2][:, 0:STRIDE * ROW], None, cmp_rows_dram,
                                             bass.IndirectOffsetOnAxis(rows_c[:, q:q + 1], 0)).then_inc(cmp_in[q % 2], 16)

        def turn_reader(n):
            return ("dve", n // 2 + 1) if n % 2 == 0 else ("act", n // 2 + 1)

        def pe_compress_turn(pe, raw, n0, n_str, first_wait):
            at = raw[0:n_str, 0:STRIDE * ROW].rearrange("p (s e x) -> p s e x", s=8, e=2)
            for c in range(2):
                for s in range(8):
                    n = n0 + 8 * c + s
                    if n - 2 >= first_wait:
                        who, v = turn_reader(n - 2)
                        pe.wait_ge(turned_dve if who == "dve" else turned_act, v)
                    for e in range(2):
                        for pr in range(2):
                            mm = nc.tensor.transpose(ps[:, 4 + n % 2, (2 * e + pr) * n_str:(2 * e + pr + 1) * n_str],
                                                     at[:, s, e, (2 * c + pr) * P:(2 * c + pr + 1) * P],
                                                     ident[0:n_str, 0:n_str])
                    mm.then_inc(turned, 1)

        def compress_copy(eng, who, dst, n0, n_str, free_at):
            for c in range(2):
                if free_at is not None:
                    eng.wait_ge(hidden, free_at + c)
                for s in range(8):
                    n = n0 + 8 * c + s
                    if turn_reader(n)[0] != who:
                        continue
                    eng.wait_ge(turned, n + 1)
                    for e in range(2):
                        for hp in range(2):
                            src = ps[HD * hp:HD * hp + HD, 4 + n % 2, 2 * e * n_str:2 * (e + 1) * n_str]
                            to = dst[HD * e:HD * e + HD, c, s, :].rearrange("p (g h n) -> p g h n", g=2, h=2)[:, :, hp, :]
                            src = src.rearrange("p (g n) -> p g n", g=2)
                            ins = nc.scalar.activation(to, src, ACT.Copy) if who == "act" else nc.vector.tensor_copy(to, src)
                    ins.then_inc(turned_act if who == "act" else turned_dve, 1)

        def pe_compress_hidden(pe, q, src, wts, n0, n_seq, n_str, last):
            for c in range(2):
                for m in range(14, 16):
                    who, v = turn_reader(n0 + 8 * c + m - 8)
                    pe.wait_ge(turned_dve if who == "dve" else turned_act, v)
                if q:
                    pe.wait_ge(gelued, 2 * (q - 1) + c + 1)
                cols = NG * n_seq * n_str
                out = ps[:, 6 + c, 0:cols]
                out1 = out.rearrange("p (a n) -> p a n", n=n_str)[:, :, 0:n_str - 1]
                for s in range(8):
                    nc.tensor.matmul(out, wts[:, s, c, :], src[:, c, s, :], start=s == 0, stop=False,
                                     skip_group_check=True)
                for s in range(8):
                    nxt = src[:, c, s, :].rearrange("p (a n) -> p a n", n=n_str)[:, :, 1:n_str]
                    mm = nc.tensor.matmul(out1, wts[:, 8 + s, c, :], nxt, start=False, stop=s == 7,
                                          skip_group_check=True)
                mm.then_inc(hidden, 1)

        def act_compress_gelu(act, q, dst, cols):
            for c in range(2):
                act.wait_ge(hidden, 2 * q + c + 1)
                if q:
                    act.wait_ge(blocks, q)
                nc.scalar.activation(dst[:, c, 0:cols], ps[:, 6 + c, 0:cols], ACT.Gelu_apprx_tanh,
                                     bias=pe_bias[:, c:c + 1]).then_inc(gelued, 1)

        def pe_compress_out(pe, q, src, n_seq, n_str):
            pe.wait_ge(gelued, 2 * q + 2)
            if q:
                pe.wait_ge(blocks_read, q)
            per = n_seq * n_str
            for h in range(NG):
                e, pr = h % 2, h // 2
                nc.tensor.matmul(ps[HD * e:HD * e + HD, 0, pr * per:(pr + 1) * per], phi2[:, 0, :],
                                 src[:, 0, h * per:(h + 1) * per], start=True, stop=True)
            for b in range(n_seq):
                for h in range(NG):
                    at = h * per + b * n_str
                    mm = nc.tensor.matmul(ps[0:n_str, 1, (b * NG + h) * HD:(b * NG + h + 1) * HD],
                                          src[:, 1, at:at + n_str], phi2[:, 1, :], start=True, stop=True)
            mm.then_inc(blocks, 1)

        def pe_stage0(pe):
            pe.wait_ge(consts_in, 16)
            pe.wait_ge(small_in, N_SMALL)
            nc.tensor.transpose(ps[:, 7, 0:76], ln_rows[:, :], ident[0:76, 0:76])
            nc.tensor.transpose(ps[:, 7, 128:160], pe_rows[:, :], ident[0:32, 0:32]).then_inc(params_turned, 1)
            pe.wait_ge(params_read, 1)
            pe.wait_ge(phi1_in, PHI1_ONCE)
            for c in range(2):
                for l in range(16):
                    mm = nc.tensor.matmul(ps[:, 7, 256 + c:257 + c], phi1[:, l, c, :],
                                          pe_cols[:, 16 * c + l:16 * c + l + 1], start=l == 0, stop=l == 15)
            mm.then_inc(params_turned, 1)
            pe.wait_ge(params_read, 2)
            for q in range(4):
                pe.wait_ge(cmp_in[q % 2], 16 * (q // 2 + 1))
                pe_compress_turn(pe, cmp_raw[q % 2], 16 * q, P, 0)
                if q:
                    pe_compress_out(pe, q - 1, gel, 2, NSTR)
                pe_compress_hidden(pe, q, xc, phi1, 16 * q, 2, NSTR, False)
            pe_compress_out(pe, 3, gel, 2, NSTR)
            meet(pe, 0)

        def act_stage0(act):
            for q in range(4):
                compress_copy(act, "act", xc, 16 * q, P, 2 * q - 1 if q else None)
                if q:
                    pass
                act_compress_gelu(act, q, gel, 512)
            meet(act, 0)

        def dve_stage0(dve):
            dve.wait_ge(consts_in, 16)
            dve.wait_ge(small_in, N_SMALL)
            nc.vector.tensor_scalar(rows_c[:, :], pages_c[:, :], float(PAGE // STRIDE), cst[:, C_K8:C_K8 + 1],
                                    ALU.mult, ALU.add)
            nc.vector.tensor_scalar(rows_s[:, :], pages_s[:, :], float(PAGE // 8), cst[:, C_K16:C_K16 + 1],
                                    ALU.mult, ALU.add).then_inc(rows_ready, 1)
            dve.wait_ge(params_turned, 1)
            nc.vector.tensor_copy(lnp[:, :], ps[:, 7, 0:76])
            nc.vector.tensor_copy(pe_cols[:, :], ps[:, 7, 128:160]).then_inc(params_read, 1)
            dve.wait_ge(params_turned, 2)
            nc.vector.tensor_copy(pe_bias[:, :], ps[:, 7, 256:258]).then_inc(params_read, 1)
            for q in range(5):
                if q < 4:
                    compress_copy(dve, "dve", xc, 16 * q, P, 2 * q - 1 if q else None)
                if q:
                    dve.wait_ge(blocks, q)
                    b = 2 * (q - 1)
                    nc.vector.tensor_copy(kc_s[:, b:b + 2, :, :].rearrange("p b g n -> p g b n"),
                                          ps[:, 0, 0:256].rearrange("p (g b n) -> p g b n", g=2, b=2))
                    nc.vector.tensor_copy(vc_s[:, b:b + 2, :],
                                          ps[0:NSTR, 1, :].rearrange("p (b x) -> p b x", b=2)).then_inc(blocks_read, 1)
            meet(dve, 0)

        rows_in = sem("rows_in")
        x_turned = sem("x_turned")
        x_read = sem("x_read")
        x_hi_ready = sem("x_hi_ready")
        mem_hi_ready = sem("mem_hi_ready")
        operands_ready = sem("operands_ready")
        x_rows = region(arena, 0, 5, D)
        m_rows = region(arena, 5 * D, 2, D)
        m_hi, m_lo = h_lo[:, 0:4, :].rearrange("p a t -> p (a t)"), h_lo[:, 4:8, :].rearrange("p a t -> p (a t)")
        m_hi, m_lo = [x[:, 0:2048].rearrange("p (k m) -> p k m", m=MEM) for x in (m_hi, m_lo)]
        mkv = region(arena, 13184, 2, 2, 512)

        def pool_stage1(pool):
            meet(pool, 0)
            pool.dma_start(x_rows[:, 0:4, :], w["x_prompt"][0].rearrange("(j p) d -> p j d", p=P)).then_inc(rows_in, 16)
            pool.dma_start(x_rows[0:SAMP, 4, :], w["x_sample"].rearrange("b t d -> (b t) d")).then_inc(rows_in, 16)
            pool.dma_start(m_rows[:, :, :], w["mem_prompt"][0].rearrange("(j p) d -> p j d", p=P)).then_inc(rows_in, 16)
            pool.wait_ge(*out_of(7))
            for l in range(2):
                pool.dma_start(o["mem_kv"][l].rearrange("(j p) x -> p j x", p=P), mkv[:, l, :, :]).then_inc(outputs, 16)
            pool.wait_ge(outputs, 32)
            meet(pool, 1)

        def pe_stage1(pe):
            pe.wait_ge(rows_in, 48)
            for n in range(14):
                if n >= 4:
                    pe.wait_ge(x_read, n - 3)
                for k in range(4):
                    if n < 10:
                        j, kk = n // 2, 4 * (n % 2) + k
                        m = P if j < 4 else SAMP
                        src = x_rows[0:m, j, kk * P:(kk + 1) * P]
                    else:
                        m = P
                        src = m_rows[:, (n - 10) // 2, (4 * (n % 2) + k) * P:(4 * (n % 2) + k + 1) * P]
                    mm = nc.tensor.transpose(ps[:, 4 + n % 4, k * m:(k + 1) * m], src, ident[0:m, 0:m])
                mm.then_inc(x_turned, 1)
            pe.wait_ge(operands_ready, 1)
            for s in range(W_MEM, W_MEM + 4):
                pe_token_slot(pe, s, 2 * s, 2, lambda k, j: m_hi[:, k, j * P:(j + 1) * P],
                              lambda k, j: m_lo[:, k, j * P:(j + 1) * P], 256)
            meet(pe, 1)

        def act_stage1(act):
            for n in range(10, 14):
                act.wait_ge(x_turned, n + 1)
                k = 4 * (n % 2)
                nc.scalar.activation(m_hi[:, k:k + 4, (n - 10) // 2 * P:((n - 10) // 2 + 1) * P],
                                     ps[:, 4 + n % 4, :].rearrange("p (k m) -> p k m", k=4), ACT.Copy).then_inc(mem_hi_ready, 1)
            act_split(act, 0)
            for s in range(W_MEM, W_MEM + 4):
                act_split(act, s + 1)
                for j in range(2):
                    t = 2 * s + j
                    act.wait_ge(tile_done, t + 1)
                    nc.scalar.activation(mkv[:, s // 2, j, 256 * (s % 2):256 * (s % 2) + 256],
                                         ps[:, 2 * (t % 2), 0:256], ACT.Copy).then_inc(read_act, 1)
            act.wait_ge(x_read, 10)
            for k in range(2):
                nc.scalar.activation(x3(x_hi)[:, 4 * k:4 * k + 4, :], resid[:, 4 * k:4 * k + 4, :], ACT.Copy).then_inc(x_hi_ready, 1)
            meet(act, 1)

        def dve_stage1(dve):
            for n in range(14):
                dve.wait_ge(x_turned, n + 1)
                k = 4 * (n % 2)
                bank = ps[:, 4 + n % 4, :]
                if n < 10:
                    m, c = (P, P * (n // 2)) if n < 8 else (SAMP, SEQ)
                    nc.vector.tensor_copy(resid[:, k:k + 4, c:c + m],
                                          bank[:, 0:4 * m].rearrange("p (k m) -> p k m", k=4)).then_inc(x_read, 1)
                else:
                    dve.wait_ge(mem_hi_ready, n - 9)
                    cols = slice((n - 10) // 2 * P, ((n - 10) // 2 + 1) * P)
                    ins = nc.vector.tensor_tensor(m_lo[:, k:k + 4, cols], bank.rearrange("p (k m) -> p k m", k=4),
                                                  m_hi[:, k:k + 4, cols].bitcast(F32), ALU.subtract)
                    ins.then_inc(x_read, 1)
            dve.wait_ge(x_read, 14)
            nc.vector.memset(x_hi[:, KD * TOK:XPAD].bitcast(F32), 0.0)
            nc.vector.memset(x_lo[:, KD * TOK:XPAD].bitcast(F32), 0.0).then_inc(operands_ready, 1)
            for s in range(W_MEM, W_MEM + 5):
                dve_split(dve, s)
            for k in range(2):
                dve.wait_ge(x_hi_ready, k + 1)
                nc.vector.tensor_tensor(x3(x_lo)[:, 4 * k:4 * k + 4, :], resid[:, 4 * k:4 * k + 4, :],
                                        x3(x_hi)[:, 4 * k:4 * k + 4, :].bitcast(F32), ALU.subtract)
            meet(dve, 1)

        def strided(start, *dims):
            return bass.AP(start.tensor, start.offset, [list(start.ap[0])] + [list(d) for d in dims])

        TURN_LAG, SUM_LAG = 3, 5

        def unit_sems(name):
            return {k: sem(f"{name}_{k}") for k in
                    ("scored", "max_ready", "exp_done", "normed", "turned", "pt_ready", "summed", "hi", "lo")}

        def pe_units(pe, us, sm):
            tiles = 0
            for n in range(len(us) + SUM_LAG):
                if n < len(us):
                    u = us[n]
                    if n >= 4:
                        pe.wait_ge(sm["exp_done"], n - 3)
                    nc.tensor.matmul(ps[:, 2 + n % 4, 0:u["n"]], u["q"], u["k"], start=True,
                                     stop=True).then_inc(sm["scored"], 1)
                v = n - TURN_LAG
                if 0 <= v < len(us):
                    u = us[v]
                    pe.wait_ge(sm["normed"], v + 1)
                    if v >= 2:
                        pe.wait_ge(sm["pt_ready"], v - 1)
                    for c in range(0, u["n"], P):
                        m = min(P, u["n"] - c)
                        mm = nc.tensor.transpose(ps[0:m, 6 + v % 2, c:c + P], u["p"][:, v % 4, c:c + m], ident)
                    mm.then_inc(sm["turned"], 1)
                v = n - SUM_LAG
                if v >= 0:
                    u = us[v]
                    pe.wait_ge(sm["pt_ready"], v + 1)
                    if tiles >= 2:
                        pe.wait_ge(sm["lo"], tiles - 1)
                    e, i = u["place"]
                    chunks = range(0, u["n"], P)
                    for c in chunks:
                        mm = nc.tensor.matmul(ps[HD * e:HD * e + HD, tiles % 2, i * P:(i + 1) * P], u["v"](c // P),
                                              u["pt"][0:min(P, u["n"] - c), v % 4, c:c + P],
                                              start=u["first"] and c == 0, stop=u["last"] and c == chunks[-1])
                    mm.then_inc(sm["summed"], 1)
                    tiles += u["closes"] is not None

        def act_units(act, us, sm):
            tiles = 0
            for n in range(len(us) + SUM_LAG + 1):
                v = n - TURN_LAG - 1
                if 0 <= v < len(us):
                    u = us[v]
                    act.wait_ge(sm["turned"], v + 1)
                    if v >= 4:
                        act.wait_ge(sm["summed"], v - 3)
                    m = min(P, u["n"])
                    nc.scalar.activation(u["pt"][0:m, v % 4, 0:max(P, u["n"])], ps[0:m, 6 + v % 2, 0:max(P, u["n"])],
                                         ACT.Copy).then_inc(sm["pt_ready"], 1)
                if n < len(us):
                    u, r = us[n], n % 4
                    act.wait_ge(sm["max_ready"], n + 1)
                    if n >= 4:
                        act.wait_ge(sm["turned"], n - 3)
                    nc.scalar.activation(u["p"][:, n % 4, 0:u["n"]], ps[:, 2 + n % 4, 0:u["n"]], ACT.Exp,
                                         bias=stat[:, 4 + r:5 + r], scale=SCALE if u["mask"] is None else -1.0,
                                         accum_out=stat[:, 8 + r:9 + r]).then_inc(sm["exp_done"], 1)
                v = n - SUM_LAG - 1
                if v >= 0 and us[v]["closes"] is not None:
                    act.wait_ge(sm["summed"], v + 1)
                    nc.scalar.activation(x_tile(x_hi, us[v]["closes"])[:, 0:SEQ], ps[:, tiles % 2, :],
                                         ACT.Copy).then_inc(sm["hi"], 1)
                    tiles += 1

        def dve_units(dve, us, sm):
            tiles = 0
            for n in range(len(us) + SUM_LAG + 2):
                v = n - 2
                if 0 <= v < len(us):
                    r = v % 4
                    dve.wait_ge(sm["exp_done"], v + 1)
                    recip = dve_chain(nc.vector.reciprocal(stat[:, 12 + r:13 + r], stat[:, 8 + r:9 + r]))
                if n < len(us):
                    u, r = us[n], n % 4
                    dve.wait_ge(sm["scored"], n + 1)
                    sc = ps[:, 2 + n % 4, 0:u["n"]]
                    if n >= 4:
                        dve.wait_ge(sm["exp_done"], n - 3)
                    if u["mask"] is None:
                        c = dve_chain(nc.vector.reduce_max(stat[:, r:r + 1], sc, AX))
                        dve.wait_ge(dve_step, c)
                        nc.vector.tensor_scalar(stat[:, 4 + r:5 + r], stat[:, r:r + 1], -SCALE, None,
                                                ALU.mult).then_inc(sm["max_ready"], 1)
                    else:
                        nc.vector.tensor_tensor_reduce(sc, sc, u["mask"], -SCALE, -3 * NEG, ALU.add, ALU.min,
                                                       stat[:, 4 + r:5 + r]).then_inc(sm["max_ready"], 1)
                if 0 <= v < len(us):
                    u, r = us[v], v % 4
                    pr = u["p"][:, v % 4, 0:u["n"]]
                    dve.wait_ge(dve_step, recip)
                    if u["gate"] is None:
                        ins = nc.vector.tensor_scalar(pr, pr, stat[:, 12 + r:13 + r], None, ALU.mult)
                    else:
                        ins = nc.vector.tensor_scalar(pr, pr, stat[:, 12 + r:13 + r], u["gate"], ALU.mult, ALU.mult)
                    ins.then_inc(sm["normed"], 1)
                v = n - SUM_LAG - 2
                if v >= 0 and us[v]["closes"] is not None:
                    dve.wait_ge(sm["hi"], tiles + 1)
                    k = us[v]["closes"]
                    nc.vector.tensor_tensor(x_tile(x_lo, k)[:, 0:SEQ], ps[:, tiles % 2, :],
                                            x_tile(x_hi, k)[:, 0:SEQ].bitcast(F32), ALU.subtract).then_inc(sm["lo"], 1)
                    tiles += 1

        def act_samples(act, k0, sm):
            nc.scalar.activation(x3(x_hi)[:, k0:KD, SEQ:TOK], o_s[:, k0:KD, :], ACT.Copy).then_inc(sm, 1)

        def dve_samples(dve, k0, sm):
            dve.wait_ge(sm, 1)
            nc.vector.tensor_tensor(x3(x_lo)[:, k0:KD, SEQ:TOK], o_s[:, k0:KD, :],
                                    x3(x_hi)[:, k0:KD, SEQ:TOK].bitcast(F32), ALU.subtract)

        def mem_sems(name):
            return {k: sem(f"{name}_{k}") for k in
                    ("k_in0", "k_in1", "v_in", "q_ready", "turned", "kt_ready", "scored", "max_ready", "exp_done", "normed",
                     "p_turned", "pt_ready", "summed", "merged")}

        def pool_mem_loads(pool, l, M, sm):
            kv = w["cache_mem_kv"][l].rearrange("b (p s) c h d -> b p s (c h d)", s=2)
            pool.memset(M["q"], 0.0).then_inc(sm["q_ready"], 1)
            for b in range(NB):
                if b >= 2:
                    pool.wait_ge(sm["turned"], b - 1)
                pool.dma_start(M["k"][:, b % 2, :, :], kv[b, :, :, 0:256]).then_inc(sm["k_in0" if b % 2 == 0 else "k_in1"], 16)
                pool.dma_start(M["v"][:, b, :, :], kv[b, :, :, 256:512]).then_inc(sm["v_in"], 16)

        def pe_mem(pe, M, sm):
            def score(b):
                pe.wait_ge(sm["kt_ready"], b + 1)
                if b == 0:
                    pe.wait_ge(sm["q_ready"], 2)
                for tt in range(2):
                    mm = nc.tensor.matmul(ps[:, 0, 0:MEM], M["q"][:, tt, b, :], M["kt"][:, b % 2, tt, :],
                                          start=b == 0 and tt == 0, stop=b == NB - 1 and tt == 1)
                mm.then_inc(sm["scored"], 1)

            for b in range(NB):
                pe.wait_ge(sm["k_in0" if b % 2 == 0 else "k_in1"], 16 * (b // 2 + 1))
                if b >= 2:
                    pe.wait_ge(sm["kt_ready"], b - 1)
                for tt in range(2):
                    for s in range(2):
                        mm = nc.tensor.transpose(ps[:, 4 + b % 2, (2 * tt + s) * P:(2 * tt + s + 1) * P],
                                                 M["k"][:, b % 2, s, tt * P:(tt + 1) * P], ident)
                mm.then_inc(sm["turned"], 1)
                if b >= 1:
                    score(b - 1)
            score(NB - 1)
            pe.wait_ge(sm["normed"], 1)
            for s in range(2):
                mm = nc.tensor.transpose(ps[:, 6, s * P:(s + 1) * P], M["p"][:, s * P:(s + 1) * P], ident)
            mm.then_inc(sm["p_turned"], 1)
            pe.wait_ge(sm["pt_ready"], 1)
            pe.wait_ge(sm["v_in"], 16 * NB)
            for b in range(NB):
                for tt in range(2):
                    c = 16 * b + 8 * tt
                    product(ps[:, 7, c:c + 8], [(M["v"][:, b, s, tt * P:(tt + 1) * P], M["pt"][:, s, c:c + 8])
                                                for s in range(2)], sm["summed"] if b == NB - 1 and tt == 1 else None)

        def act_mem(act, M, sm):
            for b in range(NB):
                act.wait_ge(sm["turned"], b + 1)
                if b >= 2:
                    act.wait_ge(sm["scored"], b - 1)
                nc.scalar.activation(M["kt"][:, b % 2, :, :], ps[:, 4 + b % 2, :].rearrange("p (t m) -> p t m", t=2),
                                     ACT.Copy).then_inc(sm["kt_ready"], 1)
            act.wait_ge(sm["max_ready"], 1)
            nc.scalar.activation(M["p"], ps[:, 0, 0:MEM], ACT.Exp, bias=stat[:, 17:18], scale=SCALE,
                                 accum_out=stat[:, 18:19]).then_inc(sm["exp_done"], 1)

        def dve_mem(dve, M, sm):
            dve.wait_ge(sm["q_ready"], 1)
            for h in range(NG):
                e, tt = h % 2, h // 2
                dst = strided(M["q"][HD * e:HD * e + HD, tt, 0, 4 * h:4 * h + 1], (P + 16, NB), (1, DEC))
                c = nc.vector.tensor_copy(dst, M["qt"][HD * e:HD * e + HD, tt, SEQ:TOK].rearrange("p (b t) -> p b t", b=NB))
            c.then_inc(sm["q_ready"], 1)
            dve.wait_ge(sm["scored"], NB)
            c = dve_chain(nc.vector.reduce_max(stat[:, 16:17], ps[:, 0, 0:MEM], AX))
            dve.wait_ge(dve_step, c)
            nc.vector.tensor_scalar(stat[:, 17:18], stat[:, 16:17], -SCALE, None, ALU.mult).then_inc(sm["max_ready"], 1)
            dve.wait_ge(sm["exp_done"], 1)
            c = dve_chain(nc.vector.reciprocal(stat[:, 19:20], stat[:, 18:19]))
            dve.wait_ge(dve_step, c)
            nc.vector.tensor_scalar(M["p"], M["p"], stat[:, 19:20], None, ALU.mult).then_inc(sm["normed"], 1)
            dve.wait_ge(sm["p_turned"], 1)
            nc.vector.tensor_copy(M["pt"], ps[:, 6, 0:MEM].rearrange("p (s m) -> p s m", s=2)).then_inc(sm["pt_ready"], 1)
            dve.wait_ge(sm["summed"], 1)
            for h in range(NG):
                e, tt = h % 2, h // 2
                src = strided(ps[HD * e:HD * e + HD, 7, 4 * h:4 * h + 1], (16, NB), (1, DEC))
                c = nc.vector.tensor_copy(o_s[HD * e:HD * e + HD, KA + tt, :].rearrange("p (b t) -> p b t", b=NB), src)
            c.then_inc(sm["merged"], 1)

        ws_in = sem("ws_in")
        ws_turned = sem("ws_turned")
        ws_copied = sem("ws_copied")
        ws_masked = sem("ws_masked")
        ws_repeated = sem("ws_repeated")
        wbd_ready = sem("wbd_ready")
        vt_turned = sem("vt_turned")
        vt_read = sem("vt_read")
        mixed = sem("mixed")
        mix_read = sem("mix_read")
        gated = sem("gated")
        gated_hi = sem("gated_hi")
        v_out = sem("v_out")
        u_free = sem("u_free")
        km_turned = sem("km_turned")
        km_read = sem("km_read")
        u_t = region(arena, 0, KA, TOK)
        v_t = region(arena, 3264, KA, TOK)
        qm_a = region(arena, 6528, 2, TOK)
        v_rows = region(arena, 7616, 5, AW)
        ws = region(arena, 15232, 4, P)
        wst = region(arena, 15744, 4, P)
        bsp = region(arena, 16256, 4, P)
        wbd = region(arena, 16768, 4, SAMP, parts=SAMP)
        km_a = region(arena, 16896, 2, MEM)
        MA = {"v": region(arena, 7616, NB, 2, 256), "k": region(arena, 0, 2, 2, 256), "kt": region(arena, 1024, 2, 2, MEM),
              "q": region(arena, 2048, 2, NB, P), "p": region(arena, 4096, 256), "pt": region(arena, 4352, 2, P), "qt": qm_a}
        pr_a, pt_a = region(arena, 4608, 4, 256), region(arena, 11712, 4, 256)
        mem_a, ua, samples_a = mem_sems("mem_a"), unit_sems("ua"), sem("samples_a")

        def group_parts(n):
            g = 2 * (n // 3)
            return [[(g, slice(0, P))], [(g, slice(0, HD)), (g + 1, slice(HD, P))], [(g + 1, slice(0, P))]][n % 3]

        def mem_units(qt, kt, rows, p, pt):
            return [{"q": qt[HD * e:HD * e + HD, tt, i * P:(i + 1) * P], "k": kt[HD * e:HD * e + HD, tt, :], "n": MEM,
                     "mask": None, "gate": None, "first": True, "last": True, "place": (e, i), "p": p, "pt": pt,
                     "closes": KA + tt if (i, e) == (NQT - 1, 1) else None,
                     "v": lambda c, h=2 * tt + e: rows[:, c, 256 + HD * h:256 + HD * h + HD]}
                    for tt in range(2) for i in range(NQT) for e in range(2)]

        units_a = mem_units(qm_a, km_a, mkv[:, 0, :, :], pr_a, pt_a)

        def pool_stage2(pool):
            pool.dma_start(ws[:, :, :], w["w_spatial"][0].rearrange("g t s -> t g s")).then_inc(ws_in, 16)
            bs = w["b_spatial"]
            pool.dma_start(bsp[:, :, :].rearrange("p g t -> p (g t)"),
                           bass.AP(bs.tensor, bs.offset, [[0, P], [1, 4 * P]])).then_inc(ws_in, 16)
            pool.wait_ge(ws_copied, 1)
            for g in range(4):
                ins = nc.gpsimd.affine_select(out=wst[:, g, :], in_=wst[:, g, :], compare_op=ALU.is_ge, fill=0.0, base=0,
                                              pattern=[[1, P]], channel_multiplier=-1)
            ins.then_inc(ws_masked, 1)
            pool_clear_sums(pool, 0)
            for m in range(KA):
                pool_sums(pool, v_t[:, m, :], m % 2, *out_of(T_INA + KA + m), 0, m)
            pool.wait_ge(u_free, 1)
            pool.wait_ge(v_out, 16)
            pool_mem_loads(pool, 0, MA, mem_a)
            meet(pool, 2)

        def pe_stage2(pe):
            pe.wait_ge(ws_in, 32)
            for g in range(4):
                mm = nc.tensor.transpose(ps[:, 7, g * P:(g + 1) * P], ws[:, g, :], ident)
            mm.then_inc(ws_turned, 1)
            pe.wait_ge(ws_masked, 1)
            for g in range(4):
                mm = nc.tensor.matmul(ps[0:SAMP, 6, 4 * g:4 * g + 4], cst[0:DEC, C_REP:C_REP + SAMP], wst[0:DEC, g, 0:DEC],
                                      start=True, stop=True)
            mm.then_inc(ws_repeated, 1)
            pe_feature_slots(pe, W_INA, 7, T_INA)
            pe.wait_ge(wbd_ready, 1)
            pe_ln(pe, 0)
            pe.wait_ge(ln_hi, KA)
            for n in range(10):
                j, part = n // 2, n % 2
                m = P if j < 4 else SAMP
                if n >= 4:
                    pe.wait_ge(vt_read, n - 3)
                for x in range(4 * part, min(4 * part + 4, KA)):
                    mm = nc.tensor.transpose(ps[0:m, 4 + n % 4, (x % 4) * P:(x % 4 + 1) * P],
                                             v_t[:, x, j * P:j * P + m], ident)
                mm.then_inc(vt_turned, 1)
            pe.wait_ge(vt_read, 10)
            pe.wait_ge(*out_of(T_OUTA - 1))
            for n in range(KA):
                if n >= 2:
                    pe.wait_ge(mix_read, n - 1)
                for g, pp in group_parts(n):
                    cols = slice(n * P + pp.start, n * P + pp.stop)
                    for j in range(NQT):
                        nc.tensor.matmul(ps[pp, 2 * (n % 2), j * P:(j + 1) * P], v_rows[:, j, cols], wst[:, g, :],
                                         start=True, stop=True)
                    mm = nc.tensor.matmul(ps[pp, 2 * (n % 2) + 1, 0:SAMP], v_rows[0:SAMP, 4, cols], wbd[:, g, :],
                                          start=True, stop=True)
                mm.then_inc(mixed, 1)
            for j in range(2):
                for tt in range(2):
                    mm = nc.tensor.transpose(ps[:, 7, tt * MEM + j * P:tt * MEM + (j + 1) * P],
                                             mkv[:, 0, j, tt * P:(tt + 1) * P], ident)
            mm.then_inc(km_turned, 1)
            pe.wait_ge(mix_read, KA)
            pe.wait_ge(km_read, 1)
            pe_mem(pe, MA, mem_a)
            pe.wait_ge(mem_a["merged"], 1)
            pe_units(pe, units_a, ua)
            meet(pe, 2)

        def act_stage2(act):
            for s in range(W_INA, W_INA + 7):
                act_split(act, s + 1)
                for n in range(2):
                    t = T_INA + 2 * (s - W_INA) + n
                    x = t - T_INA
                    act.wait_ge(tile_done, t + 1)
                    dst = (u_t[:, x, :] if x < KA else v_t[:, x - KA, :] if x < 2 * KA else qm_a[:, x - 2 * KA, :])
                    nc.scalar.activation(halves(dst), pair(t), ACT.Gelu_apprx_tanh if x < 2 * KA else ACT.Copy).then_inc(read_act, 1)
                    if KA <= x < 2 * KA:
                        act_square(act, v_t[:, x - KA, :], x % 2, *out_of(t), 0, x - KA)
            act_ln_stats(act, AW)
            for m in range(KA):
                act_gain(act, v_t[:, m, :], lnp[:, 64 + m:65 + m], lnp[:, 70 + m:71 + m], None)
            for n in range(KA):
                act.wait_ge(gated, n + 1)
                nc.scalar.activation(x_tile(x_hi, n), u_t[:, n, :], ACT.Copy).then_inc(gated_hi, 1)
            act_mem(act, MA, mem_a)
            act_units(act, units_a, ua)
            act_samples(act, KA, samples_a)
            meet(act, 2)

        def dve_stage2(dve):
            dve.wait_ge(ws_turned, 1)
            nc.vector.tensor_copy(wst[:, :, :], ps[:, 7, :].rearrange("p (g t) -> p g t", g=4)).then_inc(ws_copied, 1)
            dve.wait_ge(ws_repeated, 1)
            for g in range(4):
                ins = nc.vector.tensor_tensor(wbd[:, g, :].rearrange("p (b t) -> p b t", b=NB),
                                              strided(ps[0:SAMP, 6, 4 * g:4 * g + 1], (0, NB), (1, DEC)),
                                              strided(cst[0:SAMP, C_BD:C_BD + 1], (1, NB), (0, DEC)), ALU.mult)
            ins.then_inc(wbd_ready, 1)
            for s in range(W_INA, W_INA + 7):
                dve_split(dve, s + 1)
            dve_ln_stats(dve, AW)
            for m in range(KA):
                dve_centre(dve, v_t[:, m, :])
            for n in range(10):
                j, part = n // 2, n % 2
                m = P if j < 4 else SAMP
                dve.wait_ge(vt_turned, n + 1)
                width = 512 if part == 0 else AW - 512
                nc.vector.tensor_copy(v_rows[0:m, j, 512 * part:512 * part + width],
                                      ps[0:m, 4 + n % 4, 0:width]).then_inc(vt_read, 1)
            for n in range(KA):
                dve.wait_ge(mixed, n + 1)
                for g, pp in group_parts(n):
                    nc.vector.tensor_tensor(v_t[pp, n, 0:SEQ].rearrange("p (j t) -> p j t", j=NQT),
                                            ps[pp, 2 * (n % 2), :].rearrange("p (j t) -> p j t", j=NQT),
                                            strided(bsp[pp, g, 0:1], (0, NQT), (1, P)), ALU.add)
                    ins = nc.vector.tensor_tensor(v_t[pp, n, SEQ:TOK].rearrange("p (b t) -> p b t", b=NB),
                                                  ps[pp, 2 * (n % 2) + 1, 0:SAMP].rearrange("p (b t) -> p b t", b=NB),
                                                  strided(bsp[pp, g, 0:1], (0, NB), (1, DEC)), ALU.add)
                ins.then_inc(mix_read, 1)
                dve.wait_ge(mix_read, n + 1)
                nc.vector.tensor_tensor(u_t[:, n, :], u_t[:, n, :], v_t[:, n, :], ALU.mult).then_inc(gated, 1)
                if n >= 1:
                    dve.wait_ge(gated_hi, n)
                    nc.vector.tensor_tensor(x_tile(x_lo, n - 1), u_t[:, n - 1, :], x_tile(x_hi, n - 1).bitcast(F32), ALU.subtract)
            dve.wait_ge(gated_hi, KA)
            nc.vector.tensor_tensor(x_tile(x_lo, KA - 1), u_t[:, KA - 1, :], x_tile(x_hi, KA - 1).bitcast(F32),
                                    ALU.subtract).then_inc(u_free, 1)
            dve.wait_ge(km_turned, 1)
            nc.vector.tensor_copy(km_a[:, :, :], ps[:, 7, :].rearrange("p (t m) -> p t m", t=2)).then_inc(km_read, 1)
            dve_mem(dve, MA, mem_a)
            dve_units(dve, units_a, ua)
            dve_samples(dve, KA, samples_a)
            meet(dve, 2)

        def sp_stage2(sp):
            sp.wait_ge(vt_read, 10)
            sp.dma_start(o["gmlp_v"][0].rearrange("b t c -> (b t) c"), v_rows[0:SAMP, 4, :]).then_inc(v_out, 16)

        def pe_out(pe, l):
            pe_feature_slots(pe, W_OUTA if l == 0 else W_OUTB, 4, T_OUTA if l == 0 else T_OUTB)
            pe_ln(pe, 2 * l + 1)

        def act_out(act, l):
            s0, t0 = (W_OUTA, T_OUTA) if l == 0 else (W_OUTB, T_OUTB)
            for s in range(s0, s0 + 4):
                act_split(act, s + 1)
                for n in range(2):
                    m = 2 * (s - s0) + n
                    act_square(act, resid[:, m, :], m % 2, *out_of(t0 + m), 2 * l + 1, m)
            ln_resid("act", act, 32 * l)

        def dve_out(dve, l):
            s0, t0 = (W_OUTA, T_OUTA) if l == 0 else (W_OUTB, T_OUTB)
            for s in range(s0, s0 + 4):
                dve_split(dve, s + 1)
                for n in range(2):
                    m = 2 * (s - s0) + n
                    dve.wait_ge(tile_done, t0 + m + 1)
                    nc.vector.scalar_tensor_tensor(out=halves(resid[:, m, :]), in0=halves(resid[:, m, :]), scalar=ALPHA,
                                                   in1=pair(t0 + m), op0=ALU.mult, op1=ALU.add).then_inc(read_dve, 1)
            ln_resid("dve", dve, 32 * l)

        def pool_out(pool, l):
            t0 = T_OUTA if l == 0 else T_OUTB
            pool_clear_sums(pool, 2 * l + 1)
            for m in range(KD):
                pool_sums(pool, resid[:, m, :], m % 2, *out_of(t0 + m), 2 * l + 1, m)

        roped = sem("roped")
        kv_out = [sem("kv_out_even"), sem("kv_out_odd")]
        heads_turned = sem("heads_turned")
        heads_read = sem("heads_read")
        gates_ready = sem("gates_ready")
        gates_out = sem("gates_out")
        gates_in = sem("gates_in")
        q_bd_clear = sem("q_bd_clear")
        q_rows = region(arena, 0, 5, AW)
        k_rows = region(arena, 3840, 2, 5, 256)
        v_bank = region(arena, 6400, 5, 2, 256)
        gm = region(arena, 8960, 5, 292)
        q_t = region(arena, 10432, KA, TOK)
        qm_b = region(arena, 13696, 2, TOK)
        k_t = region(arena, 14784, 2, 2, TOK)
        gs = region(arena, 16960, NB, 3, parts=QROWS)

        def q_place(head):
            g, r = divmod(head, GQ)
            return (g // 2 * GQ + r) * 2 + g % 2

        Q_RUNS = [[(0, 3), (3, 1)], [(4, 2), (6, 2)], [(8, 1), (9, 3)]]

        def x_tok(t):
            return lambda k, j: t[:, k * TOK + j * P:k * TOK + (j + 1) * P]

        def rope(dve, v, pitch, heads):
            n = 5 * heads * 8
            a, b = (strided(v[:, 0, c:c + 1], (pitch, 5), (HD, heads), (1, 8)) for c in (0, 8))
            cos, sin = (strided(cst[:, c:c + 1], (8, 5), (0, heads), (1, 8)) for c in (C_COS, C_SIN))
            t = [x[:, i, 0:n].rearrange("p (j h x) -> p j h x", j=5, h=heads) for x in (tmp, sq) for i in range(2)]
            nc.vector.tensor_tensor(t[0], a, cos, ALU.mult)
            nc.vector.tensor_tensor(t[1], b, sin, ALU.mult)
            nc.vector.tensor_tensor(t[2], b, cos, ALU.mult)
            c = dve_chain(nc.vector.tensor_tensor(t[3], a, sin, ALU.mult))
            dve.wait_ge(dve_step, c)
            nc.vector.tensor_tensor(a, t[0], t[1], ALU.subtract)
            nc.vector.tensor_tensor(b, t[2], t[3], ALU.add).then_inc(roped, 1)
            dve.wait_ge(roped, sum(1 for _ in range(rope_count[0] + 1)))
            rope_count[0] += 1

        rope_count = [0]

        def turn_list():
            def key_groups(br, buf):
                gr = [[(k_rows[:, buf, j, pr * P:(pr + 1) * P], P, j * P) for j in range(NQT)] for pr in range(2)]
                return gr + [[(k_rows[0:SAMP, buf, NQT, pr * P:(pr + 1) * P], SAMP, pr * SAMP) for pr in range(2)]]

            q = [[(q_rows[:, j, x * P:(x + 1) * P], P, j * P) for j in range(NQT)] for x in range(KA)]
            q += [[(q_rows[0:SAMP, NQT, x * P:(x + 1) * P], SAMP, x * SAMP) for x in range(KA)]]
            m = [[(gm[:, j, 36 + tt * P:36 + (tt + 1) * P], P, j * P) for j in range(NQT)] for tt in range(2)]
            m += [[(gm[0:SAMP, NQT, 36 + tt * P:36 + (tt + 1) * P], SAMP, tt * SAMP) for tt in range(2)]]
            return [key_groups(1, 0), key_groups(2, 1), q, m]

        TURNS = turn_list()

        def turn_base(x):
            return sum(len(g) for g in TURNS[:x])

        def pe_turn(pe, x):
            for i, group in enumerate(TURNS[x]):
                n = turn_base(x) + i
                if n >= 4:
                    pe.wait_ge(heads_read, n - 3)
                for src, m, c in group:
                    mm = nc.tensor.transpose(ps[:, 4 + n % 4, c:c + m], src, ident[0:m, 0:m])
                mm.then_inc(heads_turned, 1)

        def act_turned(act, x, dsts):
            for i, (dst, cols) in enumerate(dsts):
                n = turn_base(x) + i
                act.wait_ge(heads_turned, n + 1)
                src = ps[:, 4 + n % 4, 0:cols]
                if len(dst.shape) == 3:
                    src = src.rearrange("p (a t) -> p a t", t=SAMP)
                nc.scalar.activation(dst, src, ACT.Copy).then_inc(heads_read, 1)

        def key_dsts(br):
            return [(k_t[:, br - 1, pr, 0:SEQ], SEQ) for pr in range(2)] + [(k_t[:, br - 1, :, SEQ:TOK], 2 * SAMP)]

        def pe_stage3(pe):
            pe.wait_ge(ln_lo, 16)
            for c in range(6):
                pe_token_slot(pe, W_KV + c, T_KV + 5 * c, 5, x_tok(x_hi), x_tok(x_lo), 256)
                if c == 3:
                    pe.wait_ge(roped, 2)
                    pe_turn(pe, 0)
            for c in range(5):
                pe_token_slot(pe, W_INB + c, T_INB + 5 * c, 5, x_tok(x_hi), x_tok(x_lo), IN_B[c][1])
                if c == 0:
                    pe.wait_ge(roped, 3)
                    pe_turn(pe, 1)
            pe.wait_ge(roped, 4)
            pe_turn(pe, 2)
            pe_turn(pe, 3)
            meet(pe, 3)

        def act_stage3(act):
            for c in range(6):
                act_split(act, W_KV + c + 1)
                if c in (2, 4):
                    act.wait_ge(kv_out[0 if c == 2 else 1], 32)
                for j in range(5):
                    t = T_KV + 5 * c + j
                    act.wait_ge(tile_done, t + 1)
                    dst = v_bank[:, j, c // 2 - 1, :] if c in (3, 5) else k_rows[:, {0: 0, 1: 1, 2: 0, 4: 1}[c], j, :]
                    nc.scalar.activation(dst, ps[:, 2 * (t % 2), 0:256], ACT.Copy).then_inc(read_act, 1)
                if c == 3:
                    act_turned(act, 0, key_dsts(1))
            for c in range(5):
                if c < 4:
                    act_split(act, W_INB + c + 1)
                for j in range(5):
                    t = T_INB + 5 * c + j
                    act.wait_ge(tile_done, t + 1)
                    if c < 3:
                        for first, n in Q_RUNS[c]:
                            to, at = q_place(first), 64 * (first - 4 * c)
                            ins = nc.scalar.activation(strided(q_rows[:, j, to * HD:to * HD + 1], (2 * HD, n), (1, HD)),
                                                       ps[:, 2 * (t % 2), at:at + n * HD].rearrange("p (h d) -> p h d", d=HD),
                                                       ACT.Copy)
                    else:
                        ins = nc.scalar.activation(gm[:, j, 146 * (c - 3):146 * (c - 2)], ps[:, 2 * (t % 2), 0:146], ACT.Copy)
                    ins.then_inc(read_act, 1)
                if c == 0:
                    act_turned(act, 1, key_dsts(2))
                if c == 3:
                    act.wait_ge(*out_of(T_INB + 19))
                    nc.scalar.activation(gm[:, :, 0:36], gm[:, :, 0:36], ACT.Sigmoid).then_inc(gates_ready, 1)
            act_turned(act, 2, [(q_t[:, x, 0:SEQ], SEQ) for x in range(KA)] + [(q_t[:, :, SEQ:TOK], KA * SAMP)])
            act_turned(act, 3, [(qm_b[:, x, 0:SEQ], SEQ) for x in range(2)] + [(qm_b[:, :, SEQ:TOK], 2 * SAMP)])
            meet(act, 3)

        def dve_stage3(dve):
            for c in range(6):
                dve_split(dve, W_KV + c + 1)
                if c % 2 == 0:
                    dve.wait_ge(*out_of(T_KV + 5 * c + 4))
                    rope(dve, k_rows[:, {0: 0, 2: 0, 4: 1}[c], :, :], 256, NG)
            for c in range(4):
                dve_split(dve, W_INB + c + 1)
                if c == 2:
                    dve.wait_ge(*out_of(T_INB + 14))
                    rope(dve, q_rows, AW, NH)
            dve.wait_ge(heads_read, turn_base(2) + KA + 1)
            dve.wait_ge(q_bd_clear, 1)
            for g in range(NG):
                e, pr = g % 2, g // 2
                src = strided(q_t[HD * e:HD * e + HD, pr * GQ, SEQ:SEQ + 1], (DEC, NB), (TOK, GQ), (1, DEC))
                dst = strided(q_bd[HD * e:HD * e + HD, pr, 0, 12 * g:12 * g + 1], (QROWS, NB), (DEC, GQ), (1, DEC))
                nc.vector.tensor_copy(dst, src)
            meet(dve, 3)

        def pool_stage3(pool):
            nc.gpsimd.memset(q_bd[:, :, :, :], 0.0).then_inc(q_bd_clear, 1)
            names = ("cmp", "slc", "win")
            for c in range(6):
                br, kv = c // 2, c % 2
                if kv == 0:
                    pool.wait_ge(roped, br + 1)
                else:
                    pool.wait_ge(*out_of(T_KV + 5 * c + 4))
                src = v_bank[:, :, br - 1, :] if c in (3, 5) else k_rows[:, {0: 0, 1: 1, 2: 0, 4: 1}[c], :, :]
                done = kv_out[c] if c < 2 else outputs
                pool.dma_start(o[names[br] + "_p"].rearrange("(j p) v x -> v p j x", p=P)[kv], src[:, 0:4, :]).then_inc(done, 16)
                if br < 2:
                    dst = o[names[br] + "_s"][:, kv, :]
                    pool.dma_start(dst, src[0:SAMP, NQT, :]).then_inc(done, 16)
                else:
                    for b in range(NB):
                        pool.dma_start(o["win_s"][b, 512 - DEC:512, kv, :], src[DEC * b:DEC * b + DEC, NQT, :]).then_inc(outputs, 16)
            pool.wait_ge(gates_ready, 1)
            pool.dma_start(scratch, gm[0:SAMP, NQT, 0:36]).then_inc(gates_out, 16)
            pool.wait_ge(gates_out, 16)
            for b in range(NB):
                src = bass.AP(scratch.tensor, scratch.offset + DEC * 36 * b, [[3, NH], [36, DEC], [1, 3]])
                pool.dma_start(gs[:, b, :], src).then_inc(gates_in, 16)
            meet(pool, 3)

        OUT_STAGE3 = 16 * (2 * 2 + 2 * (1 + NB))

        MB = {"v": region(xalt, 0, NB, 2, 256), "k": region(xalt, 4096, 2, 2, 256), "kt": region(xalt, 5120, 2, 2, MEM),
              "q": region(xalt, 6144, 2, NB, P), "p": region(xalt, 8192, 256), "pt": region(xalt, 8448, 2, P), "qt": qm_b}
        mem_b, ub, samples_b = mem_sems("mem_b"), unit_sems("ub"), sem("samples_b")
        phi1_b = region(arena, 0, 16, 2, P)
        xc_b = region(arena, 4096, 2, 8, P)
        gel_b = region(arena, 6144, 2, P)
        cmp_p_in = sem("cmp_p_in")
        small = {}
        at = 4096
        for name, parts, dims in (("pc", QROWS, (NB, 64)), ("pct", 64, (NB, QROWS)), ("pgt", 64, (NB, QROWS)),
                                  ("imp", QROWS, (NB, 14)), ("eq", QROWS, (NB, 14)), ("bias", QROWS, (NB, 16)), ("bx", QROWS, (P,)),
                                  ("snew", QROWS, (2, NB, DEC)), ("mx", QROWS, (NB, 2, 3)), ("st", QROWS, (4, NB))):
            small[name] = region(arena, at, *dims, parts=parts)
            at += int(np.prod(dims))
        assert at <= 6400
        c_scored, c_centred, c_exp, c_normed = (sem(f"c_{x}") for x in ("scored", "centred", "exp", "normed"))
        c_turned, c_copied, c_gated, c_imp, c_imp_read, c_imp2, c_done = (
            sem(f"c_{x}") for x in ("turned", "copied", "gated", "imp", "imp_read", "imp2", "done"))
        slc_in = [sem("slc_in_0"), sem("slc_in_1"), sem("slc_in_2")]
        win_in = [sem("win_in_even"), sem("win_in_odd")]
        s_turned, s_read_a, s_read_d, s_scored, s_max, s_exp, s_normed, s_pturned, s_pt, s_summed, s_moved, s_sum_turned, s_out = (
            sem(f"s_{x}") for x in ("turned", "read_act", "read_dve", "scored", "max", "exp", "normed", "pturned", "pt",
                                    "summed", "moved", "sum_turned", "out"))
        slc_places = [xalt[:, 0:4096], xalt[:, 4096:8192], w_raw[:, :, :].rearrange("p a c -> p (a c)")]
        slc = [x.rearrange("p (s x) -> p s x", s=8) for x in slc_places]
        win = region(arena, 0, 2, 4, 512)
        kts = region(walt, 0, 2, 1024)
        ktw = region(walt, 2048, 2, 512)
        p_sel = region(walt, 3072, 1024, parts=QROWS)
        p_win = region(walt, 4096, 512, parts=QROWS)
        p_new = region(walt, 4608, 2, SAMP, parts=QROWS)
        pt_s = region(walt, 4672, 12, QROWS)
        pt_n = region(walt, 5248, 2, QROWS, parts=SAMP)
        mkv_b = region(walt, 5376, 2, 512)
        km_b = region(walt, 6400, 2, MEM)
        sums_s = region(walt, 6912, 2, 256, parts=24)
        mkv_b_in = sem("mkv_b_in")
        km_b_turned = sem("km_b_turned")
        km_b_read = sem("km_b_read")
        pr_b, pt_b = region(arena, 0, 4, 512), region(arena, 2048, 4, 512)

        def nsa_units():
            us = []
            for k in range(KA):
                pr, r = k // GQ, k % GQ
                for i in range(NQT):
                    for e in range(2):
                        half, g = slice(HD * e, HD * e + HD), 2 * pr + e
                        hd, vcols = g * GQ + r, slice(HD * g, HD * g + HD)
                        for br in range(3):
                            gate = gm[:, i, 3 * hd + br:3 * hd + br + 1]
                            u = {"q": q_t[half, k, i * P:(i + 1) * P], "p": pr_b, "pt": pt_b, "place": (e, i),
                                 "first": br == 0, "last": br == 2, "closes": k if (i, e, br) == (NQT - 1, 1, 2) else None}
                            if br == 0:
                                u.update(n=32, k=kc_p[half, pr, :], mask=cst[:, C_CMP + 32 * i:C_CMP + 32 * i + 32],
                                         gate=gate,
                                         v=lambda c, vc=vcols: vc_p[:, vc])
                            else:
                                n = P * (i + 1)
                                u.update(n=n, k=k_t[half, br - 1, pr, 0:n],
                                         mask=cst[:, C_CAUS + 512 - n:C_CAUS + 512], gate=gate,
                                         v=lambda c, vc=vcols, br=br: v_bank[:, c, br - 1, vc])
                            us.append(u)
            return us + mem_units(qm_b, km_b, mkv_b, pr_b, pt_b)

        units_b = nsa_units()
        slc_rows = w["cache_slc_kv"].rearrange("n (a s) c h d -> (n a) (s c h d)", s=8)

        def pool_stage4(pool):
            pool_mem_loads(pool, 1, MB, mem_b)
            src = o["cmp_p"].rearrange("(n s) v x -> n (s v x)", s=STRIDE)
            pool.dma_start(walt[0:32, 0:STRIDE * ROW], src).then_inc(cmp_p_in, 16)
            load_phi1(pool, phi1_b, phi1_b_in)
            pool.wait_ge(turned, 80)
            pool.dma_start(mkv_b[:, :, :], o["mem_kv"][1].rearrange("(j p) x -> p j x", p=P)).then_inc(mkv_b_in, 16)
            pool.wait_ge(blocks, 5)
            pool.wait_ge(mem_b["merged"], 1)
            for b in range(NB):
                if b >= 3:
                    pool.wait_ge(s_summed, b - 2)
                nc.gpsimd.indirect_dma_start(slc_places[b % 3], None, slc_rows,
                                             bass.IndirectOffsetOnAxis(rows_s[:, b:b + 1], 0)).then_inc(slc_in[b % 3], 16)
                if b >= 2:
                    pool.wait_ge(s_summed, b - 1)
                pool.dma_start(win[:, b % 2, :, :], w["cache_win_kv"][b].rearrange("(p s) c h d -> p s (c h d)", s=4)
                               ).then_inc(win_in[b % 2], 16)
            meet(pool, 4)
            meet(pool, 5)

        def pe_stage4(pe):
            pe_mem(pe, MB, mem_b)
            pe.wait_ge(cmp_p_in, 16)
            pe_compress_turn(pe, walt, 64, 32, 64)
            pe.wait_ge(mkv_b_in, 16)
            pe.wait_ge(mem_b["merged"], 1)
            for j in range(2):
                for tt in range(2):
                    mm = nc.tensor.transpose(ps[:, 2, tt * MEM + j * P:tt * MEM + (j + 1) * P],
                                             mkv_b[:, j, tt * P:(tt + 1) * P], ident)
            mm.then_inc(km_b_turned, 1)
            pe.wait_ge(phi1_b_in, PHI1_ONCE)
            pe_compress_hidden(pe, 4, xc_b, phi1_b, 64, 1, 32, True)
            pe_compress_out(pe, 4, gel_b, 1, 32)
            pe.wait_ge(km_b_read, 1)
            pe.wait_ge(blocks_read, 5)
            for b in range(NB):
                product(ps[0:QROWS, 0, 64 * b:64 * b + NCS], [(q_bd[:, pr, b, :], kc_s[:, b, pr, 0:NCS]) for pr in range(2)])
            for br in range(2):
                for b in range(NB):
                    c = (br * NB + b) * DEC
                    product(ps[0:QROWS, 1, c:c + DEC],
                            [(q_bd[:, pr, b, :], k_t[:, br, pr, SEQ + DEC * b:SEQ + DEC * b + DEC]) for pr in range(2)],
                            c_scored if br == 1 and b == NB - 1 else None)
            pe.wait_ge(c_normed, 1)
            for b in range(NB):
                mm = nc.tensor.transpose(ps[0:NCS, 4, QROWS * b:QROWS * b + QROWS], small["pc"][:, b, 0:NCS],
                                         ident[0:QROWS, 0:QROWS])
            mm.then_inc(c_turned, 1)
            pe.wait_ge(c_copied, 1)
            for b in range(NB):
                mm = nc.tensor.matmul(ps[0:QROWS, 2, 14 * b:14 * b + 14], small["pct"][0:NCS, b, :],
                                      cst[0:NCS, C_OV:C_OV + 14], start=True, stop=True)
            mm.then_inc(c_imp, 1)
            pe.wait_ge(c_gated, 1)
            for b in range(NB):
                mm = nc.tensor.transpose(ps[0:NCS, 5, QROWS * b:QROWS * b + QROWS], small["pc"][:, b, 0:NCS],
                                         ident[0:QROWS, 0:QROWS])
            mm.then_inc(c_turned, 1)
            pe.wait_ge(c_imp_read, 1)
            nc.tensor.matmul(ps[0:QROWS, 3, 0:14 * NB], cst[0:QROWS, C_SUMR:C_SUMR + QROWS],
                             small["imp"].rearrange("p b j -> p (b j)"), start=True, stop=True).then_inc(c_imp2, 1)
            pe.wait_ge(c_done, 1)

            def turn_keys(b):
                if b == NB:
                    return
                pe.wait_ge(slc_in[b % 3], 16 * (b // 3 + 1))
                pe.wait_ge(win_in[b % 2], 16 * (b // 2 + 1))
                for x in range(6):
                    n = s_group(b, x)
                    bank_wait(n)
                    for s in range(4):
                        src = slc[b % 3][:, 4 * (x % 2) + s, :] if x < 4 else win[:, b % 2, s, :]
                        pr = x // 2 if x < 4 else x - 4
                        mm = nc.tensor.transpose(ps[:, 4 + n % 3, s * P:(s + 1) * P], src[:, pr * P:(pr + 1) * P], ident)
                    mm.then_inc(s_turned, 1)

            def bank_wait(n):
                if n >= 3:
                    reader, v = s_reader(n - 3)
                    pe.wait_ge(s_read_a if reader == "act" else s_read_d, v)

            def score(b):
                if b >= 1:
                    pe.wait_ge(s_exp, b)
                pe.wait_ge(s_read_a, s_group(b, 4) // 2 + 1)
                pe.wait_ge(s_read_d, s_group(b, 5) // 2 + 1)
                for x in range(2):
                    product(ps[0:QROWS, x, :], [(q_bd[:, pr, b, :], kts[:, pr, 512 * x:512 * x + 512]) for pr in range(2)])
                product(ps[0:QROWS, 2, :], [(q_bd[:, pr, b, :], ktw[:, pr, :]) for pr in range(2)], s_scored)

            def turn_probs(b):
                pe.wait_ge(s_normed, b + 1)
                n = s_group(b, 6)
                bank_wait(n)
                for s in range(8):
                    mm = nc.tensor.transpose(ps[:, 4 + n % 3, QROWS * s:QROWS * s + QROWS],
                                             p_sel[:, s * P:(s + 1) * P], ident[0:QROWS, 0:QROWS])
                mm.then_inc(s_turned, 1)
                bank_wait(n + 1)
                for s in range(4):
                    nc.tensor.transpose(ps[:, 4 + (n + 1) % 3, QROWS * s:QROWS * s + QROWS], p_win[:, s * P:(s + 1) * P],
                                        ident[0:QROWS, 0:QROWS])
                for br in range(2):
                    mm = nc.tensor.transpose(ps[0:SAMP, 4 + (n + 1) % 3, QROWS * (4 + br):QROWS * (5 + br)],
                                             p_new[:, br, :], ident[0:QROWS, 0:QROWS])
                mm.then_inc(s_turned, 1)

            def values(b):
                pe.wait_ge(s_read_a, s_group(b, 6) // 2 + 1)
                pe.wait_ge(s_read_d, s_group(b, 7) // 2 + 1)
                for pr in range(2):
                    c, vc = 24 * pr, slice(256 + P * pr, 256 + P * pr + P)
                    terms = [(pt_s[:, s, c:c + 24], slc[b % 3][:, s, vc]) for s in range(8)]
                    terms += [(pt_s[:, 8 + s, c:c + 24], win[:, b % 2, s, vc]) for s in range(4)]
                    terms += [(small["pgt"][0:NCS, b, c:c + 24], vc_s[0:NCS, b, P * pr:P * pr + P])]
                    terms += [(pt_n[:, br, c:c + 24], v_bank[0:SAMP, NQT, br, P * pr:P * pr + P]) for br in range(2)]
                    at = 256 * (b % 2) + P * pr
                    product(ps[0:24, 7, at:at + P], terms, s_summed if pr else None)

            def turn_sums(b):
                pe.wait_ge(s_moved, b + 1)
                for pr in range(2):
                    c = QROWS * b + 24 * pr
                    mm = nc.tensor.transpose(ps[:, 3, c:c + 24], sums_s[:, b % 2, P * pr:P * pr + P], ident[0:24, 0:24])
                mm.then_inc(s_sum_turned, 1)

            turn_keys(0)
            for b in range(NB):
                score(b)
                if b >= 1:
                    turn_sums(b - 1)
                turn_keys(b + 1)
                turn_probs(b)
                values(b)
            turn_sums(NB - 1)
            pe.wait_ge(s_out, 1)
            meet(pe, 4)
            pe_units(pe, units_b, ub)
            meet(pe, 5)

        def s_group(b, x):
            if x < 6:
                return max(8 * b - 2, 0) + x
            return 8 * b + x + (6 if b < NB - 1 else 0)

        def s_reader(n):
            return ("act", n // 2 + 1) if n % 2 == 0 else ("dve", n // 2 + 1)

        def s_copy(eng, who, b, xs):
            for x in xs:
                if b == NB:
                    return
                n = s_group(b, x)
                if s_reader(n)[0] != who:
                    continue
                eng.wait_ge(s_turned, n + 1)
                bank = ps[:, 4 + n % 3, :]
                if x < 4:
                    moves = [(kts[:, x // 2, 512 * (x % 2):512 * (x % 2) + 512], bank)]
                elif x < 6:
                    moves = [(ktw[:, x - 4, :], bank)]
                elif x == 6:
                    moves = [(pt_s[:, 0:8, :], bank[:, 0:8 * QROWS].rearrange("p (s m) -> p s m", m=QROWS))]
                else:
                    moves = [(pt_s[:, 8:12, :], bank[:, 0:4 * QROWS].rearrange("p (s m) -> p s m", m=QROWS)),
                             (pt_n[:, :, :], bank[0:SAMP, 4 * QROWS:6 * QROWS].rearrange("p (s m) -> p s m", m=QROWS))]
                for dst, src in moves:
                    ins = nc.scalar.activation(dst, src, ACT.Copy) if who == "act" else nc.vector.tensor_copy(dst, src)
                ins.then_inc(s_read_a if who == "act" else s_read_d, 1)

        def act_stage4(act):
            act_mem(act, MB, mem_b)
            compress_copy(act, "act", xc_b, 64, 32, None)
            act_compress_gelu(act, 4, gel_b, P)
            act.wait_ge(c_centred, 1)
            nc.scalar.activation(small["pc"][:, :, 0:NCS], small["pc"][:, :, 0:NCS], ACT.Exp, scale=SCALE).then_inc(c_exp, 1)
            def move_sums(b):
                act.wait_ge(s_summed, b + 1)
                if b >= 2:
                    act.wait_ge(s_sum_turned, b - 1)
                nc.scalar.activation(sums_s[:, b % 2, :], ps[0:24, 7, 256 * (b % 2):256 * (b % 2) + 256],
                                     ACT.Copy).then_inc(s_moved, 1)

            s_copy(act, "act", 0, range(6))
            for b in range(NB):
                if b >= 1:
                    move_sums(b - 1)
                act.wait_ge(s_scored, b + 1)
                s_copy(act, "act", b + 1, range(3))
                act.wait_ge(s_max, b + 1)
                nm, sm = stat[0:QROWS, 38:40], stat[0:QROWS, 40:44]
                nc.scalar.activation(p_sel.rearrange("p (a x) -> p a x", a=2), ps[0:QROWS, 0:2, :], ACT.Exp, bias=nm[:, 0:1],
                                     scale=SCALE, accum_out=sm[:, 0:1])
                nc.scalar.activation(p_win, ps[0:QROWS, 2, :], ACT.Exp, bias=nm[:, 1:2], scale=SCALE, accum_out=sm[:, 1:2])
                for br in range(2):
                    ins = nc.scalar.activation(small["snew"][:, br, b, :], small["snew"][:, br, b, :], ACT.Exp,
                                               bias=nm[:, br:br + 1], scale=SCALE, accum_out=sm[:, 2 + br:3 + br])
                ins.then_inc(s_exp, 1)
                s_copy(act, "act", b + 1, range(3, 6))
                s_copy(act, "act", b, range(6, 8))
            move_sums(NB - 1)
            meet(act, 4)
            act_units(act, units_b, ub)
            act_samples(act, 0, samples_b)
            meet(act, 5)
            act_split(act, W_OUTB)

        def bcast(ap, n):
            return strided(ap[:, 0:1], (ap.ap[1][0], NB), (0, n))

        def dve_stage4(dve):
            def chained(ins):
                c = dve_chain(ins)
                dve.wait_ge(dve_step, c)

            dve_mem(dve, MB, mem_b)
            compress_copy(dve, "dve", xc_b, 64, 32, None)
            dve.wait_ge(km_b_turned, 1)
            nc.vector.tensor_copy(km_b[:, :, :], ps[:, 2, :].rearrange("p (t m) -> p t m", t=2)).then_inc(km_b_read, 1)
            dve.wait_ge(blocks, 5)
            nc.vector.tensor_copy(kc_p[:, :, :], ps[:, 0, 0:64].rearrange("p (g n) -> p g n", g=2))
            nc.vector.tensor_copy(vc_p[:, :], ps[0:32, 1, 0:256]).then_inc(blocks_read, 1)
            dve.wait_ge(c_scored, 1)
            st, pc, mx, imp, eq = (small[k] for k in ("st", "pc", "mx", "imp", "eq"))
            live = pc[:, :, 0:NCS]
            sc = ps[0:QROWS, 0, :].rearrange("p (b n) -> p b n", b=NB)[:, :, 0:NCS]
            chained(nc.vector.tensor_reduce(st[:, 0, :], sc, AX, ALU.max))
            nc.vector.tensor_tensor(live, sc, bcast(st[:, 0, :], NCS), ALU.subtract).then_inc(c_centred, 1)
            snew = small["snew"].rearrange("p r b t -> p (r b) t")
            chained(nc.vector.tensor_tensor(snew, ps[0:QROWS, 1, 0:64].rearrange("p (a t) -> p a t", t=DEC),
                                            strided(cst[0:QROWS, C_NEW + 28:C_NEW + 29], (0, 2 * NB), (1, DEC)), ALU.add))
            chained(nc.vector.tensor_reduce(mx[:, :, 0, 2], small["snew"][:, 0, :, :], AX, ALU.max))
            chained(nc.vector.tensor_reduce(mx[:, :, 1, 2], small["snew"][:, 1, :, :], AX, ALU.max))
            nc.vector.tensor_copy(mx[:, :, 1, 1], mx[:, :, 1, 2])
            nc.vector.memset(small["bias"], 0.0)
            nc.vector.memset(p_new, 0.0)
            dve.wait_ge(c_exp, 1)
            chained(nc.vector.tensor_reduce(st[:, 1, :], live, AX, ALU.add))
            chained(nc.vector.reciprocal(st[:, 2, :], st[:, 1, :]))
            nc.vector.tensor_tensor(live, live, bcast(st[:, 2, :], NCS), ALU.mult).then_inc(c_normed, 1)
            dve.wait_ge(c_turned, 1)
            nc.vector.tensor_copy(small["pct"][0:NCS, :, :], ps[0:NCS, 4, 0:NB * QROWS].rearrange("p (b m) -> p b m", b=NB)
                                  ).then_inc(c_copied, 1)
            dve.wait_ge(gates_in, 16 * NB)
            nc.vector.tensor_tensor(live, live, bcast(gs[:, :, 0], NCS), ALU.mult).then_inc(c_gated, 1)
            dve.wait_ge(c_imp, 1)
            nc.vector.tensor_copy(imp, ps[0:QROWS, 2, 0:14 * NB].rearrange("p (b j) -> p b j", b=NB)).then_inc(c_imp_read, 1)
            dve.wait_ge(c_imp2, 1)
            imp2 = ps[0:QROWS, 3, 0:14 * NB].rearrange("p (b j) -> p b j", b=NB)
            j3 = strided(cst[0:QROWS, C_J:C_J + 1], (0, NB), (1, 14))
            chained(nc.vector.tensor_reduce(st[:, 3, :], imp2, AX, ALU.min))
            chained(nc.vector.tensor_tensor(eq, imp2, bcast(st[:, 3, :], 14), ALU.is_equal))
            chained(nc.vector.tensor_tensor(eq, eq, j3, ALU.mult))
            chained(nc.vector.tensor_reduce(st[:, 0, :], eq, AX, ALU.max))
            chained(nc.vector.tensor_tensor(eq, j3, bcast(st[:, 0, :], 14), ALU.is_equal))
            chained(nc.vector.tensor_scalar(small["bias"][:, :, 1:15], eq, NEG, None, ALU.mult))
            dve.wait_ge(c_turned, 2)
            nc.vector.tensor_copy(small["pgt"][0:NCS, :, :], ps[0:NCS, 5, 0:NB * QROWS].rearrange("p (b m) -> p b m", b=NB)
                                  ).then_inc(c_done, 1)
            s_copy(dve, "dve", 0, range(6))
            for b in range(NB):
                dve.wait_ge(s_scored, b + 1)
                bx = small["bx"]
                chained(nc.vector.tensor_copy(bx.rearrange("p (j i) -> p j i", j=16),
                                              strided(small["bias"][:, b, 0:1], (1, 16), (0, 8))))
                for x in range(2):
                    sc = ps[0:QROWS, x, :].rearrange("p (s i) -> p s i", s=4)
                    nc.vector.tensor_tensor_reduce(sc, sc, strided(bx[:, 0:1], (0, 4), (1, P)), 1.0,
                                                   3 * NEG, ALU.add, ALU.max, mx[:, b, 0, x:x + 1])
                edge = strided(ps[0:QROWS, 2, 0:1], (P, 4))
                chained(nc.vector.tensor_tensor(edge, edge, cst[0:QROWS, C_WIN:C_WIN + 4], ALU.add))
                chained(nc.vector.reduce_max(mx[:, b, 1, 0:1], ps[0:QROWS, 2, :], AX))
                chained(nc.vector.tensor_reduce(stat[0:QROWS, 36:38], mx[:, b, :, :], AX, ALU.max))
                nc.vector.tensor_scalar(stat[0:QROWS, 38:40], stat[0:QROWS, 36:38], -SCALE, None, ALU.mult).then_inc(s_max, 1)
                s_copy(dve, "dve", b + 1, range(4))
                dve.wait_ge(s_exp, b + 1)
                chained(nc.vector.tensor_tensor(stat[0:QROWS, 44:46], stat[0:QROWS, 40:42], stat[0:QROWS, 42:44], ALU.add))
                chained(nc.vector.reciprocal(stat[0:QROWS, 46:48], stat[0:QROWS, 44:46]))
                chained(nc.vector.tensor_tensor(stat[0:QROWS, 48:50], stat[0:QROWS, 46:48], gs[:, b, 1:3], ALU.mult))
                if b >= 1:
                    chained(nc.vector.memset(p_new[:, :, DEC * (b - 1):DEC * b], 0.0))
                for br in range(2):
                    nc.vector.tensor_scalar(p_new[:, br, DEC * b:DEC * b + DEC], small["snew"][:, br, b, :],
                                            stat[0:QROWS, 48 + br:49 + br], None, ALU.mult)
                nc.vector.tensor_scalar(p_win, p_win, stat[0:QROWS, 49:50], None, ALU.mult)
                nc.vector.tensor_scalar(p_sel, p_sel, stat[0:QROWS, 48:49], None, ALU.mult).then_inc(s_normed, 1)
                s_copy(dve, "dve", b + 1, range(4, 6))
                s_copy(dve, "dve", b, range(6, 8))
            dve.wait_ge(s_sum_turned, NB)
            for g in range(NG):
                e, pr = g % 2, g // 2
                src = strided(ps[HD * e:HD * e + HD, 3, 24 * pr + 12 * e:24 * pr + 12 * e + 1], (QROWS, NB), (DEC, GQ), (1, DEC))
                dst = strided(o_s[HD * e:HD * e + HD, pr * GQ, 0:1], (DEC, NB), (SAMP, GQ), (1, DEC))
                ins = nc.vector.tensor_copy(dst, src)
            ins.then_inc(s_out, 1)
            meet(dve, 4)
            first = strided(gm[:, 0, 0:1], (3, NH))
            chained(nc.vector.tensor_tensor(first, first, strided(cst[:, C_VAL:C_VAL + 1], (0, NH)), ALU.mult))
            dve_units(dve, units_b, ub)
            dve_samples(dve, 0, samples_b)
            meet(dve, 5)
            dve_split(dve, W_OUTB)

        y_turned = sem("y_turned")
        y_read = sem("y_read")
        y_rows = region(arena, 0, 5, D)

        def pe_stage5(pe):
            pe.wait_ge(ln_lo, 32)
            for n in range(10):
                j, m = n // 2, P if n < 8 else SAMP
                if n >= 4:
                    pe.wait_ge(y_read, n - 3)
                for k in range(4):
                    mm = nc.tensor.transpose(ps[0:m, 4 + n % 4, k * P:(k + 1) * P],
                                             resid[:, 4 * (n % 2) + k, j * P:j * P + m], ident)
                mm.then_inc(y_turned, 1)

        def dve_stage5(dve):
            for n in range(10):
                m = P if n < 8 else SAMP
                dve.wait_ge(y_turned, n + 1)
                nc.vector.tensor_copy(y_rows[0:m, n // 2, 512 * (n % 2):512 * (n % 2) + 512], ps[0:m, 4 + n % 4, :]).then_inc(y_read, 1)

        def sp_stage5(sp):
            for j in range(NQT):
                sp.wait_ge(y_read, 2 * j + 2)
                sp.dma_start(o["y_p"][j * P:(j + 1) * P, :], y_rows[:, j, :]).then_inc(outputs_sp, 16)
            sp.wait_ge(y_read, 10)
            sp.dma_start(o["y_s"], y_rows[0:SAMP, NQT, :]).then_inc(outputs_sp, 16)
            sp.wait_ge(outputs, 32 + OUT_STAGE3)
            sp.wait_ge(outputs_sp, 16 * (NB + NQT + 1))
            sp.wait_ge(v_out, 16)
            for s in kv_out:
                sp.wait_ge(s, 32)

        block = ctx.enter_context(nc.Block())

        @block.sync
        def _(sp):
            sp_stage0(sp)
            sp_slots(sp, 0, 13)
            sp_stage2(sp)
            for b in range(NB):
                sp.dma_start(o["win_s"][b, 0:512 - DEC, :, :].rearrange("t v x -> t (v x)"),
                             w["cache_win_kv"][b, DEC:512].rearrange("t c h d -> t (c h d)")).then_inc(outputs_sp, 16)
            sp_slots(sp, 13, 2)
            sp_mlp(sp, 0)
            sp_slots(sp, W_KV, 11)
            sp.wait_ge(s_summed, 6)
            sp_slots(sp, W_OUTB, 4)
            sp_mlp(sp, 1)
            sp_stage5(sp)

        @block.gpsimd
        def _(pool):
            pool_stage0(pool)
            pool_stage1(pool)
            pool_stage2(pool)
            pool_out(pool, 0)
            pool_mlp(pool, 0)
            pool_stage3(pool)
            pool_stage4(pool)
            pool_out(pool, 1)
            pool_mlp(pool, 1)

        @block.tensor
        def _(pe):
            pe_stage0(pe)
            pe_stage1(pe)
            pe_stage2(pe)
            pe_out(pe, 0)
            pe_mlp(pe, 0)
            pe_ln(pe, 2)
            pe_stage3(pe)
            pe_stage4(pe)
            pe_out(pe, 1)
            pe_mlp(pe, 1)
            pe_ln(pe, 4)
            pe_stage5(pe)

        @block.scalar
        def _(act):
            act_stage0(act)
            act_stage1(act)
            act_stage2(act)
            act_out(act, 0)
            act_mlp(act, 0)
            ln_resid("act", act, 16)
            act_stage3(act)
            act_stage4(act)
            act_out(act, 1)
            act_mlp(act, 1)
            ln_resid("act", act, 48)

        @block.vector
        def _(dve):
            dve_stage0(dve)
            dve_stage1(dve)
            dve_stage2(dve)
            dve_out(dve, 0)
            dve_mlp(dve, 0)
            ln_resid("dve", dve, 16)
            dve_stage3(dve)
            dve_stage4(dve)
            dve_out(dve, 1)
            dve_mlp(dve, 1)
            ln_resid("dve", dve, 48)
            dve_stage5(dve)


INPUTS = ["x_prompt", "x_sample", "cache_cmp_kv", "cache_slc_kv", "cache_win_kv", "cache_mem_kv", "page_table", "mem_prompt",
          "w_in_a", "ln_v_g", "ln_v_b", "w_spatial", "b_spatial", "w_out_a", "w_in_b", "w_out_b", "w_kv_shared", "cmp_pe",
          "w_phi1", "w_phi2", "w_mem_kv", "ln1_g", "ln1_b", "ln2_g", "ln2_b", "w_up", "w_down"]
OUTPUTS = [("y_p", (1, SEQ, D)), ("y_s", (NB, DEC, D)), ("cmp_p", (1, SEQ, 2, NG, HD)), ("slc_p", (1, SEQ, 2, NG, HD)),
           ("win_p", (1, SEQ, 2, NG, HD)), ("mem_kv", (2, 1, MEM, 2, 4, 64)), ("cmp_s", (NB, DEC, 2, NG, HD)),
           ("slc_s", (NB, DEC, 2, NG, HD)), ("win_s", (NB, 512, 2, NG, HD)), ("gmlp_v", (1, NB, DEC, AW))]


def kernel(**inputs):
    import concourse.bacc as bacc
    from concourse.bass_utils import run_bass_kernel_spmd

    nc = bacc.Bacc("TRN2", target_bir_lowering=False, num_devices=1)
    arrays = {f"in_{n}": np.ascontiguousarray(inputs[n]) for n in INPUTS}
    arrays["in_consts"] = shape_constants()
    w = {n[3:]: nc.dram_tensor(n, a.shape, mybir.dt.from_np(a.dtype), kind="ExternalInput").ap() for n, a in arrays.items()}
    w["b_spatial"] = w["b_spatial"][0]
    o = {n: nc.dram_tensor(f"out_{n}", s, F32, kind="ExternalOutput").ap() for n, s in OUTPUTS}
    o["y_p"] = o["y_p"][0]
    o["y_s"] = o["y_s"].rearrange("b t d -> (b t) d")
    for n in ("cmp_p", "slc_p", "win_p"):
        o[n] = o[n][0].rearrange("t v h d -> t v (h d)")
    for n in ("cmp_s", "slc_s"):
        o[n] = o[n].rearrange("b t v h d -> (b t) v (h d)")
    o["win_s"] = o["win_s"].rearrange("b t v h d -> b t v (h d)")
    o["mem_kv"] = o["mem_kv"].rearrange("l a m v h d -> (l a) m (v h d)")
    scratch = nc.dram_tensor("gate_scratch", (SAMP, 36), F32, kind="Internal").ap()
    build(nc, w, o, scratch)
    out = run_bass_kernel_spmd(nc, [arrays], core_ids=[0]).results[0]
    return tuple(out[f"out_{n}"] for n, _ in OUTPUTS)
```

```python
from contextlib import ExitStack

import numpy as np

import concourse.bass as bass
from concourse import mybir

F32 = mybir.dt.float32
F32R = mybir.dt.float32r
I32 = mybir.dt.int32
ACT = mybir.ActivationFunctionType
ALU = mybir.AluOpType
AX = mybir.AxisListType.X

P = 128
D = 1024
KD = D // P
SEQ, NB, DEC = 512, 8, 4
SAMP = NB * DEC
TOK = SEQ + SAMP
HALF = TOK // 2
NQT = SEQ // P
NT = NQT + 1
AW = 768
KA = AW // P
HD = 64
NH, NG, GQ = 12, 4, 3
FF = 4096
MEM = 256
PAST, PAGE = 1024, 128
STRIDE = 16
NSTR = PAST // STRIDE
NCS = NSTR - 1
NCP = SEQ // STRIDE - 1
ROW = 2 * NG * HD
EPS = 1e-5
ALPHA = 4.0 ** 0.25
SCALE = HD ** -0.5
NEG = -1e30
QROWS = NG * GQ * DEC

C_ID, C_ONE, C_CAUS, C_CMP, C_VAL = 0, 128, 256, 768, 896
C_COS, C_SIN, C_NEW, C_WIN = 897, 937, 977, 1037
C_OV, C_SUMR, C_J, C_BD, C_REP, C_K8, C_K16, C_EPS, C_MIX = 1041, 1055, 1103, 1117, 1125, 1157, 1158, 1159, 1160
NCONST = 1160

SLOT = 2048


def shape_constants():
    c = np.zeros((P, NCONST), np.float32)
    p = np.arange(P)
    c[:, C_ID:C_ID + P] = np.eye(P)
    c[:, C_ONE:C_ONE + P] = 1.0
    c[:, C_CAUS + 384:C_CAUS + 512] = np.where(p[None, :] <= p[:, None], 0.0, NEG)
    for i in range(NQT):
        n = np.arange(32)
        seen = (STRIDE * n[None, :] + 31 <= (P * i + p)[:, None]) & (n[None, :] < NCP)
        c[:, C_CMP + 32 * i:C_CMP + 32 * i + 32] = np.where(seen, 0.0, NEG)
    c[:, C_VAL] = (p >= 31)
    inv = (500000.0 ** (-np.arange(8, dtype=np.float32) / 8)).astype(np.float32)
    for j in range(NQT + 1):
        pos = (P * j + p if j < NQT else PAST + p % DEC).astype(np.float32)
        ang = pos[:, None] * inv[None, :]
        c[:, C_COS + 8 * j:C_COS + 8 * j + 8] = np.cos(ang)
        c[:, C_SIN + 8 * j:C_SIN + 8 * j + 8] = np.sin(ang)
    t = p % DEC
    for a in range(60):
        c[:, C_NEW + a] = np.where((a >= 28) & (a < 32) & (a - 28 <= t), 0.0, NEG)
    for s in range(4):
        c[:, C_WIN + s] = np.where(s >= t + 1, 0.0, NEG)
    for j in range(1, 15):
        c[:NCS, C_OV + j - 1] = (STRIDE * p[:NCS] < 64 * j + 64) & (STRIDE * p[:NCS] + 32 > 64 * j)
        c[:, C_J + j - 1] = j
    r = np.arange(QROWS)
    c[:QROWS, C_SUMR:C_SUMR + QROWS] = (r[:, None] // 12 == r[None, :] // 12) & (r[:, None] % 4 == r[None, :] % 4)
    c[:, C_BD:C_BD + 8] = p[:, None] // 4 == np.arange(8)[None, :]
    c[:DEC, C_REP:C_REP + 32] = p[:DEC, None] == np.arange(32)[None, :] % 4
    c[:, C_K8] = p % 8
    c[:, C_K16] = p % 16
    c[:, C_EPS] = EPS
    return c


def weight_slots(w):
    def cols(m, c0, n):
        return [(slice(0, P), slice(0, KD), m.rearrange("(k p) n -> p k n", p=P)[:, :, c0:c0 + n])]

    def merged(m, c0):
        m3 = m.rearrange("(h d) n -> d h n", d=HD)
        loads = [(slice(HD * e, HD * e + HD), slice(GQ * q, GQ * q + GQ),
                  m3[:, 6 * q + GQ * e:6 * q + GQ * e + GQ, c0:c0 + 256]) for q in range(2) for e in range(2)]
        return loads + [(slice(0, P), slice(KA, KD), m[AW:D, :].rearrange("(k p) n -> p k n", p=P)[:, :, c0:c0 + 256])]

    def down(m, half, tile):
        rows = m[half * FF // 2:(half + 1) * FF // 2, tile * P:(tile + 1) * P]
        return [(slice(0, P), slice(0, 16), rows.rearrange("(k p) n -> p k n", p=P))]

    slots = [cols(w["w_mem_kv"][l], 256 * c, 256) for l in range(2) for c in range(2)]
    slots += [cols(w["w_in_a"][0], 256 * c, 256) for c in range(7)]
    slots += [cols(w["w_out_a"][0], 256 * c, 256) for c in range(4)]
    mlp = [[], []]
    for l in range(2):
        for h in range(2):
            mlp[l] += [cols(w["w_up"][l], h * FF // 2 + 256 * c, 256) for c in range(8)]
            mlp[l] += [down(w["w_down"][l], h, m) for m in range(8)]
    slots += mlp[0]
    slots += [cols(w["w_kv_shared"], 256 * c, 256) for c in range(6)]
    slots += [cols(w["w_in_b"][0], c0, n) for c0, n in IN_B]
    slots += [merged(w["w_out_b"][0], 256 * c) for c in range(4)]
    slots += mlp[1]
    return slots


IN_B = [(0, 256), (256, 256), (512, 256), (768, 146), (914, 146)]
W_MEM, W_INA, W_OUTA, W_MLP0, W_KV, W_INB, W_OUTB, W_MLP1 = 0, 4, 11, 15, 47, 53, 58, 62
N_SLOTS = 94
T_MEM, T_INA, T_OUTA, T_MLP0 = 0, 8, 22, 30
T_KV = T_MLP0 + 2 * (16 + 8)
T_INB = T_KV + 30
T_OUTB = T_INB + 25
T_MLP1 = T_OUTB + 8


def build(nc, w, o, scratch):
    with ExitStack() as ctx:
        base = [(nc.sbuf_base + 31) // 32 * 32]

        def sb(name, shape, dt=F32, at=None):
            size = int(np.prod(shape[1:])) * 4
            if at is None:
                at = base[0]
                base[0] += (size + 31) // 32 * 32
            addr[name] = at
            return nc.alloc_sbuf_tensor_at(name, shape, dt, offset=at)

        addr = {}

        def sem(name):
            return ctx.enter_context(nc.semaphore(name))

        ps = ctx.enter_context(nc.psum_tensor("ps", [P, 8, 512], F32))

        cst = sb("cst", [P, NCONST])
        resid = sb("resid", [P, KD, TOK])
        XPAD = KD * TOK + 96
        x_hi = sb("x_hi", [P, XPAD], F32R)
        x_lo = sb("x_lo", [P, XPAD], F32R)
        w_raw = sb("w_raw", [P, 2, SLOT])
        w_hi = sb("w_hi", [P, 2, SLOT], F32R)
        w_lo = sb("w_lo", [P, 2, SLOT], F32R)
        arena = sb("arena", [P, 2 * 16 * TOK])
        h_hi = sb("h_hi", [P, 16, TOK], F32R, at=addr["arena"])
        h_lo = sb("h_lo", [P, 16, TOK], F32R, at=addr["arena"] + 16 * TOK * 4)
        xalt = sb("xalt", [P, 2 * KD * TOK], F32, at=addr["x_hi"])
        walt = sb("walt", [P, 4 * SLOT], F32, at=addr["w_hi"])
        sum1 = sb("sum1", [P, TOK])
        sum2 = sb("sum2", [P, TOK])
        sq = sb("sq", [P, 2, TOK])
        mean = sb("mean", [P, TOK])
        rstd = sb("rstd", [P, TOK])
        tmp = sb("tmp", [P, 2, TOK])
        lnp = sb("lnp", [P, 76])
        kc_s = sb("kc_s", [P, NB, 2, NSTR])
        vc_s = sb("vc_s", [NSTR, NB, NG * HD])
        pe_bias = sb("pe_bias", [P, 2])
        phi2 = sb("phi2", [P, 2, HD])
        kc_p = sb("kc_p", [P, 2, 32])
        vc_p = sb("vc_p", [32, NG * HD])
        pages_c = sb("pages_c", [P, 4], I32)
        rows_c = sb("rows_c", [P, 4], I32)
        pages_s = sb("pages_s", [P, NB], I32)
        rows_s = sb("rows_s", [P, NB], I32)
        q_bd = sb("q_bd", [P, 2, NB, QROWS])
        o_s = sb("o_s", [P, KD, SAMP])
        stat = sb("stat", [P, 64])
        assert base[0] <= nc.sbuf_usable_end, base[0]

        def x_tile(t, k):
            return t[:, k * TOK:(k + 1) * TOK]

        def x3(t):
            return t[:, 0:KD * TOK].rearrange("p (k t) -> p k t", k=KD)

        ident = cst[:, C_ID:C_ID + P]
        ones = cst[:, C_ONE:C_ONE + P]

        def region(t, at, *shape, parts=P):
            n = int(np.prod(shape))
            v = t[0:parts, at:at + n]
            names = "abcd"[:len(shape)]
            if len(shape) == 1:
                return v
            return v.rearrange(f"p ({' '.join(names)}) -> p {' '.join(names)}",
                               **{x: s for x, s in zip(names[:-1], shape[:-1])})

        stage_end = sem("stage_end")
        consts_in = sem("consts_in")
        raw_in = [sem("raw_in_even"), sem("raw_in_odd")]
        hi_ready = sem("hi_ready")
        split_ready = sem("split_ready")
        tile_done = sem("tile_done")
        read_act = sem("read_act")
        read_dve = sem("read_dve")
        outputs = sem("outputs")
        outputs_sp = sem("outputs_sp")
        dve_step = sem("dve_step")
        steps = {"dve": 0}

        def dve_chain(ins):
            steps["dve"] += 1
            ins.then_inc(dve_step, 1)
            return steps["dve"]

        def meet(eng, stage):
            eng.drain().then_inc(stage_end, 1)
            eng.wait_ge(stage_end, 4 * (stage + 1))

        def tiles_through(s):
            return sum(tiles_of[:s + 1])

        slots = weight_slots(w)
        assert len(slots) == N_SLOTS
        loads_of = [len(s) for s in slots]
        mlp_tiles = ([2] * 8 + [1] * 8) * 2
        tiles_of = [2] * 15 + mlp_tiles + [5] * 11 + [2] * 4 + mlp_tiles

        def loaded(s):
            return 16 * sum(loads_of[i] for i in range(s % 2, s + 1, 2))

        dve_reads = [T_OUTA <= t < T_MLP0 or T_OUTB <= t < T_MLP1
                     or any(0 <= t - t0 < 48 and (t - t0) % 24 >= 16 for t0 in (T_MLP0, T_MLP1))
                     for t in range(T_MLP1 + 48)]

        def out_of(t):
            n = sum(x == dve_reads[t] for x in dve_reads[:t + 1])
            return (read_dve if dve_reads[t] else read_act), n

        def load_slot(sp, s, lots):
            for parts, ks, src in lots:
                n = src.shape[-1]
                dst = w_raw[parts, s % 2, 0:slot_k(s) * n].rearrange("p (k c) -> p k c", c=n)
                sp.dma_start(dst[:, ks, :], src).then_inc(raw_in[s % 2], 16)

        def slot_k(s):
            return max(ks.stop for _, ks, _ in slots[s])

        def slot_n(s):
            return slot_k(s) * slots[s][0][2].shape[-1]

        def split_hi(act, par, loaded_at, tiles_at, n):
            act.wait_ge(raw_in[par], loaded_at)
            if tiles_at is not None:
                act.wait_ge(tile_done, tiles_at)
            nc.scalar.activation(w_hi[:, par, 0:n], w_raw[:, par, 0:n], ACT.Copy).then_inc(hi_ready, 1)

        def split_lo(dve, s1, par, n):
            dve.wait_ge(hi_ready, s1)
            nc.vector.tensor_tensor(w_lo[:, par, 0:n], w_raw[:, par, 0:n], w_hi[:, par, 0:n].bitcast(F32),
                                    ALU.subtract).then_inc(split_ready, 1)

        def act_split(act, s):
            if s < N_SLOTS:
                split_hi(act, s % 2, loaded(s), tiles_through(s - 2) if s >= 2 else None, slot_n(s))

        def dve_split(dve, s):
            if s < N_SLOTS:
                split_lo(dve, s + 1, s % 2, slot_n(s))

        def product(out, terms, inc=None):
            for n, (lhsT, rhs) in enumerate(terms):
                mm = nc.tensor.matmul(out, lhsT, rhs, start=n == 0, stop=n == len(terms) - 1)
            if inc is not None:
                mm.then_inc(inc, 1)

        def split_terms(a_hi, a_lo, b_hi, b_lo):
            return [(a_hi, b_hi), (a_hi, b_lo), (a_lo, b_hi)]

        def feature_tile(pe, par, bank, c0, nk, width, src_hi, src_lo, late=None):
            wv_hi = w_hi[:, par, 0:nk * width].rearrange("p (k c) -> p k c", c=width)
            wv_lo = w_lo[:, par, 0:nk * width].rearrange("p (k c) -> p k c", c=width)
            for half in range(2):
                cols = slice(half * HALF, (half + 1) * HALF)
                for k in range(nk):
                    if late is not None and half == 0 and k == late[0]:
                        pe.wait_ge(h_lo_ready, late[1])
                    terms = split_terms(wv_hi[:, k, c0:c0 + P], wv_lo[:, k, c0:c0 + P],
                                        src_hi(k)[:, cols], src_lo(k)[:, cols])
                    for x, (lhsT, rhs) in enumerate(terms):
                        mm = nc.tensor.matmul(ps[:, bank + half, 0:HALF], lhsT, rhs, start=k == 0 and x == 0,
                                              stop=k == nk - 1 and x == 2)
            mm.then_inc(tile_done, 1)

        def xk(t):
            return lambda k: x_tile(t, k)

        def pair(t):
            return ps[:, 2 * (t % 2):2 * (t % 2) + 2, 0:HALF]

        def halves(ap):
            return ap.rearrange("p (h t) -> p h t", h=2)

        def pe_feature_slots(pe, s0, n_slots, t0):
            for s in range(s0, s0 + n_slots):
                pe.wait_ge(split_ready, s + 1)
                for n in range(2):
                    t = t0 + 2 * (s - s0) + n
                    if t >= 2:
                        pe.wait_ge(*out_of(t - 2))
                    feature_tile(pe, s % 2, 2 * (t % 2), P * n, KD, 256, xk(x_hi), xk(x_lo))

        def pe_token_slot(pe, s, t0, n_tok_tiles, a_hi, a_lo, width, ln_at=None):
            pe.wait_ge(split_ready, s + 1)
            wv_hi = w_hi[:, s % 2, 0:KD * width].rearrange("p (k c) -> p k c", c=width)
            wv_lo = w_lo[:, s % 2, 0:KD * width].rearrange("p (k c) -> p k c", c=width)
            if ln_at is not None:
                pe.wait_ge(*out_of(t0 - 1))
                for k in range(KD):
                    pe.wait_ge(ln_lo, ln_at + k + 1)
                    for j in range(2):
                        terms = split_terms(a_hi(k, j), a_lo(k, j), wv_hi[:, k, :], wv_lo[:, k, :])
                        for x, (lhsT, rhs) in enumerate(terms):
                            mm = nc.tensor.matmul(ps[:, 2 * ((t0 + j) % 2), 0:width], lhsT, rhs,
                                                  start=k == 0 and x == 0, stop=k == KD - 1 and x == 2)
                        if k == KD - 1:
                            mm.then_inc(tile_done, 1)
            for j in range(0 if ln_at is None else 2, n_tok_tiles):
                t = t0 + j
                if t >= 2:
                    pe.wait_ge(*out_of(t - 2))
                terms = []
                for k in range(KD):
                    terms += split_terms(a_hi(k, j), a_lo(k, j), wv_hi[:, k, :], wv_lo[:, k, :])
                product(ps[:, 2 * (t % 2), 0:width], terms, tile_done)

        sums_used = sem("sums_used")
        sq_ready = sem("sq_ready")
        sum1_done = sem("sum1_done")
        sum2_done = sem("sum2_done")
        mean_ready = sem("mean_ready")
        std_ready = sem("std_ready")
        var_ready = sem("var_ready")
        v_normed = sem("v_normed")
        centred = sem("centred")
        scaled = sem("scaled")
        ln_hi = sem("ln_hi")
        ln_lo = sem("ln_lo")
        ln_whole = sem("ln_whole")
        n_ln = {"pe": 0, "act": 0, "dve": 0}

        LN_TILES = [KA, KD, KD, KD, KD]

        def sums_at(ln):
            return sum(LN_TILES[:ln]) + ln + 1

        def act_square(act, src, par, ready, ready_at, ln, m):
            act.wait_ge(ready, ready_at)
            act.wait_ge(sum2_done, sums_at(ln) + m - 1)
            nc.scalar.activation(sq[:, par, :], src, ACT.Square).then_inc(sq_ready, 1)

        def pool_sums(pool, src, par, ready, ready_at, ln, m):
            pool.wait_ge(ready, ready_at)
            pool.wait_ge(sum1_done, sums_at(ln) + m)
            nc.gpsimd.tensor_tensor(sum1[:, :], sum1[:, :], src, ALU.add).then_inc(sum1_done, 1)
            pool.wait_ge(sq_ready, sum(LN_TILES[:ln]) + m + 1)
            pool.wait_ge(sum2_done, sums_at(ln) + m)
            nc.gpsimd.tensor_tensor(sum2[:, :], sum2[:, :], sq[:, par, :], ALU.add).then_inc(sum2_done, 1)

        def pool_clear_sums(pool, ln):
            if ln:
                pool.wait_ge(sums_used, 2 * ln)
            nc.gpsimd.memset(sum1[:, :], 0.0).then_inc(sum1_done, 1)
            nc.gpsimd.memset(sum2[:, :], 0.0).then_inc(sum2_done, 1)

        def pe_ln(pe, ln):
            for b, v, done in ((4, sum1, sum1_done), (6, sum2, sum2_done)):
                pe.wait_ge(done, sums_at(ln) + LN_TILES[ln])
                for half in range(2):
                    mm = nc.tensor.matmul(ps[:, b + half, 0:HALF], ones, v[:, half * HALF:(half + 1) * HALF],
                                          start=True, stop=True)
                mm.then_inc(sums_used, 1)

        def act_ln_stats(act, n_feat):
            n = n_ln["act"] = n_ln["act"] + 1
            nc.scalar.activation(stat[:, 63:64], cst[:, C_EPS:C_EPS + 1], ACT.Sqrt)
            act.wait_ge(sums_used, 2 * n - 1)
            nc.scalar.activation(halves(mean[:, :]), ps[:, 4:6, 0:HALF], ACT.Copy, scale=1.0 / n_feat).then_inc(mean_ready, 1)
            act.wait_ge(var_ready, n)
            nc.scalar.activation(tmp[:, 0, :], tmp[:, 0, :], ACT.Sqrt,
                                 bias=cst[:, C_EPS:C_EPS + 1]).then_inc(std_ready, 1)

        def dve_ln_stats(dve, n_feat):
            n = n_ln["dve"] = n_ln["dve"] + 1
            dve.wait_ge(mean_ready, n)
            c = dve_chain(nc.vector.tensor_tensor(tmp[:, 1, :], mean[:, :], mean[:, :], ALU.mult))
            dve.wait_ge(dve_step, c)
            dve.wait_ge(sums_used, 2 * n)
            nc.vector.scalar_tensor_tensor(out=halves(tmp[:, 0, :]), in0=ps[:, 6:8, 0:HALF], scalar=1.0 / n_feat,
                                           in1=halves(tmp[:, 1, :]), op0=ALU.mult, op1=ALU.subtract).then_inc(var_ready, 1)
            dve.wait_ge(std_ready, n)
            c = dve_chain(nc.vector.reciprocal(rstd[:, :], tmp[:, 0, :]))
            dve.wait_ge(dve_step, c)

        def pool_ln(pool, j):
            pool.wait_ge(mean_ready, j + 2)
            for m in range(KD):
                nc.gpsimd.tensor_tensor(resid[:, m, :], resid[:, m, :], mean[:, :], ALU.subtract).then_inc(centred, 1)
            if j < 3:
                for m in range(KD):
                    pool.wait_ge(ln_lo, KD * j + m + 1)
                    nc.gpsimd.tensor_scalar(resid[:, m, :], resid[:, m, :], lnp[:, 16 * j + 8 + m:16 * j + 9 + m], None,
                                            ALU.add).then_inc(ln_whole, 1)

        def dve_ln(dve, j):
            dve_ln_stats(dve, D)
            for m in range(KD + 2):
                if m < KD:
                    dve.wait_ge(centred, KA + KD * j + m + 1)
                    nc.vector.scalar_tensor_tensor(out=resid[:, m, :], in0=resid[:, m, :], scalar=lnp[:, 16 * j + m:16 * j + m + 1],
                                                   in1=rstd[:, :], op0=ALU.mult, op1=ALU.mult).then_inc(scaled, 1)
                if m >= 2 and j < 3:
                    n = m - 2
                    dve.wait_ge(ln_hi, KD * j + n + 1)
                    nc.vector.scalar_tensor_tensor(out=x_tile(x_lo, n), in0=resid[:, n, :],
                                                   scalar=lnp[:, 16 * j + 8 + n:16 * j + 9 + n],
                                                   in1=x_tile(x_hi, n).bitcast(F32), op0=ALU.add,
                                                   op1=ALU.subtract).then_inc(ln_lo, 1)

        def act_ln(act, j):
            act_ln_stats(act, D)
            for m in range(KD):
                act.wait_ge(scaled, KA + KD * j + m + 1)
                nc.scalar.activation(x_tile(x_hi, m) if j < 3 else resid[:, m, :], resid[:, m, :], ACT.Identity,
                                     bias=lnp[:, 16 * j + 8 + m:16 * j + 9 + m]).then_inc(ln_hi, 1)

        sq_h_ready = sem("sq_h_ready")
        h_hi_ready = sem("h_hi_ready")
        h_lo_ready = sem("h_lo_ready")
        MLP_W, MLP_T = (W_MLP0, W_MLP1), (T_MLP0, T_MLP1)

        def each(eng, count, body, last_apart, first_apart=False):
            if first_apart:
                body(0, True, False)
            with eng.Fori(int(first_apart), count - 1 if last_apart else count) as i:
                body(i, False, False)
            if last_apart:
                body(count - 1, False, True)

        def pe_mlp(pe, l):
            for h in range(2):
                s0, t0 = MLP_W[l] + 16 * h, MLP_T[l] + 24 * h
                up_read, down_read = out_of(t0)[1], out_of(t0 + 16)[1]

                def up(i, first, last):
                    for e in range(2):
                        if first and e == 0:
                            first_slot()
                            continue
                        pe.wait_ge(split_ready, s0 + e + 1 + 2 * i)
                        for n in range(2):
                            pe.wait_ge(read_act, up_read + 2 * e + n - 2 + 4 * i)
                            feature_tile(pe, (s0 + e) % 2, 2 * ((t0 + n) % 2), P * n, KD, 256, xk(x_hi), xk(x_lo))

                def down(i, first, last):
                    for e in range(2):
                        pe.wait_ge(split_ready, s0 + 8 + e + 1 + 2 * i)
                        pe.wait_ge(read_dve, down_read + e - 2 + 2 * i)
                        if first and e == 1:
                            pe.wait_ge(*out_of(t0 + 15))
                        feature_tile(pe, (s0 + e) % 2, 2 * ((t0 + e) % 2), 0, 16, P,
                                     lambda k: h_hi[:, k, :], lambda k: h_lo[:, k, :],
                                     (13, 32 * l + 16 * h + 16) if first and e == 0 else None)

                def first_slot():
                    pe.wait_ge(split_ready, s0 + 1)
                    wv_hi, wv_lo = (x[:, s0 % 2, :].rearrange("p (k c) -> p k c", c=256) for x in (w_hi, w_lo))
                    for k in range(KD):
                        pe.wait_ge(ln_lo, KD * 2 * l + k + 1)
                        for n in range(2):
                            cw = slice(P * n, P * n + P)
                            for half in range(2):
                                cols = slice(half * HALF, (half + 1) * HALF)
                                terms = split_terms(wv_hi[:, k, cw], wv_lo[:, k, cw],
                                                    x_tile(x_hi, k)[:, cols], x_tile(x_lo, k)[:, cols])
                                for x, (lhsT, rhs) in enumerate(terms):
                                    mm = nc.tensor.matmul(ps[:, 2 * ((t0 + n) % 2) + half, 0:HALF], lhsT, rhs,
                                                          start=k == 0 and x == 0, stop=k == KD - 1 and x == 2)
                            if k == KD - 1:
                                mm.then_inc(tile_done, 1)

                pe.wait_ge(*out_of(t0 - 1))
                each(pe, 4, up, False, h == 0)
                pe.wait_ge(*out_of(t0 + 14))
                pe.wait_ge(h_lo_ready, 32 * l + 16 * h + 13)
                each(pe, 4, down, False, True)

        def act_mlp(act, l):
            for h in range(2):
                s0, t0, q0 = MLP_W[l] + 16 * h, MLP_T[l] + 24 * h, 32 * l + 16 * h

                def split(i, e, phase, tiles):
                    s = s0 + phase + e + 1
                    split_hi(act, s % 2, loaded(s) + 16 * i, tiles, SLOT)

                def up(i, first, last):
                    for e in range(2):
                        if not (first and e == 0):
                            split(i, e, 0, t0 + 2 * e + 4 * i)
                        for n in range(2):
                            t, q = t0 + 2 * e + n, q0 + 2 * e + n
                            act.wait_ge(tile_done, t + 1 + 4 * i)
                            act.wait_ge(sq_h_ready, max(q - 1, 0) + 4 * i)
                            nc.scalar.activation(halves(tmp[:, n, :]), pair(t), ACT.Relu).then_inc(read_act, 1)
                            act.wait_ge(read_act, out_of(t)[1] + 4 * i)
                            nc.scalar.activation(h_hi[:, bass.ds(4 * i + 2 * e + n, 1), :], tmp[:, n:n + 1, :],
                                                 ACT.Square).then_inc(h_hi_ready, 1)

                def down(i, first, last):
                    for e in range(2):
                        if not (last and e == 1 and s0 + 16 == N_SLOTS):
                            split(i, e, 8, t0 + 16 + e + 2 * i)
                        if h == 1:
                            t = t0 + 16 + e
                            act_square(act, resid[:, bass.ds(2 * i + e, 1), :], e, read_dve, out_of(t)[1] + 2 * i,
                                       2 * l + 2, 2 * i + e)

                each(act, 4, up, False, h == 0)
                each(act, 4, down, h == 1)

        def dve_mlp(dve, l):
            for h in range(2):
                s0, t0, q0 = MLP_W[l] + 16 * h, MLP_T[l] + 24 * h, 32 * l + 16 * h

                def up(i, first, last):
                    for e in range(2):
                        if not (first and e == 0):
                            split_lo(dve, s0 + e + 2 + 2 * i, (s0 + e + 1) % 2, SLOT)
                        for n in range(2):
                            q = q0 + 2 * e + n
                            dve.wait_ge(sq_h_ready, q + 1 + 4 * i)
                            dve.wait_ge(h_hi_ready, q + 1 + 4 * i)
                            j = bass.ds(4 * i + 2 * e + n, 1)
                            nc.vector.tensor_tensor(h_lo[:, j, :], sq[:, n:n + 1, :], h_hi[:, j, :].bitcast(F32),
                                                    ALU.subtract).then_inc(h_lo_ready, 1)

                def down(i, first, last):
                    for e in range(2):
                        if not (last and e == 1 and s0 + 16 == N_SLOTS):
                            split_lo(dve, s0 + 8 + e + 2 + 2 * i, (s0 + e + 1) % 2, SLOT)
                        t = t0 + 16 + e
                        dve.wait_ge(tile_done, t + 1 + 2 * i)
                        r = resid[:, bass.ds(2 * i + e, 1), :].rearrange("p a (h t) -> p (a h) t", h=2)
                        if h == 0:
                            dve.wait_ge(ln_whole, KD * (2 * l + 1))
                            nc.vector.scalar_tensor_tensor(out=r, in0=r, scalar=ALPHA, in1=pair(t), op0=ALU.mult,
                                                           op1=ALU.add).then_inc(read_dve, 1)
                        else:
                            nc.vector.tensor_tensor(r, r, pair(t), ALU.add).then_inc(read_dve, 1)

                each(dve, 4, up, False, h == 0)
                each(dve, 4, down, h == 1)

        def pool_mlp(pool, l):
            pool_clear_sums(pool, 2 * l + 2)
            for h in range(2):
                t0, q0 = MLP_T[l] + 24 * h, 32 * l + 16 * h

                def up(i, first, last):
                    for e in range(2):
                        for n in range(2):
                            t, q = t0 + 2 * e + n, q0 + 2 * e + n
                            pool.wait_ge(read_act, out_of(t)[1] + 4 * i)
                            pool.wait_ge(h_lo_ready, max(q - 1, 0) + 4 * i)
                            nc.gpsimd.tensor_tensor(sq[:, n, :], tmp[:, n, :], tmp[:, n, :],
                                                    ALU.mult).then_inc(sq_h_ready, 1)

                def down(i, first, last):
                    for e in range(2):
                        pool_sums(pool, resid[:, bass.ds(2 * i + e, 1), :].rearrange("p a t -> p (a t)"), e,
                                  read_dve, out_of(t0 + 16 + e)[1] + 2 * i, 2 * l + 2, 2 * i + e)

                each(pool, 4, up, False)
                if h == 1:
                    each(pool, 4, down, False)

        def sp_mlp(sp, l):
            m_up, m_down = w["w_up"][l].rearrange("(k p) n -> p k n", p=P), w["w_down"][l]
            for h in range(2):
                s0 = MLP_W[l] + 16 * h

                def up(i, first, last):
                    for e in range(2):
                        s = s0 + e
                        sp.wait_ge(split_ready, s - 1 + 2 * i)
                        dst = w_raw[:, s % 2, :].rearrange("p (k c) -> p k c", c=256)
                        sp.dma_start(dst, m_up[:, :, bass.ds(h * FF // 2 + 256 * e + 512 * i, 256)]).then_inc(raw_in[s % 2], 16)

                def down(i, first, last):
                    for e in range(2):
                        s = s0 + 8 + e
                        sp.wait_ge(split_ready, s - 1 + 2 * i)
                        dst = w_raw[:, s % 2, :].rearrange("p (k c) -> p k c", c=P)
                        rows = m_down[h * FF // 2:(h + 1) * FF // 2, bass.ds(P * e + 2 * P * i, P)]
                        sp.dma_start(dst, rows.rearrange("(k p) n -> p k n", p=P)).then_inc(raw_in[s % 2], 16)

                each(sp, 4, up, False)
                each(sp, 4, down, False)

        def sp_slots(sp, s0, n):
            for s in range(s0, s0 + n):
                if s >= 2:
                    sp.wait_ge(split_ready, s - 1)
                load_slot(sp, s, slots[s])

        small_in = sem("small_in")
        phi1_in = sem("phi1_in")
        phi1_b_in = sem("phi1_b_in")
        cmp_in = [sem("cmp_in_even"), sem("cmp_in_odd")]
        rows_ready = sem("rows_ready")
        turned = sem("turned")
        turned_act = sem("turned_act")
        turned_dve = sem("turned_dve")
        params_turned = sem("params_turned")
        params_read = sem("params_read")
        hidden = sem("hidden")
        gelued = sem("gelued")
        blocks = sem("blocks")
        blocks_read = sem("blocks_read")

        cmp_raw = [xalt, walt]
        xc = region(arena, 0, 2, 8, 512)
        phi1 = region(arena, 8192, 16, 2, P)
        gel = region(arena, 12288, 2, 512)
        pe_rows = region(arena, 13312, P, parts=32)
        pe_cols = region(arena, 13440, 32)
        ln_rows = region(arena, 13472, P, parts=76)
        pe_row = region(arena, 13600, 2 * P, parts=1)

        def load_phi1(eng, dst, done):
            for e in range(2):
                src = w["w_phi1"].rearrange("(l e) c d n -> e d l c n", e=2)[e]
                for c in range(2):
                    eng.dma_start(dst[HD * e:HD * e + HD, :, c, :], src[:, :, c, :]).then_inc(done, 16)

        def sp_stage0(sp):
            pt = w["page_table"]
            sp.dma_start(cst[:, :], w["consts"]).then_inc(consts_in, 16)
            for q in range(4):
                sp.dma_start(pages_c[:, q:q + 1], bass.AP(pt.tensor, pt.offset + 16 * q, [[1, 16], [0, 8], [1, 1]])
                             ).then_inc(consts_in, 16)
            load_phi1(sp, phi1, phi1_in)
            for b in range(NB):
                sp.dma_start(pages_s[:, b:b + 1], bass.AP(pt.tensor, pt.offset + 8 * b, [[1, 8], [0, 16], [1, 1]])
                             ).then_inc(small_in, 16)
            row = 0
            for l in range(2):
                for name in ("ln1_g", "ln1_b", "ln2_g", "ln2_b"):
                    sp.dma_start(ln_rows[row:row + 8, :], w[name][l].rearrange("(k p) -> k p", p=P)).then_inc(small_in, 16)
                    row += 8
            for name in ("ln_v_g", "ln_v_b"):
                sp.dma_start(ln_rows[row:row + KA, :], w[name][0].rearrange("(k p) -> k p", p=P)).then_inc(small_in, 16)
                row += KA
            for c in range(2):
                for e in range(2):
                    src = w["cmp_pe"].rearrange("(l e) c d -> e c l d", e=2)[e, c]
                    sp.dma_start(pe_rows[16 * c:16 * c + 16, HD * e:HD * e + HD], src).then_inc(small_in, 16)
            for c in range(2):
                sp.dma_start(phi2[:, c, :], w["w_phi2"][c]).then_inc(small_in, 16)

        N_SMALL = 16 * (NB + 8 + 2 + 4 + 2)
        PHI1_ONCE = 16 * 4
        cmp_rows_dram = w["cache_cmp_kv"].rearrange("n (a s) c h d -> (n a) (s c h d)", s=STRIDE)

        def pool_stage0(pool):
            pool.wait_ge(rows_ready, 1)
            for q in range(4):
                if q >= 2:
                    pool.wait_ge(turned, 16 * (q - 1))
                nc.gpsimd.indirect_dma_start(cmp_raw[q % 2][:, 0:STRIDE * ROW], None, cmp_rows_dram,
                                             bass.IndirectOffsetOnAxis(rows_c[:, q:q + 1], 0)).then_inc(cmp_in[q % 2], 16)

        def turn_reader(n):
            return ("dve", n // 2 + 1) if n % 2 == 0 else ("act", n // 2 + 1)

        def pe_compress_turn(pe, raw, n0, n_str, first_wait, cs=(0, 1)):
            at = raw[0:n_str, 0:STRIDE * ROW].rearrange("p (s e x) -> p s e x", s=8, e=2)
            for c in cs:
                for s in range(8):
                    n = n0 + 8 * c + s
                    if n - 4 >= first_wait:
                        who, v = turn_reader(n - 4)
                        pe.wait_ge(turned_dve if who == "dve" else turned_act, v)
                    for e in range(2):
                        for pr in range(2):
                            mm = nc.tensor.transpose(ps[:, 2 + n % 4, (2 * e + pr) * n_str:(2 * e + pr + 1) * n_str],
                                                     at[:, s, e, (2 * c + pr) * P:(2 * c + pr + 1) * P],
                                                     ident[0:n_str, 0:n_str])
                    mm.then_inc(turned, 1)

        def compress_copy(eng, who, dst, n0, n_str, free_at, cs=(0, 1)):
            for c in cs:
                if free_at is not None:
                    eng.wait_ge(hidden, free_at + c)
                for s in range(8):
                    n = n0 + 8 * c + s
                    if turn_reader(n)[0] != who:
                        continue
                    eng.wait_ge(turned, n + 1)
                    for e in range(2):
                        for hp in range(2):
                            src = ps[HD * hp:HD * hp + HD, 2 + n % 4, 2 * e * n_str:2 * (e + 1) * n_str]
                            to = dst[HD * e:HD * e + HD, c, s, :].rearrange("p (g h n) -> p g h n", g=2, h=2)[:, :, hp, :]
                            src = src.rearrange("p (g n) -> p g n", g=2)
                            ins = nc.scalar.activation(to, src, ACT.Copy) if who == "act" else nc.vector.tensor_copy(to, src)
                    ins.then_inc(turned_act if who == "act" else turned_dve, 1)

        def pe_compress_hidden(pe, q, src, wts, n0, n_seq, n_str, cs=(0, 1)):
            for c in cs:
                for m in range(14, 16):
                    who, v = turn_reader(n0 + 8 * c + m - 8)
                    pe.wait_ge(turned_dve if who == "dve" else turned_act, v)
                if q:
                    pe.wait_ge(gelued, 2 * (q - 1) + c + 1)
                cols = NG * n_seq * n_str
                out = ps[:, 6 + c, 0:cols]
                out1 = out.rearrange("p (a n) -> p a n", n=n_str)[:, :, 0:n_str - 1]
                for s in range(8):
                    nc.tensor.matmul(out, wts[:, s, c, :], src[:, c, s, :], start=s == 0, stop=False,
                                     skip_group_check=True)
                for s in range(8):
                    nxt = src[:, c, s, :].rearrange("p (a n) -> p a n", n=n_str)[:, :, 1:n_str]
                    mm = nc.tensor.matmul(out1, wts[:, 8 + s, c, :], nxt, start=False, stop=s == 7,
                                          skip_group_check=True)
                mm.then_inc(hidden, 1)

        def act_compress_gelu(act, q, dst, cols, cs=(0, 1)):
            for c in cs:
                act.wait_ge(hidden, 2 * q + c + 1)
                if q:
                    act.wait_ge(blocks, q)
                nc.scalar.activation(dst[:, c, 0:cols], ps[:, 6 + c, 0:cols], ACT.Gelu_apprx_tanh,
                                     bias=pe_bias[:, c:c + 1]).then_inc(gelued, 1)

        def pe_compress_out(pe, q, src, n_seq, n_str):
            pe.wait_ge(gelued, 2 * q + 2)
            if q:
                pe.wait_ge(blocks_read, q)
            per = n_seq * n_str
            for h in range(NG):
                e, pr = h % 2, h // 2
                nc.tensor.matmul(ps[HD * e:HD * e + HD, 0, pr * per:(pr + 1) * per], phi2[:, 0, :],
                                 src[:, 0, h * per:(h + 1) * per], start=True, stop=True)
            for b in range(n_seq):
                for h in range(NG):
                    at = h * per + b * n_str
                    mm = nc.tensor.matmul(ps[0:n_str, 1, (b * NG + h) * HD:(b * NG + h + 1) * HD],
                                          src[:, 1, at:at + n_str], phi2[:, 1, :], start=True, stop=True)
            mm.then_inc(blocks, 1)

        def pe_stage0(pe):
            def params():
                pe.wait_ge(small_in, N_SMALL)
                nc.tensor.transpose(ps[:, 7, 0:76], ln_rows[:, :], ident[0:76, 0:76])
                nc.tensor.transpose(ps[:, 7, 128:160], pe_rows[:, :], ident[0:32, 0:32]).then_inc(params_turned, 1)
                pe.wait_ge(params_read, 1)
                pe.wait_ge(phi1_in, PHI1_ONCE)
                for c in range(2):
                    for l in range(16):
                        mm = nc.tensor.matmul(ps[0:1, 7, 256 + P * c:256 + P * c + P], pe_cols[:, 16 * c + l:16 * c + l + 1],
                                              phi1[:, l, c, :], start=l == 0, stop=l == 15)
                mm.then_inc(params_turned, 1)
                pe.wait_ge(params_read, 2)
                for c in range(2):
                    mm = nc.tensor.transpose(ps[:, 7, 160 + c:161 + c], pe_row[:, P * c:P * c + P], ident[0:1, 0:1])
                mm.then_inc(params_turned, 1)
                pe.wait_ge(params_read, 3)

            pe.wait_ge(consts_in, 16 * 5)
            for q in range(4):
                if q == 0:
                    pe.wait_ge(cmp_in[0], 16)
                    pe_compress_turn(pe, cmp_raw[0], 0, P, 0)
                    params()
                pe_compress_hidden(pe, q, xc, phi1, 16 * q, 2, NSTR, (0,))
                if q < 3:
                    pe.wait_ge(cmp_in[(q + 1) % 2], 16 * ((q + 1) // 2 + 1))
                    pe_compress_turn(pe, cmp_raw[(q + 1) % 2], 16 * (q + 1), P, 0, (0,))
                pe_compress_hidden(pe, q, xc, phi1, 16 * q, 2, NSTR, (1,))
                if q < 3:
                    pe_compress_turn(pe, cmp_raw[(q + 1) % 2], 16 * (q + 1), P, 0, (1,))
                    pe_compress_out(pe, q, gel, 2, NSTR)
            pe_compress_out(pe, 3, gel, 2, NSTR)
            meet(pe, 0)

        def act_stage0(act):
            compress_copy(act, "act", xc, 0, P, None)
            for q in range(4):
                for c in range(2):
                    if q == 3 and c == 0:
                        act.wait_ge(turned, 64)
                        act_split(act, 0)
                        act_split(act, 1)
                    act_compress_gelu(act, q, gel, 512, (c,))
                    if q < 3:
                        compress_copy(act, "act", xc, 16 * (q + 1), P, 2 * q + 1, (c,))
            meet(act, 0)

        def dve_stage0(dve):
            def params():
                dve.wait_ge(small_in, N_SMALL)
                nc.vector.tensor_scalar(rows_s[:, :], pages_s[:, :], float(PAGE // 8), cst[:, C_K16:C_K16 + 1],
                                        ALU.mult, ALU.add).then_inc(rows_ready, 1)
                dve.wait_ge(params_turned, 1)
                nc.vector.tensor_copy(lnp[:, :], ps[:, 7, 0:76])
                nc.vector.tensor_copy(pe_cols[:, :], ps[:, 7, 128:160]).then_inc(params_read, 1)
                dve.wait_ge(params_turned, 2)
                nc.vector.tensor_copy(pe_row[:, :], ps[0:1, 7, 256:512]).then_inc(params_read, 1)
                dve.wait_ge(params_turned, 3)
                nc.vector.tensor_copy(pe_bias[:, :], ps[:, 7, 160:162]).then_inc(params_read, 1)

            dve.wait_ge(consts_in, 16 * 5)
            nc.vector.tensor_scalar(rows_c[:, :], pages_c[:, :], float(PAGE // STRIDE), cst[:, C_K8:C_K8 + 1],
                                    ALU.mult, ALU.add).then_inc(rows_ready, 1)
            for q in range(5):
                if q < 4:
                    compress_copy(dve, "dve", xc, 16 * q, P, 2 * q - 1 if q else None)
                if q == 0:
                    params()
                if q == 4:
                    dve_split(dve, 0)
                    dve_split(dve, 1)
                if q:
                    dve.wait_ge(blocks, q)
                    b = 2 * (q - 1)
                    nc.vector.tensor_copy(kc_s[:, b:b + 2, :, :].rearrange("p b g n -> p g b n"),
                                          ps[:, 0, 0:256].rearrange("p (g b n) -> p g b n", g=2, b=2))
                    nc.vector.tensor_copy(vc_s[:, b:b + 2, :],
                                          ps[0:NSTR, 1, :].rearrange("p (b x) -> p b x", b=2)).then_inc(blocks_read, 1)
            meet(dve, 0)

        rows_in = sem("rows_in")
        x_turned = sem("x_turned")
        x_read = sem("x_read")
        x_hi_ready = sem("x_hi_ready")
        mem_hi_ready = sem("mem_hi_ready")
        operands_ready = sem("operands_ready")
        x_rows = region(xalt, 0, 5, D)
        m_rows = region(xalt, 5 * D, 2, D)
        m_hi, m_lo = h_lo[:, 0:4, :].rearrange("p a t -> p (a t)"), h_lo[:, 4:8, :].rearrange("p a t -> p (a t)")
        m_hi, m_lo = [x[:, 0:2048].rearrange("p (k m) -> p k m", m=MEM) for x in (m_hi, m_lo)]
        mkv = region(arena, 13184, 2, 2, 512)

        def pool_stage1(pool):
            pool.wait_ge(turned, 48)
            pool.dma_start(x_rows[:, 0:4, :], w["x_prompt"][0].rearrange("(j p) d -> p j d", p=P)).then_inc(rows_in, 16)
            pool.dma_start(x_rows[0:SAMP, 4, :], w["x_sample"].rearrange("b t d -> (b t) d")).then_inc(rows_in, 16)
            pool.dma_start(m_rows[:, :, :], w["mem_prompt"][0].rearrange("(j p) d -> p j d", p=P)).then_inc(rows_in, 16)
            meet(pool, 0)
            meet(pool, 1)

        def pe_stage1(pe):
            pe.wait_ge(rows_in, 48)
            for n in range(14):
                if n >= 4:
                    pe.wait_ge(x_read, n - 3)
                for k in range(4):
                    if n < 10:
                        j, kk = n // 2, 4 * (n % 2) + k
                        m = P if j < 4 else SAMP
                        src = x_rows[0:m, j, kk * P:(kk + 1) * P]
                    else:
                        m = P
                        src = m_rows[:, (n - 10) // 2, (4 * (n % 2) + k) * P:(4 * (n % 2) + k + 1) * P]
                    mm = nc.tensor.transpose(ps[:, 4 + n % 4, k * m:(k + 1) * m], src, ident[0:m, 0:m])
                mm.then_inc(x_turned, 1)
            pe.wait_ge(operands_ready, 1)
            for s in range(W_MEM, W_MEM + 4):
                pe_token_slot(pe, s, 2 * s, 2, lambda k, j: m_hi[:, k, j * P:(j + 1) * P],
                              lambda k, j: m_lo[:, k, j * P:(j + 1) * P], 256)
            meet(pe, 1)

        def act_stage1(act):
            for n in range(10, 14):
                act.wait_ge(x_turned, n + 1)
                k = 4 * (n % 2)
                nc.scalar.activation(m_hi[:, k:k + 4, (n - 10) // 2 * P:((n - 10) // 2 + 1) * P],
                                     ps[:, 4 + n % 4, :].rearrange("p (k m) -> p k m", k=4), ACT.Copy).then_inc(mem_hi_ready, 1)
            for s in range(W_MEM, W_MEM + 4):
                if s:
                    act_split(act, s + 1)
                if s == W_MEM + 1:
                    act.wait_ge(x_read, 10)
                if s in (W_MEM + 1, W_MEM + 2):
                    k = s - W_MEM - 1
                    nc.scalar.activation(x3(x_hi)[:, 4 * k:4 * k + 4, :], resid[:, 4 * k:4 * k + 4, :],
                                         ACT.Copy).then_inc(x_hi_ready, 1)
                for j in range(2):
                    t = 2 * s + j
                    act.wait_ge(tile_done, t + 1)
                    nc.scalar.activation(mkv[:, s // 2, j, 256 * (s % 2):256 * (s % 2) + 256],
                                         ps[:, 2 * (t % 2), 0:256], ACT.Copy).then_inc(read_act, 1)
            meet(act, 1)

        def dve_stage1(dve):
            for n in range(14):
                dve.wait_ge(x_turned, n + 1)
                k = 4 * (n % 2)
                bank = ps[:, 4 + n % 4, :]
                if n < 10:
                    m, c = (P, P * (n // 2)) if n < 8 else (SAMP, SEQ)
                    nc.vector.tensor_copy(resid[:, k:k + 4, c:c + m],
                                          bank[:, 0:4 * m].rearrange("p (k m) -> p k m", k=4)).then_inc(x_read, 1)
                else:
                    dve.wait_ge(mem_hi_ready, n - 9)
                    cols = slice((n - 10) // 2 * P, ((n - 10) // 2 + 1) * P)
                    ins = nc.vector.tensor_tensor(m_lo[:, k:k + 4, cols], bank.rearrange("p (k m) -> p k m", k=4),
                                                  m_hi[:, k:k + 4, cols].bitcast(F32), ALU.subtract)
                    ins.then_inc(x_read, 1)
            dve.wait_ge(x_read, 14)
            nc.vector.memset(x_hi[:, KD * TOK:XPAD].bitcast(F32), 0.0)
            nc.vector.memset(x_lo[:, KD * TOK:XPAD].bitcast(F32), 0.0).then_inc(operands_ready, 1)
            for s in range(W_MEM, W_MEM + 5):
                if s >= 2:
                    dve_split(dve, s)
                if s in (W_MEM + 2, W_MEM + 3):
                    k = s - W_MEM - 2
                    dve.wait_ge(x_hi_ready, k + 1)
                    nc.vector.tensor_tensor(x3(x_lo)[:, 4 * k:4 * k + 4, :], resid[:, 4 * k:4 * k + 4, :],
                                            x3(x_hi)[:, 4 * k:4 * k + 4, :].bitcast(F32), ALU.subtract)
            meet(dve, 1)

        def strided(start, *dims):
            return bass.AP(start.tensor, start.offset, [list(start.ap[0])] + [list(d) for d in dims])

        TURN_LAG, SUM_LAG = 3, 5

        def unit_sems(name):
            return {k: sem(f"{name}_{k}") for k in
                    ("scored", "max_ready", "exp_done", "normed", "turned", "pt_ready", "summed", "hi", "lo")}

        def pe_units(pe, us, sm):
            tiles = 0
            for n in range(len(us) + SUM_LAG):
                if n < len(us):
                    u = us[n]
                    if n >= 4:
                        pe.wait_ge(sm["exp_done"], n - 3)
                    nc.tensor.matmul(ps[:, 2 + n % 4, 0:u["n"]], u["q"], u["k"], start=True,
                                     stop=True).then_inc(sm["scored"], 1)
                v = n - TURN_LAG
                if 0 <= v < len(us):
                    u = us[v]
                    pe.wait_ge(sm["normed"], v + 1)
                    if v >= 2:
                        pe.wait_ge(sm["pt_ready"], v - 1)
                    for c in range(0, u["n"], P):
                        m = min(P, u["n"] - c)
                        mm = nc.tensor.transpose(ps[0:m, 6 + v % 2, c:c + P], u["p"][:, v % 4, c:c + m], ident)
                    mm.then_inc(sm["turned"], 1)
                v = n - SUM_LAG
                if v >= 0:
                    u = us[v]
                    pe.wait_ge(sm["pt_ready"], v + 1)
                    if tiles >= 2:
                        pe.wait_ge(sm["lo"], tiles - 1)
                    e, i = u["place"]
                    chunks = range(0, u["n"], P)
                    for c in chunks:
                        mm = nc.tensor.matmul(ps[HD * e:HD * e + HD, tiles % 2, i * P:(i + 1) * P], u["v"](c // P),
                                              u["pt"][0:min(P, u["n"] - c), v % 4, c:c + P],
                                              start=u["first"] and c == 0, stop=u["last"] and c == chunks[-1])
                    mm.then_inc(sm["summed"], 1)
                    tiles += u["closes"] is not None

        def act_units(act, us, sm):
            tiles = 0
            for n in range(len(us) + SUM_LAG + 1):
                v = n - TURN_LAG - 1
                if 0 <= v < len(us):
                    u = us[v]
                    act.wait_ge(sm["turned"], v + 1)
                    if v >= 4:
                        act.wait_ge(sm["summed"], v - 3)
                    m = min(P, u["n"])
                    nc.scalar.activation(u["pt"][0:m, v % 4, 0:max(P, u["n"])], ps[0:m, 6 + v % 2, 0:max(P, u["n"])],
                                         ACT.Copy).then_inc(sm["pt_ready"], 1)
                if n < len(us):
                    u, r = us[n], n % 4
                    act.wait_ge(sm["max_ready"], n + 1)
                    if n >= 4:
                        act.wait_ge(sm["turned"], n - 3)
                    nc.scalar.activation(u["p"][:, n % 4, 0:u["n"]], ps[:, 2 + n % 4, 0:u["n"]], ACT.Exp,
                                         bias=stat[:, 4 + r:5 + r], scale=SCALE if u["mask"] is None else -1.0,
                                         accum_out=stat[:, 8 + r:9 + r]).then_inc(sm["exp_done"], 1)
                v = n - SUM_LAG - 1
                if v >= 0 and us[v]["closes"] is not None:
                    act.wait_ge(sm["summed"], v + 1)
                    nc.scalar.activation(x_tile(x_hi, us[v]["closes"])[:, 0:SEQ], ps[:, tiles % 2, :],
                                         ACT.Copy).then_inc(sm["hi"], 1)
                    tiles += 1

        def dve_units(dve, us, sm):
            tiles = 0
            for n in range(len(us) + SUM_LAG + 2):
                v = n - 2
                if 0 <= v < len(us):
                    r = v % 4
                    dve.wait_ge(sm["exp_done"], v + 1)
                    recip = dve_chain(nc.vector.reciprocal(stat[:, 12 + r:13 + r], stat[:, 8 + r:9 + r]))
                if n < len(us):
                    u, r = us[n], n % 4
                    dve.wait_ge(sm["scored"], n + 1)
                    sc = ps[:, 2 + n % 4, 0:u["n"]]
                    if n >= 4:
                        dve.wait_ge(sm["exp_done"], n - 3)
                    if u["mask"] is None:
                        c = dve_chain(nc.vector.reduce_max(stat[:, r:r + 1], sc, AX))
                        dve.wait_ge(dve_step, c)
                        nc.vector.tensor_scalar(stat[:, 4 + r:5 + r], stat[:, r:r + 1], -SCALE, None,
                                                ALU.mult).then_inc(sm["max_ready"], 1)
                    else:
                        nc.vector.tensor_tensor_reduce(sc, sc, u["mask"], -SCALE, -3 * NEG, ALU.add, ALU.min,
                                                       stat[:, 4 + r:5 + r]).then_inc(sm["max_ready"], 1)
                if 0 <= v < len(us):
                    u, r = us[v], v % 4
                    pr = u["p"][:, v % 4, 0:u["n"]]
                    dve.wait_ge(dve_step, recip)
                    if u["gate"] is None:
                        ins = nc.vector.tensor_scalar(pr, pr, stat[:, 12 + r:13 + r], None, ALU.mult)
                    else:
                        ins = nc.vector.tensor_scalar(pr, pr, stat[:, 12 + r:13 + r], u["gate"], ALU.mult, ALU.mult)
                    ins.then_inc(sm["normed"], 1)
                v = n - SUM_LAG - 2
                if v >= 0 and us[v]["closes"] is not None:
                    dve.wait_ge(sm["hi"], tiles + 1)
                    k = us[v]["closes"]
                    nc.vector.tensor_tensor(x_tile(x_lo, k)[:, 0:SEQ], ps[:, tiles % 2, :],
                                            x_tile(x_hi, k)[:, 0:SEQ].bitcast(F32), ALU.subtract).then_inc(sm["lo"], 1)
                    tiles += 1

        def act_samples(act, k0):
            nc.scalar.activation(x3(x_hi)[:, k0:KD, SEQ:TOK], o_s[:, k0:KD, :], ACT.Copy).then_inc(samples_hi, 1)

        def dve_samples(dve, k0, times):
            dve.wait_ge(samples_hi, times)
            nc.vector.tensor_tensor(x3(x_lo)[:, k0:KD, SEQ:TOK], o_s[:, k0:KD, :],
                                    x3(x_hi)[:, k0:KD, SEQ:TOK].bitcast(F32), ALU.subtract)

        def mem_sems(name):
            return {k: sem(f"{name}_{k}") for k in
                    ("k_in0", "k_in1", "v_in", "q_ready", "turned", "kt_ready", "scored", "max_ready", "exp_done", "normed",
                     "p_turned", "pt_ready", "summed", "merged")}

        def pool_mem_loads(pool, l, M, sm):
            kv = w["cache_mem_kv"][l].rearrange("b (p s) c h d -> b p s (c h d)", s=2)
            for b in range(NB):
                if b == 2:
                    pool.memset(M["q"], 0.0).then_inc(sm["q_ready"], 1)
                if b >= 2:
                    pool.wait_ge(sm["turned"], b - 1)
                pool.dma_start(M["k"][:, b % 2, :, :], kv[b, :, :, 0:256]).then_inc(sm["k_in0" if b % 2 == 0 else "k_in1"], 16)
                pool.dma_start(M["v"][:, b, :, :], kv[b, :, :, 256:512]).then_inc(sm["v_in"], 16)

        def pe_mem(pe, M, sm):
            def score(b):
                pe.wait_ge(sm["kt_ready"], b + 1)
                if b == 0:
                    pe.wait_ge(sm["q_ready"], 2)
                for tt in range(2):
                    mm = nc.tensor.matmul(ps[:, 0, 0:MEM], M["q"][:, tt, b, :], M["kt"][:, b % 2, tt, :],
                                          start=b == 0 and tt == 0, stop=b == NB - 1 and tt == 1)
                mm.then_inc(sm["scored"], 1)

            for b in range(NB):
                pe.wait_ge(sm["k_in0" if b % 2 == 0 else "k_in1"], 16 * (b // 2 + 1))
                if b >= 2:
                    pe.wait_ge(sm["kt_ready"], b - 1)
                for tt in range(2):
                    for s in range(2):
                        mm = nc.tensor.transpose(ps[:, 4 + b % 2, (2 * tt + s) * P:(2 * tt + s + 1) * P],
                                                 M["k"][:, b % 2, s, tt * P:(tt + 1) * P], ident)
                mm.then_inc(sm["turned"], 1)
                if b >= 1:
                    score(b - 1)
            score(NB - 1)
            pe.wait_ge(sm["normed"], 1)
            for s in range(2):
                mm = nc.tensor.transpose(ps[:, 6, s * P:(s + 1) * P], M["p"][:, s * P:(s + 1) * P], ident)
            mm.then_inc(sm["p_turned"], 1)
            pe.wait_ge(sm["pt_ready"], 1)
            pe.wait_ge(sm["v_in"], 16 * NB)
            for x in range(2 * NB):
                b, tt = x // 2, x % 2
                product(ps[0:8, x // 4, x % 4 * P:(x % 4 + 1) * P],
                        [(M["pt"][:, s, 8 * x:8 * x + 8], M["v"][:, b, s, tt * P:(tt + 1) * P]) for s in range(2)],
                        sm["summed"] if x == 2 * NB - 1 else None)
            pe.wait_ge(sm["exp_done"], 2)
            pe.wait_ge(sm["normed"], 2)
            for x in range(2 * NB):
                mm = nc.tensor.transpose(ps[:, 7, 8 * x:8 * x + 8], M["sums"][:, x * P:(x + 1) * P], ident[0:8, 0:8])
            mm.then_inc(sm["p_turned"], 1)

        def act_mem(act, M, sm):
            for b in range(NB):
                act.wait_ge(sm["turned"], b + 1)
                if b >= 2:
                    act.wait_ge(sm["scored"], b - 1)
                nc.scalar.activation(M["kt"][:, b % 2, :, :], ps[:, 4 + b % 2, :].rearrange("p (t m) -> p t m", t=2),
                                     ACT.Copy).then_inc(sm["kt_ready"], 1)
            act.wait_ge(sm["max_ready"], 1)
            nc.scalar.activation(M["p"], ps[:, 0, 0:MEM], ACT.Exp, bias=stat[:, 17:18], scale=SCALE,
                                 accum_out=stat[:, 18:19]).then_inc(sm["exp_done"], 1)
            act.wait_ge(sm["summed"], 1)
            nc.scalar.activation(M["sums"][:, 0:8 * P].rearrange("p (b c) -> p b c", b=2), ps[0:8, 0:2, :],
                                 ACT.Copy).then_inc(sm["exp_done"], 1)

        def dve_mem(dve, M, sm):
            dve.wait_ge(sm["q_ready"], 1)
            for h in range(NG):
                e, tt = h % 2, h // 2
                dst = strided(M["q"][HD * e:HD * e + HD, tt, 0, 4 * h:4 * h + 1], (P + 16, NB), (1, DEC))
                c = nc.vector.tensor_copy(dst, M["qt"][HD * e:HD * e + HD, tt, SEQ:TOK].rearrange("p (b t) -> p b t", b=NB))
            c.then_inc(sm["q_ready"], 1)
            dve.wait_ge(sm["scored"], NB)
            c = dve_chain(nc.vector.reduce_max(stat[:, 16:17], ps[:, 0, 0:MEM], AX))
            dve.wait_ge(dve_step, c)
            nc.vector.tensor_scalar(stat[:, 17:18], stat[:, 16:17], -SCALE, None, ALU.mult).then_inc(sm["max_ready"], 1)
            dve.wait_ge(sm["exp_done"], 1)
            c = dve_chain(nc.vector.reciprocal(stat[:, 19:20], stat[:, 18:19]))
            dve.wait_ge(dve_step, c)
            nc.vector.tensor_scalar(M["p"], M["p"], stat[:, 19:20], None, ALU.mult).then_inc(sm["normed"], 1)
            dve.wait_ge(sm["p_turned"], 1)
            nc.vector.tensor_copy(M["pt"], ps[:, 6, 0:MEM].rearrange("p (s m) -> p s m", s=2)).then_inc(sm["pt_ready"], 1)
            dve.wait_ge(sm["summed"], 1)
            nc.vector.tensor_copy(M["sums"][:, 8 * P:16 * P].rearrange("p (b c) -> p b c", b=2),
                                  ps[0:8, 2:4, :]).then_inc(sm["normed"], 1)
            dve.wait_ge(sm["p_turned"], 2)
            for h in range(NG):
                e, tt = h % 2, h // 2
                src = strided(ps[HD * e:HD * e + HD, 7, 4 * h:4 * h + 1], (16, NB), (1, DEC))
                c = nc.vector.tensor_copy(o_s[HD * e:HD * e + HD, KA + tt, :].rearrange("p (b t) -> p b t", b=NB), src)
            c.then_inc(sm["merged"], 1)

        ws_in = sem("ws_in")
        ws_turned = sem("ws_turned")
        ws_copied = sem("ws_copied")
        ws_masked = sem("ws_masked")
        ws_repeated = sem("ws_repeated")
        wbd_ready = sem("wbd_ready")
        vt_turned = sem("vt_turned")
        vt_read = sem("vt_read")
        mixed = sem("mixed")
        mix_read = sem("mix_read")
        gated = sem("gated")
        gated_hi = sem("gated_hi")
        v_out = sem("v_out")
        u_free = sem("u_free")
        km_turned = sem("km_turned")
        km_read = sem("km_read")
        u_t = region(arena, 0, KA, TOK)
        v_t = region(arena, 3264, KA, TOK)
        qm_a = region(arena, 6528, 2, TOK)
        v_rows = region(arena, 7616, 5, AW)
        ws = region(arena, 15232, 4, P)
        wst = region(arena, 15744, 4, P)
        bsp = region(arena, 16256, 4, P)
        wbd = region(arena, 16768, 4, SAMP, parts=SAMP)
        km_a = region(arena, 16896, 2, MEM)
        MA = {"v": region(arena, 7616, NB, 2, 256), "k": region(arena, 0, 2, 2, 256), "kt": region(arena, 1024, 2, 2, MEM),
              "q": region(arena, 2048, 2, NB, P), "p": region(arena, 4096, 256), "pt": region(arena, 4352, 2, P), "qt": qm_a,
              "sums": region(arena, 0, 16 * P, parts=8)}
        pr_a, pt_a = region(arena, 4608, 4, 256), region(arena, 11712, 4, 256)
        mem_a, ua, samples_hi = mem_sems("mem_a"), unit_sems("ua"), sem("samples_hi")

        def group_parts(n):
            g = 2 * (n // 3)
            return [[(g, slice(0, P))], [(g, slice(0, HD)), (g + 1, slice(HD, P))], [(g + 1, slice(0, P))]][n % 3]

        def mem_units(qt, kt, rows, p, pt):
            return [{"q": qt[HD * e:HD * e + HD, tt, i * P:(i + 1) * P], "k": kt[HD * e:HD * e + HD, tt, :], "n": MEM,
                     "mask": None, "gate": None, "first": True, "last": True, "place": (e, i), "p": p, "pt": pt,
                     "closes": KA + tt if (i, e) == (NQT - 1, 1) else None,
                     "v": lambda c, h=2 * tt + e: rows[:, c, 256 + HD * h:256 + HD * h + HD]}
                    for tt in range(2) for i in range(NQT) for e in range(2)]

        units_a = mem_units(qm_a, km_a, mkv[:, 0, :, :], pr_a, pt_a)

        def pool_stage2(pool):
            pool.dma_start(ws[:, :, :], w["w_spatial"][0].rearrange("g t s -> t g s")).then_inc(ws_in, 16)
            bs = w["b_spatial"]
            pool.dma_start(bsp[:, :, :].rearrange("p g t -> p (g t)"),
                           bass.AP(bs.tensor, bs.offset, [[0, P], [1, 4 * P]])).then_inc(ws_in, 16)
            pool.wait_ge(*out_of(7))
            for l in range(2):
                pool.dma_start(o["mem_kv"][l].rearrange("(j p) x -> p j x", p=P), mkv[:, l, :, :]).then_inc(outputs, 16)
            pool.wait_ge(ws_copied, 1)
            for g in range(4):
                ins = nc.gpsimd.affine_select(out=wst[:, g, :], in_=wst[:, g, :], compare_op=ALU.is_ge, fill=0.0, base=0,
                                              pattern=[[1, P]], channel_multiplier=-1)
            ins.then_inc(ws_masked, 1)
            pool_clear_sums(pool, 0)
            for m in range(KA):
                pool_sums(pool, v_t[:, m, :], m % 2, *out_of(T_INA + KA + m), 0, m)
            pool.wait_ge(mean_ready, 1)
            for m in range(KA):
                nc.gpsimd.tensor_tensor(v_t[:, m, :], v_t[:, m, :], mean[:, :], ALU.subtract).then_inc(centred, 1)
            for n in range(KA):
                pool.wait_ge(mix_read, n + 1)
                nc.gpsimd.tensor_tensor(u_t[:, n, :], u_t[:, n, :], v_t[:, n, :], ALU.mult).then_inc(gated, 1)
            pool.wait_ge(u_free, 1)
            pool.wait_ge(v_out, 16)
            pool_mem_loads(pool, 0, MA, mem_a)
            pool.wait_ge(outputs, 32)
            meet(pool, 2)

        def pe_stage2(pe):
            pe_feature_slots(pe, W_INA, 2, T_INA)
            pe.wait_ge(ws_in, 32)
            for g in range(4):
                mm = nc.tensor.transpose(ps[:, 7, g * P:(g + 1) * P], ws[:, g, :], ident)
            mm.then_inc(ws_turned, 1)
            pe_feature_slots(pe, W_INA + 2, 5, T_INA + 4)
            pe.wait_ge(ws_masked, 1)
            for g in range(4):
                mm = nc.tensor.matmul(ps[0:SAMP, 6, 4 * g:4 * g + 4], cst[0:DEC, C_REP:C_REP + SAMP], wst[0:DEC, g, 0:DEC],
                                      start=True, stop=True)
            mm.then_inc(ws_repeated, 1)
            pe.wait_ge(wbd_ready, 1)
            pe_ln(pe, 0)
            pe.wait_ge(v_normed, KA)
            for n in range(10):
                j, part = n // 2, n % 2
                m = P if j < 4 else SAMP
                if n >= 4:
                    pe.wait_ge(vt_read, n - 3)
                for x in range(4 * part, min(4 * part + 4, KA)):
                    mm = nc.tensor.transpose(ps[0:m, 4 + n % 4, (x % 4) * P:(x % 4 + 1) * P],
                                             v_t[:, x, j * P:j * P + m], ident)
                mm.then_inc(vt_turned, 1)
            pe.wait_ge(vt_read, 10)
            pe.wait_ge(*out_of(T_OUTA - 1))
            for n in range(KA):
                if n >= 2:
                    pe.wait_ge(mix_read, n - 1)
                for g, pp in group_parts(n):
                    cols = slice(n * P + pp.start, n * P + pp.stop)
                    for j in range(NQT):
                        nc.tensor.matmul(ps[pp, 2 * (n % 2), j * P:(j + 1) * P], v_rows[:, j, cols], wst[:, g, :],
                                         start=True, stop=True)
                    mm = nc.tensor.matmul(ps[pp, 2 * (n % 2) + 1, 0:SAMP], v_rows[0:SAMP, 4, cols], wbd[:, g, :],
                                          start=True, stop=True)
                mm.then_inc(mixed, 1)
            for j in range(2):
                for tt in range(2):
                    mm = nc.tensor.transpose(ps[:, 7, tt * MEM + j * P:tt * MEM + (j + 1) * P],
                                             mkv[:, 0, j, tt * P:(tt + 1) * P], ident)
            mm.then_inc(km_turned, 1)
            pe.wait_ge(mix_read, KA)
            pe.wait_ge(km_read, 1)
            pe_units(pe, units_a, ua)
            pe.wait_ge(ua["lo"], 2)
            pe_mem(pe, MA, mem_a)
            meet(pe, 2)

        def act_stage2(act):
            for s in range(W_INA, W_INA + 7):
                act_split(act, s + 1)
                for n in range(2):
                    t = T_INA + 2 * (s - W_INA) + n
                    x = t - T_INA
                    act.wait_ge(tile_done, t + 1)
                    dst = (u_t[:, x, :] if x < KA else v_t[:, x - KA, :] if x < 2 * KA else qm_a[:, x - 2 * KA, :])
                    nc.scalar.activation(halves(dst), pair(t), ACT.Gelu_apprx_tanh if x < 2 * KA else ACT.Copy).then_inc(read_act, 1)
                    if KA <= x < 2 * KA:
                        act_square(act, v_t[:, x - KA, :], x % 2, *out_of(t), 0, x - KA)
            act_ln_stats(act, AW)
            for m in range(KA):
                act.wait_ge(scaled, m + 1)
                nc.scalar.activation(v_t[:, m, :], v_t[:, m, :], ACT.Identity,
                                     bias=lnp[:, 70 + m:71 + m]).then_inc(v_normed, 1)
            for n in range(KA):
                act.wait_ge(gated, n + 1)
                nc.scalar.activation(x_tile(x_hi, n), u_t[:, n, :], ACT.Copy).then_inc(gated_hi, 1)
            act_units(act, units_a, ua)
            act_mem(act, MA, mem_a)
            act.wait_ge(mem_a["merged"], 1)
            act_samples(act, KA)
            meet(act, 2)

        def dve_stage2(dve):
            for s in range(W_INA, W_INA + 2):
                dve_split(dve, s + 1)
            dve.wait_ge(ws_turned, 1)
            nc.vector.tensor_copy(wst[:, :, :], ps[:, 7, :].rearrange("p (g t) -> p g t", g=4)).then_inc(ws_copied, 1)
            for s in range(W_INA + 2, W_INA + 7):
                dve_split(dve, s + 1)
            dve.wait_ge(ws_repeated, 1)
            for g in range(4):
                ins = nc.vector.tensor_tensor(wbd[:, g, :].rearrange("p (b t) -> p b t", b=NB),
                                              strided(ps[0:SAMP, 6, 4 * g:4 * g + 1], (0, NB), (1, DEC)),
                                              strided(cst[0:SAMP, C_BD:C_BD + 1], (1, NB), (0, DEC)), ALU.mult)
            ins.then_inc(wbd_ready, 1)
            dve_ln_stats(dve, AW)
            for m in range(KA):
                dve.wait_ge(centred, m + 1)
                nc.vector.scalar_tensor_tensor(out=v_t[:, m, :], in0=v_t[:, m, :], scalar=lnp[:, 64 + m:65 + m],
                                               in1=rstd[:, :], op0=ALU.mult, op1=ALU.mult).then_inc(scaled, 1)
            for n in range(10):
                j, part = n // 2, n % 2
                m = P if j < 4 else SAMP
                dve.wait_ge(vt_turned, n + 1)
                width = 512 if part == 0 else AW - 512
                nc.vector.tensor_copy(v_rows[0:m, j, 512 * part:512 * part + width],
                                      ps[0:m, 4 + n % 4, 0:width]).then_inc(vt_read, 1)

            def gated_lo(n):
                dve.wait_ge(gated_hi, n + 1)
                return nc.vector.tensor_tensor(x_tile(x_lo, n), u_t[:, n, :], x_tile(x_hi, n).bitcast(F32), ALU.subtract)

            for n in range(KA):
                dve.wait_ge(mixed, n + 1)
                for g, pp in group_parts(n):
                    nc.vector.tensor_tensor(v_t[pp, n, 0:SEQ].rearrange("p (j t) -> p j t", j=NQT),
                                            ps[pp, 2 * (n % 2), :].rearrange("p (j t) -> p j t", j=NQT),
                                            strided(bsp[pp, g, 0:1], (0, NQT), (1, P)), ALU.add)
                    ins = nc.vector.tensor_tensor(v_t[pp, n, SEQ:TOK].rearrange("p (b t) -> p b t", b=NB),
                                                  ps[pp, 2 * (n % 2) + 1, 0:SAMP].rearrange("p (b t) -> p b t", b=NB),
                                                  strided(bsp[pp, g, 0:1], (0, NB), (1, DEC)), ALU.add)
                ins.then_inc(mix_read, 1)
                if n >= 2:
                    gated_lo(n - 2)
            dve.wait_ge(km_turned, 1)
            nc.vector.tensor_copy(km_a[:, :, :], ps[:, 7, :].rearrange("p (t m) -> p t m", t=2)).then_inc(km_read, 1)
            for n in (KA - 2, KA - 1):
                ins = gated_lo(n)
            ins.then_inc(u_free, 1)
            dve_units(dve, units_a, ua)
            dve_mem(dve, MA, mem_a)
            dve_samples(dve, KA, 1)
            meet(dve, 2)

        def sp_stage2(sp):
            sp.wait_ge(vt_read, 10)
            sp.dma_start(o["gmlp_v"][0].rearrange("b t c -> (b t) c"), v_rows[0:SAMP, 4, :]).then_inc(v_out, 16)

        def pe_out(pe, l):
            pe_feature_slots(pe, W_OUTA if l == 0 else W_OUTB, 4, T_OUTA if l == 0 else T_OUTB)
            pe_ln(pe, 2 * l + 1)

        def act_out(act, l):
            s0, t0 = (W_OUTA, T_OUTA) if l == 0 else (W_OUTB, T_OUTB)
            for s in range(s0, s0 + 4):
                act_split(act, s + 1)
                for n in range(2):
                    m = 2 * (s - s0) + n
                    act_square(act, resid[:, m, :], m % 2, *out_of(t0 + m), 2 * l + 1, m)
            act_split(act, MLP_W[l] + 1)
            act_ln(act, 2 * l)

        def dve_out(dve, l):
            s0, t0 = (W_OUTA, T_OUTA) if l == 0 else (W_OUTB, T_OUTB)
            for s in range(s0, s0 + 4):
                dve_split(dve, s + 1)
                for n in range(2):
                    m = 2 * (s - s0) + n
                    dve.wait_ge(tile_done, t0 + m + 1)
                    if l:
                        dve.wait_ge(ln_whole, KD * 2)
                    nc.vector.scalar_tensor_tensor(out=halves(resid[:, m, :]), in0=halves(resid[:, m, :]), scalar=ALPHA,
                                                   in1=pair(t0 + m), op0=ALU.mult, op1=ALU.add).then_inc(read_dve, 1)
            dve_split(dve, MLP_W[l] + 1)
            dve_ln(dve, 2 * l)

        def pool_out(pool, l):
            t0 = T_OUTA if l == 0 else T_OUTB
            pool_clear_sums(pool, 2 * l + 1)
            for m in range(KD):
                pool_sums(pool, resid[:, m, :], m % 2, *out_of(t0 + m), 2 * l + 1, m)
            pool_ln(pool, 2 * l)

        roped = sem("roped")
        kv_out = [sem("kv_out_even"), sem("kv_out_odd")]
        heads_turned = sem("heads_turned")
        heads_read = sem("heads_read")
        gates_ready = sem("gates_ready")
        gates_out = sem("gates_out")
        gates_in = sem("gates_in")
        q_bd_clear = sem("q_bd_clear")
        q_rows = region(arena, 0, 5, AW)
        k_rows = region(arena, 3840, 2, 5, 256)
        v_bank = region(arena, 6400, 5, 2, 256)
        gm = region(arena, 8960, 5, 292)
        q_t = region(arena, 10432, KA, TOK)
        qm_b = region(arena, 13696, 2, TOK)
        k_t = region(arena, 14784, 2, 2, TOK)
        gs = region(arena, 16960, NB, 3, parts=QROWS)

        def q_place(head):
            g, r = divmod(head, GQ)
            return (g // 2 * GQ + r) * 2 + g % 2

        Q_RUNS = [[(0, 3), (3, 1)], [(4, 2), (6, 2)], [(8, 1), (9, 3)]]

        def x_tok(t):
            return lambda k, j: t[:, k * TOK + j * P:k * TOK + (j + 1) * P]

        def rope(dve, v, pitch, heads):
            n = 5 * heads * 8
            a, b = (strided(v[:, 0, c:c + 1], (pitch, 5), (HD, heads), (1, 8)) for c in (0, 8))
            cos, sin = (strided(cst[:, c:c + 1], (8, 5), (0, heads), (1, 8)) for c in (C_COS, C_SIN))
            t = [x[:, i, 0:n].rearrange("p (j h x) -> p j h x", j=5, h=heads) for x in (tmp, sq) for i in range(2)]
            nc.vector.tensor_tensor(t[0], a, cos, ALU.mult)
            nc.vector.tensor_tensor(t[1], b, sin, ALU.mult)
            nc.vector.tensor_tensor(t[2], b, cos, ALU.mult)
            c = dve_chain(nc.vector.tensor_tensor(t[3], a, sin, ALU.mult))
            dve.wait_ge(dve_step, c)
            nc.vector.tensor_tensor(a, t[0], t[1], ALU.subtract)
            nc.vector.tensor_tensor(b, t[2], t[3], ALU.add).then_inc(roped, 1)
            rope_count[0] += 1
            dve.wait_ge(roped, rope_count[0])

        rope_count = [0]

        def turn_list():
            def key_groups(br, buf):
                gr = [[(k_rows[:, buf, j, pr * P:(pr + 1) * P], P, j * P) for j in range(NQT)] for pr in range(2)]
                return gr + [[(k_rows[0:SAMP, buf, NQT, pr * P:(pr + 1) * P], SAMP, pr * SAMP) for pr in range(2)]]

            q = [[(q_rows[:, j, x * P:(x + 1) * P], P, j * P) for j in range(NQT)] for x in range(KA)]
            q += [[(q_rows[0:SAMP, NQT, x * P:(x + 1) * P], SAMP, x * SAMP) for x in range(KA)]]
            m = [[(gm[:, j, 36 + tt * P:36 + (tt + 1) * P], P, j * P) for j in range(NQT)] for tt in range(2)]
            m += [[(gm[0:SAMP, NQT, 36 + tt * P:36 + (tt + 1) * P], SAMP, tt * SAMP) for tt in range(2)]]
            return [key_groups(1, 0), key_groups(2, 1), q, m]

        TURNS = turn_list()

        def turn_base(x):
            return sum(len(g) for g in TURNS[:x])

        def pe_turn(pe, x):
            for i, group in enumerate(TURNS[x]):
                n = turn_base(x) + i
                if n >= 4:
                    pe.wait_ge(heads_read, n - 3)
                for src, m, c in group:
                    mm = nc.tensor.transpose(ps[:, 4 + n % 4, c:c + m], src, ident[0:m, 0:m])
                mm.then_inc(heads_turned, 1)

        def act_turned(act, x, dsts):
            for i, (dst, cols) in enumerate(dsts):
                n = turn_base(x) + i
                act.wait_ge(heads_turned, n + 1)
                src = ps[:, 4 + n % 4, 0:cols]
                if len(dst.shape) == 3:
                    src = src.rearrange("p (a t) -> p a t", t=SAMP)
                nc.scalar.activation(dst, src, ACT.Copy).then_inc(heads_read, 1)

        def key_dsts(br):
            return [(k_t[:, br - 1, pr, 0:SEQ], SEQ) for pr in range(2)] + [(k_t[:, br - 1, :, SEQ:TOK], 2 * SAMP)]

        def pe_stage3(pe):
            for c in range(6):
                pe_token_slot(pe, W_KV + c, T_KV + 5 * c, 5, x_tok(x_hi), x_tok(x_lo), 256, KD if c == 0 else None)
                if c == 3:
                    pe.wait_ge(roped, 2)
                    pe_turn(pe, 0)
            for c in range(5):
                pe_token_slot(pe, W_INB + c, T_INB + 5 * c, 5, x_tok(x_hi), x_tok(x_lo), IN_B[c][1])
                if c == 0:
                    pe.wait_ge(roped, 3)
                    pe_turn(pe, 1)
            pe.wait_ge(roped, 4)
            pe_turn(pe, 2)
            pe_turn(pe, 3)
            meet(pe, 3)

        def act_stage3(act):
            for c in range(6):
                if c:
                    act_split(act, W_KV + c + 1)
                if c in (2, 4):
                    act.wait_ge(kv_out[0 if c == 2 else 1], 32)
                for j in range(5):
                    t = T_KV + 5 * c + j
                    act.wait_ge(tile_done, t + 1)
                    dst = v_bank[:, j, c // 2 - 1, :] if c in (3, 5) else k_rows[:, {0: 0, 1: 1, 2: 0, 4: 1}[c], j, :]
                    nc.scalar.activation(dst, ps[:, 2 * (t % 2), 0:256], ACT.Copy).then_inc(read_act, 1)
                if c == 3:
                    act_turned(act, 0, key_dsts(1))
            for c in range(5):
                if c < 4:
                    act_split(act, W_INB + c + 1)
                for j in range(5):
                    t = T_INB + 5 * c + j
                    act.wait_ge(tile_done, t + 1)
                    if c < 3:
                        for first, n in Q_RUNS[c]:
                            to, at = q_place(first), 64 * (first - 4 * c)
                            ins = nc.scalar.activation(strided(q_rows[:, j, to * HD:to * HD + 1], (2 * HD, n), (1, HD)),
                                                       ps[:, 2 * (t % 2), at:at + n * HD].rearrange("p (h d) -> p h d", d=HD),
                                                       ACT.Copy)
                    else:
                        ins = nc.scalar.activation(gm[:, j, 146 * (c - 3):146 * (c - 2)], ps[:, 2 * (t % 2), 0:146], ACT.Copy)
                    ins.then_inc(read_act, 1)
                if c == 0:
                    act_turned(act, 1, key_dsts(2))
                if c == 3:
                    act.wait_ge(*out_of(T_INB + 19))
                    nc.scalar.activation(gm[:, :, 0:36], gm[:, :, 0:36], ACT.Sigmoid).then_inc(gates_ready, 1)
            act_turned(act, 2, [(q_t[:, x, 0:SEQ], SEQ) for x in range(KA)] + [(q_t[:, :, SEQ:TOK], KA * SAMP)])
            act_turned(act, 3, [(qm_b[:, x, 0:SEQ], SEQ) for x in range(2)] + [(qm_b[:, :, SEQ:TOK], 2 * SAMP)])
            meet(act, 3)

        def dve_stage3(dve):
            for c in range(6):
                if c:
                    dve_split(dve, W_KV + c + 1)
                if c % 2 == 0:
                    dve.wait_ge(*out_of(T_KV + 5 * c + 4))
                    rope(dve, k_rows[:, {0: 0, 2: 0, 4: 1}[c], :, :], 256, NG)
            for c in range(4):
                dve_split(dve, W_INB + c + 1)
                if c == 2:
                    dve.wait_ge(*out_of(T_INB + 14))
                    rope(dve, q_rows, AW, NH)
            dve.wait_ge(heads_read, turn_base(2) + KA + 1)
            dve.wait_ge(q_bd_clear, 1)
            for g in range(NG):
                e, pr = g % 2, g // 2
                src = strided(q_t[HD * e:HD * e + HD, pr * GQ, SEQ:SEQ + 1], (DEC, NB), (TOK, GQ), (1, DEC))
                dst = strided(q_bd[HD * e:HD * e + HD, pr, 0, 12 * g:12 * g + 1], (QROWS, NB), (DEC, GQ), (1, DEC))
                nc.vector.tensor_copy(dst, src)
            meet(dve, 3)

        def pool_stage3(pool):
            nc.gpsimd.memset(q_bd[:, :, :, :], 0.0).then_inc(q_bd_clear, 1)
            names = ("cmp", "slc", "win")
            for c in range(6):
                br, kv = c // 2, c % 2
                if kv == 0:
                    pool.wait_ge(roped, br + 1)
                else:
                    pool.wait_ge(*out_of(T_KV + 5 * c + 4))
                src = v_bank[:, :, br - 1, :] if c in (3, 5) else k_rows[:, {0: 0, 1: 1, 2: 0, 4: 1}[c], :, :]
                done = kv_out[c] if c < 2 else outputs
                pool.dma_start(o[names[br] + "_p"].rearrange("(j p) v x -> v p j x", p=P)[kv], src[:, 0:4, :]).then_inc(done, 16)
                if br < 2:
                    dst = o[names[br] + "_s"][:, kv, :]
                    pool.dma_start(dst, src[0:SAMP, NQT, :]).then_inc(done, 16)
                else:
                    for b in range(NB):
                        pool.dma_start(o["win_s"][b, 512 - DEC:512, kv, :], src[DEC * b:DEC * b + DEC, NQT, :]).then_inc(outputs, 16)
            pool.wait_ge(gates_ready, 1)
            pool.dma_start(scratch, gm[0:SAMP, NQT, 0:36]).then_inc(gates_out, 16)
            pool.wait_ge(gates_out, 16)
            for b in range(NB):
                src = bass.AP(scratch.tensor, scratch.offset + DEC * 36 * b, [[3, NH], [36, DEC], [1, 3]])
                pool.dma_start(gs[:, b, :], src).then_inc(gates_in, 16)
            meet(pool, 3)

        OUT_STAGE3 = 16 * (2 * 2 + 2 * (1 + NB))

        MB = {"v": region(xalt, 0, NB, 2, 256), "k": region(xalt, 4096, 2, 2, 256), "kt": region(xalt, 5120, 2, 2, MEM),
              "q": region(xalt, 6144, 2, NB, P), "p": region(xalt, 8192, 256), "pt": region(xalt, 8448, 2, P), "qt": qm_b,
              "sums": region(xalt, 4096, 16 * P, parts=8)}
        mem_b, ub = mem_sems("mem_b"), unit_sems("ub")
        phi1_b = region(arena, 0, 16, 2, P)
        xc_b = region(arena, 4096, 2, 8, P)
        gel_b = region(arena, 6144, 2, P)
        cmp_p_in = sem("cmp_p_in")
        small = {}
        at = 4096
        for name, parts, dims in (("pc", QROWS, (NB, 64)), ("pct", 64, (NB, QROWS)), ("pgt", 64, (NB, QROWS)),
                                  ("imp", QROWS, (NB, 14)), ("eq", QROWS, (NB, 14)), ("bias", QROWS, (NB, 16)), ("bx", QROWS, (P,)),
                                  ("snew", QROWS, (2, NB, DEC)), ("mx", QROWS, (NB, 2, 3)), ("st", QROWS, (4, NB))):
            small[name] = region(arena, at, *dims, parts=parts)
            at += int(np.prod(dims))
        assert at <= 6400
        c_scored, c_centred, c_exp, c_normed = (sem(f"c_{x}") for x in ("scored", "centred", "exp", "normed"))
        c_turned, c_copied, c_gated, c_imp, c_imp_read, c_imp2, c_done = (
            sem(f"c_{x}") for x in ("turned", "copied", "gated", "imp", "imp_read", "imp2", "done"))
        slc_in = [sem("slc_in_0"), sem("slc_in_1"), sem("slc_in_2")]
        win_in = [sem("win_in_even"), sem("win_in_odd")]
        s_turned, s_read_a, s_read_d, s_scored, s_max, s_exp, s_normed, s_pturned, s_pt, s_summed, s_moved, s_sum_turned, s_out = (
            sem(f"s_{x}") for x in ("turned", "read_act", "read_dve", "scored", "max", "exp", "normed", "pturned", "pt",
                                    "summed", "moved", "sum_turned", "out"))
        slc_places = [w_raw[:, :, :].rearrange("p a c -> p (a c)"), xalt[:, 0:4096], xalt[:, 4096:8192]]
        slc = [x.rearrange("p (s x) -> p s x", s=8) for x in slc_places]
        win = region(arena, 0, 2, 4, 512)
        kts = region(walt, 0, 2, 1024)
        ktw = region(walt, 2048, 2, 512)
        p_sel = region(walt, 3072, 1024, parts=QROWS)
        p_win = region(walt, 4096, 512, parts=QROWS)
        p_new = region(walt, 4608, 2, SAMP, parts=QROWS)
        pt_s = region(walt, 4672, 12, QROWS)
        pt_n = region(walt, 5248, 2, QROWS, parts=SAMP)
        mkv_b = region(walt, 6144, 2, 512)
        km_b = region(walt, 7168, 2, MEM)
        sums_s = region(walt, 5376, 2, 256, parts=24)
        mkv_b_in = sem("mkv_b_in")
        km_b_turned = sem("km_b_turned")
        km_b_read = sem("km_b_read")
        pr_b, pt_b = region(arena, 0, 4, 512), region(arena, 2048, 4, 512)

        def nsa_units():
            us = []
            for k in range(KA):
                pr, r = k // GQ, k % GQ
                for i in range(NQT):
                    for e in range(2):
                        half, g = slice(HD * e, HD * e + HD), 2 * pr + e
                        hd, vcols = g * GQ + r, slice(HD * g, HD * g + HD)
                        for br in range(3):
                            gate = gm[:, i, 3 * hd + br:3 * hd + br + 1]
                            u = {"q": q_t[half, k, i * P:(i + 1) * P], "p": pr_b, "pt": pt_b, "place": (e, i),
                                 "first": br == 0, "last": br == 2, "closes": k if (i, e, br) == (NQT - 1, 1, 2) else None}
                            if br == 0:
                                u.update(n=32, k=kc_p[half, pr, :], mask=cst[:, C_CMP + 32 * i:C_CMP + 32 * i + 32],
                                         gate=gate,
                                         v=lambda c, vc=vcols: vc_p[:, vc])
                            else:
                                n = P * (i + 1)
                                u.update(n=n, k=k_t[half, br - 1, pr, 0:n],
                                         mask=cst[:, C_CAUS + 512 - n:C_CAUS + 512], gate=gate,
                                         v=lambda c, vc=vcols, br=br: v_bank[:, c, br - 1, vc])
                            us.append(u)
            return us + mem_units(qm_b, km_b, mkv_b, pr_b, pt_b)

        units_b = nsa_units()
        slc_rows = w["cache_slc_kv"].rearrange("n (a s) c h d -> (n a) (s c h d)", s=8)

        def pool_stage4(pool):
            def slc_load(b):
                nc.gpsimd.indirect_dma_start(slc_places[b % 3], None, slc_rows,
                                             bass.IndirectOffsetOnAxis(rows_s[:, b:b + 1], 0)).then_inc(slc_in[b % 3], 16)

            pool_mem_loads(pool, 1, MB, mem_b)
            src = o["cmp_p"].rearrange("(n s) v x -> n (s v x)", s=STRIDE)
            pool.dma_start(walt[0:32, 0:STRIDE * ROW], src).then_inc(cmp_p_in, 16)
            load_phi1(pool, phi1_b, phi1_b_in)
            slc_load(0)
            pool.wait_ge(turned, 80)
            pool.dma_start(mkv_b[:, :, :], o["mem_kv"][1].rearrange("(j p) x -> p j x", p=P)).then_inc(mkv_b_in, 16)
            pool.wait_ge(blocks, 5)
            pool.wait_ge(mem_b["merged"], 1)
            for b in range(NB):
                if b >= 3:
                    pool.wait_ge(s_summed, b - 2)
                if b >= 1:
                    slc_load(b)
                if b >= 2:
                    pool.wait_ge(s_summed, b - 1)
                pool.dma_start(win[:, b % 2, :, :], w["cache_win_kv"][b].rearrange("(p s) c h d -> p s (c h d)", s=4)
                               ).then_inc(win_in[b % 2], 16)
            meet(pool, 4)
            meet(pool, 5)

        def pe_stage4(pe):
            pe_mem(pe, MB, mem_b)
            pe.wait_ge(cmp_p_in, 16)
            pe_compress_turn(pe, walt, 64, 32, 64)
            pe.wait_ge(phi1_b_in, PHI1_ONCE)
            pe_compress_hidden(pe, 4, xc_b, phi1_b, 64, 1, 32)
            pe_compress_out(pe, 4, gel_b, 1, 32)
            pe.wait_ge(mkv_b_in, 16)
            pe.wait_ge(turned_dve, 40)
            pe.wait_ge(mem_b["merged"], 1)
            for j in range(2):
                for tt in range(2):
                    mm = nc.tensor.transpose(ps[:, 2, tt * MEM + j * P:tt * MEM + (j + 1) * P],
                                             mkv_b[:, j, tt * P:(tt + 1) * P], ident)
            mm.then_inc(km_b_turned, 1)
            pe.wait_ge(km_b_read, 1)
            pe.wait_ge(blocks_read, 5)
            for b in range(NB):
                product(ps[0:QROWS, 0, 64 * b:64 * b + NCS], [(q_bd[:, pr, b, :], kc_s[:, b, pr, 0:NCS]) for pr in range(2)])
            for br in range(2):
                for b in range(NB):
                    c = (br * NB + b) * DEC
                    product(ps[0:QROWS, 1, c:c + DEC],
                            [(q_bd[:, pr, b, :], k_t[:, br, pr, SEQ + DEC * b:SEQ + DEC * b + DEC]) for pr in range(2)],
                            c_scored if br == 1 and b == NB - 1 else None)
            pe.wait_ge(c_normed, 1)
            for b in range(NB):
                mm = nc.tensor.transpose(ps[0:NCS, 4, QROWS * b:QROWS * b + QROWS], small["pc"][:, b, 0:NCS],
                                         ident[0:QROWS, 0:QROWS])
            mm.then_inc(c_turned, 1)
            pe.wait_ge(c_copied, 1)
            for b in range(NB):
                mm = nc.tensor.matmul(ps[0:QROWS, 2, 14 * b:14 * b + 14], small["pct"][0:NCS, b, :],
                                      cst[0:NCS, C_OV:C_OV + 14], start=True, stop=True)
            mm.then_inc(c_imp, 1)
            pe.wait_ge(c_gated, 1)
            for b in range(NB):
                mm = nc.tensor.transpose(ps[0:NCS, 5, QROWS * b:QROWS * b + QROWS], small["pc"][:, b, 0:NCS],
                                         ident[0:QROWS, 0:QROWS])
            mm.then_inc(c_turned, 1)
            pe.wait_ge(c_imp_read, 1)
            nc.tensor.matmul(ps[0:QROWS, 3, 0:14 * NB], cst[0:QROWS, C_SUMR:C_SUMR + QROWS],
                             small["imp"].rearrange("p b j -> p (b j)"), start=True, stop=True).then_inc(c_imp2, 1)

            def turn_keys(b):
                if b == NB:
                    return
                pe.wait_ge(slc_in[b % 3], 16 * (b // 3 + 1))
                pe.wait_ge(win_in[b % 2], 16 * (b // 2 + 1))
                for x in range(6):
                    n = s_group(b, x)
                    bank_wait(n)
                    for s in range(4):
                        src = slc[b % 3][:, 4 * (x % 2) + s, :] if x < 4 else win[:, b % 2, s, :]
                        pr = x // 2 if x < 4 else x - 4
                        mm = nc.tensor.transpose(ps[:, 4 + n % 3, s * P:(s + 1) * P], src[:, pr * P:(pr + 1) * P], ident)
                    mm.then_inc(s_turned, 1)

            def bank_wait(n):
                if n >= 3:
                    reader, v = s_reader(n - 3)
                    pe.wait_ge(s_read_a if reader == "act" else s_read_d, v)

            def score(b):
                if b >= 1:
                    pe.wait_ge(s_exp, 2 * b)
                pe.wait_ge(s_read_a, s_group(b, 4) // 2 + 1)
                pe.wait_ge(s_read_d, s_group(b, 5) // 2 + 1)
                product(ps[0:QROWS, 2, :], [(q_bd[:, pr, b, :], ktw[:, pr, :]) for pr in range(2)], s_scored)
                for x in range(2):
                    product(ps[0:QROWS, x, :], [(q_bd[:, pr, b, :], kts[:, pr, 512 * x:512 * x + 512]) for pr in range(2)],
                            s_scored if x else None)

            def turn_probs(b):
                pe.wait_ge(s_normed, b + 1)
                n = s_group(b, 6)
                bank_wait(n)
                for s in range(8):
                    mm = nc.tensor.transpose(ps[:, 4 + n % 3, QROWS * s:QROWS * s + QROWS],
                                             p_sel[:, s * P:(s + 1) * P], ident[0:QROWS, 0:QROWS])
                mm.then_inc(s_turned, 1)
                bank_wait(n + 1)
                for s in range(4):
                    nc.tensor.transpose(ps[:, 4 + (n + 1) % 3, QROWS * s:QROWS * s + QROWS], p_win[:, s * P:(s + 1) * P],
                                        ident[0:QROWS, 0:QROWS])
                for br in range(2):
                    mm = nc.tensor.transpose(ps[0:SAMP, 4 + (n + 1) % 3, QROWS * (4 + br):QROWS * (5 + br)],
                                             p_new[:, br, :], ident[0:QROWS, 0:QROWS])
                mm.then_inc(s_turned, 1)

            def values(b):
                pe.wait_ge(s_read_a, s_group(b, 6) // 2 + 1)
                pe.wait_ge(s_read_d, s_group(b, 7) // 2 + 1)
                for pr in range(2):
                    c, vc = 24 * pr, slice(256 + P * pr, 256 + P * pr + P)
                    terms = [(pt_s[:, s, c:c + 24], slc[b % 3][:, s, vc]) for s in range(8)]
                    terms += [(pt_s[:, 8 + s, c:c + 24], win[:, b % 2, s, vc]) for s in range(4)]
                    terms += [(small["pgt"][0:NCS, b, c:c + 24], vc_s[0:NCS, b, P * pr:P * pr + P])]
                    terms += [(pt_n[:, br, c:c + 24], v_bank[0:SAMP, NQT, br, P * pr:P * pr + P]) for br in range(2)]
                    at = 256 * (b % 2) + P * pr
                    product(ps[0:24, 7, at:at + P], terms, s_summed if pr else None)

            def turn_sums(b):
                pe.wait_ge(s_moved, b + 1)
                for pr in range(2):
                    c = QROWS * b + 24 * pr
                    mm = nc.tensor.transpose(ps[:, 3, c:c + 24], sums_s[:, b % 2, P * pr:P * pr + P], ident[0:24, 0:24])
                mm.then_inc(s_sum_turned, 1)

            pe.wait_ge(c_copied, 2)
            turn_keys(0)
            pe.wait_ge(c_done, 1)
            for b in range(NB):
                score(b)
                if b >= 1:
                    turn_sums(b - 1)
                turn_keys(b + 1)
                turn_probs(b)
                values(b)
            turn_sums(NB - 1)
            pe.wait_ge(s_out, 1)
            meet(pe, 4)
            pe_units(pe, units_b, ub)
            meet(pe, 5)

        def s_group(b, x):
            if x < 6:
                return max(8 * b - 2, 0) + x
            return 8 * b + x + (6 if b < NB - 1 else 0)

        def s_reader(n):
            return ("act", n // 2 + 1) if n % 2 == 0 else ("dve", n // 2 + 1)

        def s_copy(eng, who, b, xs):
            for x in xs:
                if b == NB:
                    return
                n = s_group(b, x)
                if s_reader(n)[0] != who:
                    continue
                eng.wait_ge(s_turned, n + 1)
                bank = ps[:, 4 + n % 3, :]
                if x < 4:
                    moves = [(kts[:, x // 2, 512 * (x % 2):512 * (x % 2) + 512], bank)]
                elif x < 6:
                    moves = [(ktw[:, x - 4, :], bank)]
                elif x == 6:
                    moves = [(pt_s[:, 0:8, :], bank[:, 0:8 * QROWS].rearrange("p (s m) -> p s m", m=QROWS))]
                else:
                    moves = [(pt_s[:, 8:12, :], bank[:, 0:4 * QROWS].rearrange("p (s m) -> p s m", m=QROWS)),
                             (pt_n[:, :, :], bank[0:SAMP, 4 * QROWS:6 * QROWS].rearrange("p (s m) -> p s m", m=QROWS))]
                for dst, src in moves:
                    ins = nc.scalar.activation(dst, src, ACT.Copy) if who == "act" else nc.vector.tensor_copy(dst, src)
                ins.then_inc(s_read_a if who == "act" else s_read_d, 1)

        def act_stage4(act):
            act_mem(act, MB, mem_b)
            compress_copy(act, "act", xc_b, 64, 32, None)
            act_compress_gelu(act, 4, gel_b, P)
            act.wait_ge(c_centred, 1)
            nc.scalar.activation(small["pc"][:, :, 0:NCS], small["pc"][:, :, 0:NCS], ACT.Exp, scale=SCALE).then_inc(c_exp, 1)
            def move_sums(b):
                act.wait_ge(s_summed, b + 1)
                if b >= 2:
                    act.wait_ge(s_sum_turned, b - 1)
                nc.scalar.activation(sums_s[:, b % 2, :], ps[0:24, 7, 256 * (b % 2):256 * (b % 2) + 256],
                                     ACT.Copy).then_inc(s_moved, 1)

            s_copy(act, "act", 0, range(6))
            for b in range(NB):
                if b >= 1:
                    move_sums(b - 1)
                act.wait_ge(s_max, 2 * b + 1)
                nm, sm = stat[0:QROWS, 38:40], stat[0:QROWS, 40:44]
                nc.scalar.activation(p_win, ps[0:QROWS, 2, :], ACT.Exp, bias=nm[:, 1:2], scale=SCALE, accum_out=sm[:, 1:2])
                nc.scalar.activation(small["snew"][:, 1, b, :], small["snew"][:, 1, b, :], ACT.Exp,
                                     bias=nm[:, 1:2], scale=SCALE, accum_out=sm[:, 3:4]).then_inc(s_exp, 1)
                act.wait_ge(s_scored, 2 * b + 2)
                s_copy(act, "act", b + 1, range(1))
                act.wait_ge(s_max, 2 * b + 2)
                nc.scalar.activation(p_sel.rearrange("p (a x) -> p a x", a=2), ps[0:QROWS, 0:2, :], ACT.Exp, bias=nm[:, 0:1],
                                     scale=SCALE, accum_out=sm[:, 0:1])
                nc.scalar.activation(small["snew"][:, 0, b, :], small["snew"][:, 0, b, :], ACT.Exp,
                                     bias=nm[:, 0:1], scale=SCALE, accum_out=sm[:, 2:3]).then_inc(s_exp, 1)
                s_copy(act, "act", b + 1, range(1, 3))
                s_copy(act, "act", b + 1, range(3, 6))
                s_copy(act, "act", b, range(6, 8))
            move_sums(NB - 1)
            act_split(act, W_OUTB)
            meet(act, 4)
            act_units(act, units_b, ub)
            act_samples(act, 0)
            meet(act, 5)

        def bcast(ap, n):
            return strided(ap[:, 0:1], (ap.ap[1][0], NB), (0, n))

        def dve_stage4(dve):
            def chained(ins):
                c = dve_chain(ins)
                dve.wait_ge(dve_step, c)

            dve_mem(dve, MB, mem_b)
            compress_copy(dve, "dve", xc_b, 64, 32, None)
            dve.wait_ge(blocks, 5)
            nc.vector.tensor_copy(kc_p[:, :, :], ps[:, 0, 0:64].rearrange("p (g n) -> p g n", g=2))
            nc.vector.tensor_copy(vc_p[:, :], ps[0:32, 1, 0:256]).then_inc(blocks_read, 1)
            dve.wait_ge(km_b_turned, 1)
            nc.vector.tensor_copy(km_b[:, :, :], ps[:, 2, :].rearrange("p (t m) -> p t m", t=2)).then_inc(km_b_read, 1)
            dve.wait_ge(c_scored, 1)
            st, pc, mx, imp, eq = (small[k] for k in ("st", "pc", "mx", "imp", "eq"))
            live = pc[:, :, 0:NCS]
            sc = ps[0:QROWS, 0, :].rearrange("p (b n) -> p b n", b=NB)[:, :, 0:NCS]
            chained(nc.vector.tensor_reduce(st[:, 0, :], sc, AX, ALU.max))
            nc.vector.tensor_tensor(live, sc, bcast(st[:, 0, :], NCS), ALU.subtract).then_inc(c_centred, 1)
            snew = small["snew"].rearrange("p r b t -> p (r b) t")
            chained(nc.vector.tensor_tensor(snew, ps[0:QROWS, 1, 0:64].rearrange("p (a t) -> p a t", t=DEC),
                                            strided(cst[0:QROWS, C_NEW + 28:C_NEW + 29], (0, 2 * NB), (1, DEC)), ALU.add))
            chained(nc.vector.tensor_reduce(mx[:, :, 0, 2], small["snew"][:, 0, :, :], AX, ALU.max))
            chained(nc.vector.tensor_reduce(mx[:, :, 1, 2], small["snew"][:, 1, :, :], AX, ALU.max))
            nc.vector.tensor_copy(mx[:, :, 1, 1], mx[:, :, 1, 2])
            nc.vector.memset(small["bias"], 0.0)
            nc.vector.memset(p_new, 0.0)
            dve.wait_ge(c_exp, 1)
            chained(nc.vector.tensor_reduce(st[:, 1, :], live, AX, ALU.add))
            chained(nc.vector.reciprocal(st[:, 2, :], st[:, 1, :]))
            nc.vector.tensor_tensor(live, live, bcast(st[:, 2, :], NCS), ALU.mult).then_inc(c_normed, 1)
            dve.wait_ge(c_turned, 1)
            nc.vector.tensor_copy(small["pct"][0:NCS, :, :], ps[0:NCS, 4, 0:NB * QROWS].rearrange("p (b m) -> p b m", b=NB)
                                  ).then_inc(c_copied, 1)
            dve.wait_ge(gates_in, 16 * NB)
            nc.vector.tensor_tensor(live, live, bcast(gs[:, :, 0], NCS), ALU.mult).then_inc(c_gated, 1)
            dve.wait_ge(c_imp, 1)
            nc.vector.tensor_copy(imp, ps[0:QROWS, 2, 0:14 * NB].rearrange("p (b j) -> p b j", b=NB)).then_inc(c_imp_read, 1)
            dve.wait_ge(c_turned, 2)
            nc.vector.tensor_copy(small["pgt"][0:NCS, :, :], ps[0:NCS, 5, 0:NB * QROWS].rearrange("p (b m) -> p b m", b=NB)
                                  ).then_inc(c_copied, 1)
            dve.wait_ge(c_imp2, 1)
            imp2 = ps[0:QROWS, 3, 0:14 * NB].rearrange("p (b j) -> p b j", b=NB)
            j3 = strided(cst[0:QROWS, C_J:C_J + 1], (0, NB), (1, 14))
            chained(nc.vector.tensor_reduce(st[:, 3, :], imp2, AX, ALU.min))
            chained(nc.vector.tensor_tensor(eq, imp2, bcast(st[:, 3, :], 14), ALU.is_equal))
            chained(nc.vector.tensor_tensor(eq, eq, j3, ALU.mult))
            chained(nc.vector.tensor_reduce(st[:, 0, :], eq, AX, ALU.max))
            chained(nc.vector.tensor_tensor(eq, j3, bcast(st[:, 0, :], 14), ALU.is_equal))
            nc.vector.tensor_scalar(small["bias"][:, :, 1:15], eq, NEG, None, ALU.mult).then_inc(c_done, 1)
            dve.wait_ge(c_done, 1)
            s_copy(dve, "dve", 0, range(6))
            for b in range(NB):
                bx = small["bx"]
                copied = dve_chain(nc.vector.tensor_copy(bx.rearrange("p (j i) -> p j i", j=16),
                                                         strided(small["bias"][:, b, 0:1], (1, 16), (0, 8))))
                if b >= 1:
                    nc.vector.memset(p_new[:, :, DEC * (b - 1):DEC * b], 0.0)
                dve.wait_ge(s_scored, 2 * b + 1)
                edge = strided(ps[0:QROWS, 2, 0:1], (P, 4))
                chained(nc.vector.tensor_tensor(edge, edge, cst[0:QROWS, C_WIN:C_WIN + 4], ALU.add))
                chained(nc.vector.reduce_max(mx[:, b, 1, 0:1], ps[0:QROWS, 2, :], AX))
                chained(nc.vector.tensor_reduce(stat[0:QROWS, 37:38], mx[:, b, 1, :], AX, ALU.max))
                nc.vector.tensor_scalar(stat[0:QROWS, 39:40], stat[0:QROWS, 37:38], -SCALE, None, ALU.mult).then_inc(s_max, 1)
                dve.wait_ge(s_scored, 2 * b + 2)
                dve.wait_ge(dve_step, copied)
                for x in range(2):
                    sc = ps[0:QROWS, x, :].rearrange("p (s i) -> p s i", s=4)
                    ins = nc.vector.tensor_tensor_reduce(sc, sc, strided(bx[:, 0:1], (0, 4), (1, P)), 1.0,
                                                         3 * NEG, ALU.add, ALU.max, mx[:, b, 0, x:x + 1])
                chained(ins)
                chained(nc.vector.tensor_reduce(stat[0:QROWS, 36:37], mx[:, b, 0, :], AX, ALU.max))
                nc.vector.tensor_scalar(stat[0:QROWS, 38:39], stat[0:QROWS, 36:37], -SCALE, None, ALU.mult).then_inc(s_max, 1)

                def scales(br):
                    x, y, z, v = (stat[0:QROWS, c + br:c + br + 1] for c in (40, 42, 44, 46))
                    chained(nc.vector.tensor_tensor(z, x, y, ALU.add))
                    chained(nc.vector.reciprocal(v, z))
                    chained(nc.vector.tensor_tensor(stat[0:QROWS, 48 + br:49 + br], v, gs[:, b, 1 + br:2 + br], ALU.mult))
                    nc.vector.tensor_scalar(p_new[:, br, DEC * b:DEC * b + DEC], small["snew"][:, br, b, :],
                                            stat[0:QROWS, 48 + br:49 + br], None, ALU.mult)

                dve.wait_ge(s_exp, 2 * b + 1)
                scales(1)
                nc.vector.tensor_scalar(p_win, p_win, stat[0:QROWS, 49:50], None, ALU.mult)
                s_copy(dve, "dve", b + 1, range(2))
                dve.wait_ge(s_exp, 2 * b + 2)
                scales(0)
                nc.vector.tensor_scalar(p_sel, p_sel, stat[0:QROWS, 48:49], None, ALU.mult).then_inc(s_normed, 1)
                s_copy(dve, "dve", b + 1, range(2, 6))
                s_copy(dve, "dve", b, range(6, 8))
            dve.wait_ge(s_sum_turned, NB)
            for g in range(NG):
                e, pr = g % 2, g // 2
                src = strided(ps[HD * e:HD * e + HD, 3, 24 * pr + 12 * e:24 * pr + 12 * e + 1], (QROWS, NB), (DEC, GQ), (1, DEC))
                dst = strided(o_s[HD * e:HD * e + HD, pr * GQ, 0:1], (DEC, NB), (SAMP, GQ), (1, DEC))
                ins = nc.vector.tensor_copy(dst, src)
            ins.then_inc(s_out, 1)
            dve_split(dve, W_OUTB)
            meet(dve, 4)
            first = strided(gm[:, 0, 0:1], (3, NH))
            chained(nc.vector.tensor_tensor(first, first, strided(cst[:, C_VAL:C_VAL + 1], (0, NH)), ALU.mult))
            dve_units(dve, units_b, ub)
            dve_samples(dve, 0, 2)
            meet(dve, 5)

        y_turned = sem("y_turned")
        y_read = sem("y_read")
        y_rows = region(arena, 0, 5, D)

        def pe_stage5(pe):
            for n in range(10):
                j = n % NT
                m = P if j < NQT else SAMP
                pe.wait_ge(ln_hi, KD * 3 + (4 if n < NT else 8))
                if n >= 4:
                    pe.wait_ge(y_read, n - 3)
                for k in range(4):
                    mm = nc.tensor.transpose(ps[0:m, 4 + n % 4, k * P:(k + 1) * P],
                                             resid[:, 4 * (n // NT) + k, j * P:j * P + m], ident)
                mm.then_inc(y_turned, 1)

        def dve_stage5(dve):
            for n in range(10):
                m = P if n % NT < NQT else SAMP
                dve.wait_ge(y_turned, n + 1)
                nc.vector.tensor_copy(y_rows[0:m, n % NT, 512 * (n // NT):512 * (n // NT) + 512], ps[0:m, 4 + n % 4, :]).then_inc(y_read, 1)

        def sp_stage5(sp):
            for j in range(NQT):
                sp.wait_ge(y_read, NT + j + 1)
                sp.dma_start(o["y_p"][j * P:(j + 1) * P, :], y_rows[:, j, :]).then_inc(outputs_sp, 16)
            sp.wait_ge(y_read, 10)
            sp.dma_start(o["y_s"], y_rows[0:SAMP, NQT, :]).then_inc(outputs_sp, 16)
            sp.wait_ge(outputs, 32 + OUT_STAGE3)
            sp.wait_ge(outputs_sp, 16 * (NB + NQT + 1))
            sp.wait_ge(v_out, 16)
            for s in kv_out:
                sp.wait_ge(s, 32)

        block = ctx.enter_context(nc.Block())

        @block.sync
        def _(sp):
            sp_stage0(sp)
            sp_slots(sp, 0, 13)
            sp_stage2(sp)
            for b in range(NB):
                sp.dma_start(o["win_s"][b, 0:512 - DEC, :, :].rearrange("t v x -> t (v x)"),
                             w["cache_win_kv"][b, DEC:512].rearrange("t c h d -> t (c h d)")).then_inc(outputs_sp, 16)
            sp_slots(sp, 13, 2)
            sp_mlp(sp, 0)
            sp_slots(sp, W_KV, 11)
            sp.wait_ge(s_summed, 7)
            sp_slots(sp, W_OUTB, 4)
            sp_mlp(sp, 1)
            sp_stage5(sp)

        @block.gpsimd
        def _(pool):
            pool_stage0(pool)
            pool_stage1(pool)
            pool_stage2(pool)
            pool_out(pool, 0)
            pool_mlp(pool, 0)
            pool_ln(pool, 1)
            pool_stage3(pool)
            pool_stage4(pool)
            pool_out(pool, 1)
            pool_mlp(pool, 1)
            pool_ln(pool, 3)

        @block.tensor
        def _(pe):
            pe_stage0(pe)
            pe_stage1(pe)
            pe_stage2(pe)
            pe_out(pe, 0)
            pe_mlp(pe, 0)
            pe_ln(pe, 2)
            pe_stage3(pe)
            pe_stage4(pe)
            pe_out(pe, 1)
            pe_mlp(pe, 1)
            pe_ln(pe, 4)
            pe_stage5(pe)

        @block.scalar
        def _(act):
            act_stage0(act)
            act_stage1(act)
            act_stage2(act)
            act_out(act, 0)
            act_mlp(act, 0)
            act_split(act, W_KV + 1)
            act_ln(act, 1)
            act_stage3(act)
            act_stage4(act)
            act_out(act, 1)
            act_mlp(act, 1)
            act_ln(act, 3)

        @block.vector
        def _(dve):
            dve_stage0(dve)
            dve_stage1(dve)
            dve_stage2(dve)
            dve_out(dve, 0)
            dve_mlp(dve, 0)
            dve_split(dve, W_KV + 1)
            dve_ln(dve, 1)
            dve_stage3(dve)
            dve_stage4(dve)
            dve_out(dve, 1)
            dve_mlp(dve, 1)
            dve_ln(dve, 3)
            dve_stage5(dve)


INPUTS = ["x_prompt", "x_sample", "cache_cmp_kv", "cache_slc_kv", "cache_win_kv", "cache_mem_kv", "page_table", "mem_prompt",
          "w_in_a", "ln_v_g", "ln_v_b", "w_spatial", "b_spatial", "w_out_a", "w_in_b", "w_out_b", "w_kv_shared", "cmp_pe",
          "w_phi1", "w_phi2", "w_mem_kv", "ln1_g", "ln1_b", "ln2_g", "ln2_b", "w_up", "w_down"]
OUTPUTS = [("y_p", (1, SEQ, D)), ("y_s", (NB, DEC, D)), ("cmp_p", (1, SEQ, 2, NG, HD)), ("slc_p", (1, SEQ, 2, NG, HD)),
           ("win_p", (1, SEQ, 2, NG, HD)), ("mem_kv", (2, 1, MEM, 2, 4, 64)), ("cmp_s", (NB, DEC, 2, NG, HD)),
           ("slc_s", (NB, DEC, 2, NG, HD)), ("win_s", (NB, 512, 2, NG, HD)), ("gmlp_v", (1, NB, DEC, AW))]


def kernel(**inputs):
    import concourse.bacc as bacc
    from concourse.bass_utils import run_bass_kernel_spmd

    nc = bacc.Bacc("TRN2", target_bir_lowering=False, num_devices=1)
    arrays = {f"in_{n}": np.ascontiguousarray(inputs[n]) for n in INPUTS}
    arrays["in_consts"] = shape_constants()
    w = {n[3:]: nc.dram_tensor(n, a.shape, mybir.dt.from_np(a.dtype), kind="ExternalInput").ap() for n, a in arrays.items()}
    w["b_spatial"] = w["b_spatial"][0]
    o = {n: nc.dram_tensor(f"out_{n}", s, F32, kind="ExternalOutput").ap() for n, s in OUTPUTS}
    o["y_p"] = o["y_p"][0]
    o["y_s"] = o["y_s"].rearrange("b t d -> (b t) d")
    for n in ("cmp_p", "slc_p", "win_p"):
        o[n] = o[n][0].rearrange("t v h d -> t v (h d)")
    for n in ("cmp_s", "slc_s"):
        o[n] = o[n].rearrange("b t v h d -> (b t) v (h d)")
    o["win_s"] = o["win_s"].rearrange("b t v h d -> b t v (h d)")
    o["mem_kv"] = o["mem_kv"].rearrange("l a m v h d -> (l a) m (v h d)")
    scratch = nc.dram_tensor("gate_scratch", (SAMP, 36), F32, kind="Internal").ap()
    build(nc, w, o, scratch)
    out = run_bass_kernel_spmd(nc, [arrays], core_ids=[0]).results[0]
    return tuple(out[f"out_{n}"] for n, _ in OUTPUTS)
```
